# Optimizing a Trainium2 kernel written in Bass

```python
import math
import jax, jax.numpy as jnp
from jax import lax
import numpy as np

D_MODEL = 1024
BATCH = 1
SEQ = 256
DEPTH = 2

MIX_WIDTH = D_MODEL
GMLP_WIDTH = MIX_WIDTH // 2
N_GMLP_HEADS = 8
GMLP_HEAD_DIM = GMLP_WIDTH // N_GMLP_HEADS
CHUNK = 128
DIFF_WIDTH = MIX_WIDTH - GMLP_WIDTH
N_DIFF_HEADS = 4
DIFF_V_DIM = DIFF_WIDTH // N_DIFF_HEADS
DIFF_HEAD_DIM = DIFF_V_DIM // 2
BLOCK_Q = 128
IN_WIDTH = 2 * GMLP_WIDTH + 3 * DIFF_WIDTH
D_FF = ((8 * D_MODEL // 3 + 127) // 128) * 128
N_EXPERTS = 8
TOP_K = 2
D_FF_EXPERT = D_FF
N_DENSE = (DEPTH + 1) // 2
N_MOE = DEPTH // 2
N_MOD = 6
EPS = 1e-6

kernel_name = "hybrid_gmlp_diffattn_moe_adaln"

def _rms(x):
    xf = x.astype(jnp.float32)
    return (xf * lax.rsqrt(jnp.mean(xf * xf, axis=-1, keepdims=True) + EPS)).astype(x.dtype)

def rmsnorm(x, g):
    return _rms(x) * g

def swiglu(h, w_gate, w_up, w_down):
    return (jax.nn.silu(h @ w_gate) * (h @ w_up)) @ w_down

def gmlp_mixer(u, v, vnorm_g, w_s, b_s):
    B, S, _ = u.shape
    u = jax.nn.gelu(u)
    v = jax.nn.gelu(v).reshape(B, S // CHUNK, CHUNK, N_GMLP_HEADS, GMLP_HEAD_DIM)
    v = _rms(v) * vnorm_g.reshape(N_GMLP_HEADS, GMLP_HEAD_DIM)
    causal = jnp.tril(jnp.ones((CHUNK, CHUNK), dtype=bool))
    ws = jnp.where(causal[None], w_s, jnp.zeros_like(w_s))
    vm = jnp.einsum('gts,bcsgd->bctgd', ws, v) + b_s.T[:, :, None]
    return u * vm.reshape(B, S, GMLP_WIDTH)

def diff_attention(q, k, v, lam, lam_init, subln_g):
    B, S, H, _, dh = q.shape
    scale = dh ** -0.5
    nb = S // BLOCK_Q
    qb = q.reshape(B, nb, BLOCK_Q, H, 2, dh).transpose(1, 0, 2, 3, 4, 5)
    kpos = jnp.arange(S)

    def block(args):
        qi, i = args
        s = jnp.einsum('bqhmd,bkhmd->bhmqk', qi, k).astype(jnp.float32) * scale
        qpos = i * BLOCK_Q + jnp.arange(BLOCK_Q)
        allowed = kpos[None, :] <= qpos[:, None]
        s = jnp.where(allowed, s, -jnp.inf)
        p = jax.nn.softmax(s, axis=-1)
        a = p[:, :, 0] - lam * p[:, :, 1]
        return jnp.einsum('bhqk,bkhd->bqhd', a.astype(v.dtype), v)

    o = lax.map(block, (qb, jnp.arange(nb)))
    o = o.transpose(1, 0, 2, 3, 4).reshape(B, S, H, v.shape[-1])
    o = _rms(o) * subln_g * (1.0 - lam_init)
    return o.reshape(B, S, H * v.shape[-1])

def moe_swiglu(h, w_router, w_gate, w_up, w_down):
    B, S, D = h.shape
    hf = h.reshape(B * S, D)
    logits = (hf @ w_router).astype(jnp.float32)
    top_v, top_i = lax.top_k(logits, TOP_K)
    top_w = jax.nn.softmax(top_v, axis=-1)
    gates = jnp.sum(jax.nn.one_hot(top_i, N_EXPERTS, dtype=jnp.float32) * top_w[..., None], axis=1)
    gates = gates.astype(h.dtype)
    out = jnp.zeros_like(hf)
    for e in range(N_EXPERTS):
        out = out + gates[:, e:e + 1] * swiglu(hf, w_gate[e], w_up[e], w_down[e])
    return out.reshape(B, S, D)

def setup_inputs(seed: int = 0) -> dict:
    key = jax.random.key(seed)
    ks = jax.random.split(key, 32)
    f32 = jnp.float32
    nrm = lambda k, shape, s: jax.random.normal(k, shape, f32) * s
    D = D_MODEL
    return {
        "x": nrm(ks[0], (BATCH, SEQ, D), 1.0),
        "c": nrm(ks[1], (BATCH, D), 1.0),
        "w_ada": nrm(ks[2], (DEPTH, D, N_MOD * D), 0.5 * D ** -0.5),
        "b_ada": nrm(ks[3], (DEPTH, N_MOD * D), 0.02),
        "norm1_g": 1.0 + nrm(ks[4], (DEPTH, D), 0.02),
        "norm2_g": 1.0 + nrm(ks[5], (DEPTH, D), 0.02),
        "w_in": nrm(ks[6], (DEPTH, D, IN_WIDTH), D ** -0.5),
        "w_out": nrm(ks[7], (DEPTH, MIX_WIDTH, D), MIX_WIDTH ** -0.5),
        "gmlp_vnorm_g": 1.0 + nrm(ks[8], (DEPTH, GMLP_WIDTH), 0.02),
        "gmlp_ws": nrm(ks[9], (DEPTH, N_GMLP_HEADS, CHUNK, CHUNK), CHUNK ** -0.5),
        "gmlp_bs": 1.0 + nrm(ks[10], (DEPTH, N_GMLP_HEADS, CHUNK), 0.1),
        "lam_q1": nrm(ks[11], (DEPTH, DIFF_HEAD_DIM), 0.1),
        "lam_k1": nrm(ks[12], (DEPTH, DIFF_HEAD_DIM), 0.1),
        "lam_q2": nrm(ks[13], (DEPTH, DIFF_HEAD_DIM), 0.1),
        "lam_k2": nrm(ks[14], (DEPTH, DIFF_HEAD_DIM), 0.1),
        "diff_subln_g": 1.0 + nrm(ks[15], (DEPTH, DIFF_V_DIM), 0.02),
        "ffn_w_gate": nrm(ks[16], (N_DENSE, D, D_FF), D ** -0.5),
        "ffn_w_up": nrm(ks[17], (N_DENSE, D, D_FF), D ** -0.5),
        "ffn_w_down": nrm(ks[18], (N_DENSE, D_FF, D), D_FF ** -0.5),
        "w_router": nrm(ks[19], (N_MOE, D, N_EXPERTS), D ** -0.5),
        "moe_w_gate": nrm(ks[20], (N_MOE, N_EXPERTS, D, D_FF_EXPERT), D ** -0.5),
        "moe_w_up": nrm(ks[21], (N_MOE, N_EXPERTS, D, D_FF_EXPERT), D ** -0.5),
        "moe_w_down": nrm(ks[22], (N_MOE, N_EXPERTS, D_FF_EXPERT, D), D_FF_EXPERT ** -0.5),
        "final_g": 1.0 + nrm(ks[23], (D,), 0.02),
    }

def reference(x, c, w_ada, b_ada, norm1_g, norm2_g, w_in, w_out, gmlp_vnorm_g, gmlp_ws, gmlp_bs,
              lam_q1, lam_k1, lam_q2, lam_k2, diff_subln_g, ffn_w_gate, ffn_w_up, ffn_w_down,
              w_router, moe_w_gate, moe_w_up, moe_w_down, final_g):
    B, S, D = x.shape
    sc = jax.nn.silu(c)
    splits = [GMLP_WIDTH, 2 * GMLP_WIDTH, 2 * GMLP_WIDTH + DIFF_WIDTH, 2 * GMLP_WIDTH + 2 * DIFF_WIDTH]
    for l in range(DEPTH):
        mod = sc @ w_ada[l] + b_ada[l]
        sh1, sc1, g1, sh2, sc2, g2 = [m[:, None, :] for m in jnp.split(mod, N_MOD, axis=-1)]

        h = rmsnorm(x, norm1_g[l]) * (1.0 + sc1) + sh1
        z = h @ w_in[l]
        u_a, v_a, q_b, k_b, v_b = jnp.split(z, splits, axis=-1)
        out_a = gmlp_mixer(u_a, v_a, gmlp_vnorm_g[l], gmlp_ws[l], gmlp_bs[l])
        lam_init = 0.8 - 0.6 * math.exp(-0.3 * l)
        lam = (jnp.exp(jnp.sum((lam_q1[l] * lam_k1[l]).astype(jnp.float32)))
               - jnp.exp(jnp.sum((lam_q2[l] * lam_k2[l]).astype(jnp.float32))) + lam_init)
        q = q_b.reshape(B, S, N_DIFF_HEADS, 2, DIFF_HEAD_DIM)
        k = k_b.reshape(B, S, N_DIFF_HEADS, 2, DIFF_HEAD_DIM)
        v = v_b.reshape(B, S, N_DIFF_HEADS, DIFF_V_DIM)
        out_b = diff_attention(q, k, v, lam, lam_init, diff_subln_g[l])
        y = jnp.concatenate([out_a, out_b], axis=-1) @ w_out[l]
        x = x + g1 * y

        h = rmsnorm(x, norm2_g[l]) * (1.0 + sc2) + sh2
        if l % 2 == 0:
            i = l // 2
            f = swiglu(h, ffn_w_gate[i], ffn_w_up[i], ffn_w_down[i])
        else:
            i = l // 2
            f = moe_swiglu(h, w_router[i], moe_w_gate[i], moe_w_up[i], moe_w_down[i])
        x = x + g2 * f
    return rmsnorm(x, final_g)


_drawn_inputs = setup_inputs


def setup_inputs(seed=0):
    import zlib

    import numpy as np

    out = dict(_drawn_inputs(seed))
    spreads = {}
    factors = {'norm1_g': 7.039,
     'norm2_g': 3.762,
     'gmlp_vnorm_g': 8.0,
     'lam_q1': 4.446,
     'lam_k1': 4.929,
     'lam_q2': 6.103,
     'lam_k2': 5.383,
     'diff_subln_g': 25.076,
     'final_g': 8.525}
    for name, (base, spread) in spreads.items():
        noise = np.random.default_rng([zlib.crc32(name.encode()), seed]).standard_normal(out[name].shape)
        drawn = base * np.exp(spread * noise) if base else spread * noise
        out[name] = __import__('jax').numpy.asarray(drawn.astype(out[name].dtype))
    for name, factor in factors.items():
        out[name] = (out[name] * factor).astype(out[name].dtype)
    return out
```

```python
import math
from contextlib import ExitStack

import numpy as np
import concourse.bass as bass
from concourse import mybir
from concourse.alu_op_type import AluOpType as ALU

ACT = mybir.ActivationFunctionType
AX = mybir.AxisListType
F32 = mybir.dt.float32
F32R = mybir.dt.float32r
I32 = mybir.dt.int32
U32 = mybir.dt.uint32

P = 128
D = 1024
KT = D // P
SEQ = 256
NT = SEQ // P
DEPTH = 2
GW = 512
NG = 8
GD = GW // NG
NH = 4
DV = 128
DH = 64
INW = 2 * GW + 3 * NH * DV
FF = 2816
NE = 8
FB = 256
NBLK = FF // FB
CB = 512
EPS = 1e-6
NEG = -1e30
RING = 11
NB = 3
CHUNK = 2048
SUB = 1024
MOD_BLOCKS = 12
SPLITS_PER_BLOCK = 6
EXPERT_CHUNKS = 3 * NBLK
EXPERT_SPLITS = SPLITS_PER_BLOCK * NBLK
SILU_AFTER = [None, 1] + [0] * (NBLK - 2)
SH1, SC1, G1, SH2, SC2, G2 = range(6)


BESIDE_IN = [[(0, 4), (0, 5), (0, 6), (0, 7), (0, 8)], [(1, 6), (1, 7), (1, 8), (1, 9), (1, 10)]]
BESIDE_OUT = [(0, 9), (1, 11)]
BESIDE_FFN = [(0, 10), (0, 11), (1, 0), (1, 1), (1, 2), (1, 3), (1, 4), (1, 5), None, None, None, None]


def chunk_stream():
    s = [("ada", 0, j, half) for j in range(4) for half in range(2)]
    for layer in range(DEPTH):
        for j in range(INW // CB):
            for half in range(2):
                s.append(("in", layer, j, half))
                s.append(("ada", *BESIDE_IN[layer][j], half))
        for j in range(D // CB):
            s += [("out", layer, j, half) for half in range(2)]
            if j == 0:
                s += [("ada", *BESIDE_OUT[layer], half) for half in range(2)]
        if layer == 0:
            for b in range(NBLK + 1):
                if b < NBLK:
                    s += [("gate", 0, b, 0), ("up", 0, b, 0)]
                if BESIDE_FFN[b]:
                    s.append(("ada", *BESIDE_FFN[b], 0))
                if b >= 1:
                    s.append(("down", 0, b - 1, 0))
                if BESIDE_FFN[b]:
                    s.append(("ada", *BESIDE_FFN[b], 1))
    return s


def expert_chunks():
    s = []
    for b in range(NBLK + 1):
        if b < NBLK:
            s += [("gate", b), ("up", b)]
        if b >= 1:
            s.append(("down", b - 1))
    return s


def trunk(nc, t, out):
    STREAM = chunk_stream()
    WHERE = {c: n for n, c in enumerate(STREAM)}
    ADA = [(c[1], c[2]) for c in STREAM if c[0] == "ada" and c[3] == 0]
    N0 = len(STREAM)
    EXPERT = expert_chunks()
    EWHERE = {c: n for n, c in enumerate(EXPERT)}
    S_IN = [0, 0]
    S_OUT = [0, 0]
    S_IN[0] = 0
    S_OUT[0] = S_IN[0] + 4 * (INW // CB)
    S_FFN = S_OUT[0] + 4 * (D // CB)
    S_IN[1] = S_FFN + EXPERT_SPLITS
    S_OUT[1] = S_IN[1] + 4 * (INW // CB)
    S_MOE = S_OUT[1] + 4 * (D // CB)
    assert S_MOE % NB == 0 or True

    def split_in_block(b, q):
        return 0 + q if b == 0 else 4 + (b - 1) * 6 + q

    def down_split(b, c):
        return (4 + b * 6 + 4 + c) if b + 1 < NBLK else 4 + b * 6 + c

    ctx = ExitStack()
    with ctx:
        at = [(nc.sbuf_base + 63) // 64 * 64]

        def sb(name, shape, dt=F32, offset=None):
            size = int(np.prod(shape[1:])) * 4
            size = (size + 31) // 32 * 32
            where = at[0] if offset is None else offset
            assert where + size <= nc.sbuf_usable_end, (name, where + size)
            h = nc.alloc_sbuf_tensor_at(name, shape, dt, offset=where)
            if offset is None:
                at[0] += size
            return h

        raw = sb("raw", [P, RING, CHUNK])
        w_hi = sb("w_hi", [P, NB, SUB], F32R)
        w_lo = sb("w_lo", [P, NB, SUB], F32R)
        mod = sb("mod", [P, 6, D])
        x = sb("x", [P, NT, D])
        gain = sb("gain", [P, D])
        ident = sb("ident", [P, P])
        ones = sb("ones", [P, P])
        before = sb("before", [P, P])
        upto = sb("upto", [P, P])
        future = sb("future", [P, P])
        slot_no = sb("slot_no", [P, P])
        slot_int = sb("slot_int", [P, P], I32)
        ada_acc = sb("ada_acc", [P, 2, CB])
        ada_bias = sb("ada_bias", [P, CB])
        silu_c = sb("silu_c", [P, KT])
        c_rows = sb("c_rows", [KT, P])
        eps_col = sb("eps_col", [P, 1])
        ssq = sb("ssq", [P, NT])
        std = sb("std", [P, NT])
        rstd = sb("rstd", [P, NT])
        lam_sum = sb("lam_sum", [P, 2])
        lam_exp = sb("lam_exp", [P, 2])
        lam = sb("lam", [P, 1])
        small = at[0]
        base = at[0]
        hT_hi = sb("hT_hi", [P, KT, SEQ], F32R)
        hT_lo = sb("hT_lo", [P, KT, SEQ], F32R)
        z = sb("z", [P, NT, INW])
        wsT = sb("wsT", [P, NG, P])
        ws_raw = sb("ws_raw", [P, NG, P])
        prob = sb("prob", [P, 2, 3 * P])
        aT = sb("aT", [P, 3 * P])
        subln = sb("subln", [P, DV])
        gstat = sb("gstat", [P, 4 * NG * NT])
        hstat = sb("hstat", [P, 6 * 2 * NT])
        bsT = sb("bsT", [P, NG])
        o = base
        qT = sb("qT", [P, NH, SEQ], offset=o); o += NH * SEQ * 4
        kT = sb("kT", [P, NH, SEQ], offset=o); o += NH * SEQ * 4
        vgain = sb("vgain", [P, GW], offset=o); o += GW * 4
        lam_rows = sb("lam_rows", [P, 4, DH], offset=o); o += 4 * DH * 4
        vsq = sb("vsq", [P, GW], offset=o); o += GW * 4
        assert o <= base + 2 * KT * SEQ * 4
        zbase = base + 2 * KT * SEQ * 4
        h_tok = sb("h_tok", [P, NT, D], offset=zbase)
        y_scaled = sb("y_scaled", [P, 2, CB], offset=zbase + NT * D * 4)
        o = zbase + NT * D * 4 + 2 * CB * 4
        f_silu = sb("f_silu", [P, NT, FB], offset=o); o += NT * FB * 4
        f_act = sb("f_act", [P, NT, FB], offset=o); o += NT * FB * 4
        fT_hi = sb("fT_hi", [P, NT, FB], F32R, offset=o); o += NT * FB * 4
        fT_lo = sb("fT_lo", [P, NT, FB], F32R, offset=o); o += NT * FB * 4
        o = base
        htok_hi = sb("htok_hi", [P, NT, D], F32R, offset=o); o += NT * D * 4
        htok_lo = sb("htok_lo", [P, NT, D], F32R, offset=o); o += NT * D * 4
        f_scaled = sb("f_scaled", [P, 2, CB], offset=base)
        y_hi = sb("y_hi", [P, D], F32R, offset=o)
        m_htok = sb("m_htok", [P, NT, D], offset=o)
        o += D * 4
        y_lo = sb("y_lo", [P, D], F32R, offset=o); o += D * 4
        m_acc = sb("m_acc", [P, NT, D], offset=o)
        r_hT = sb("r_hT", [P, KT, SEQ], offset=o)
        o += NT * D * 4
        hgT_hi = sb("hgT_hi", [P, KT, P], F32R, offset=o); o += KT * P * 4
        hgT_lo = sb("hgT_lo", [P, KT, P], F32R, offset=o); o += KT * P * 4
        m_silu = sb("m_silu", [P, FB], offset=o); o += FB * 4
        m_act = sb("m_act", [P, FB], offset=o); o += FB * 4
        mT_hi = sb("mT_hi", [P, FB], F32R, offset=o); o += FB * 4
        mT_lo = sb("mT_lo", [P, FB], F32R, offset=o); o += FB * 4
        pick = sb("pick", [P, NT, P], F32R, offset=o); o += NT * P * 4
        put = sb("put", [P, NT, P], F32R, offset=o); o += NT * P * 4
        gate_col = sb("gate_col", [P, NT], offset=o); o += 32
        slot_gate = sb("slot_gate", [P, 1], offset=o); o += 32
        slot_of = sb("slot_of", [P, NT, 2 * NE + 1], offset=o); o += 160
        gate_of = sb("gate_of", [P, NT, 2 * NE + 1], offset=o); o += 160
        w_route = sb("w_route", [P, KT, NE], offset=o); o += KT * NE * 4
        logit = sb("logit", [P, NT, NE], offset=o); o += 64
        top = sb("top", [P, NT, 8], offset=o); o += 64
        top_i = sb("top_i", [P, NT, 8], U32, offset=o); o += 64
        top_f = sb("top_f", [P, NT, 8], offset=o); o += 64
        gap = sb("gap", [P, NT, 1], offset=o); o += 32
        e2 = sb("e2", [P, NT, 1], offset=o); o += 32
        w1 = sb("w1", [P, NT, 1], offset=o); o += 32
        w2 = sb("w2", [P, NT, 1], offset=o); o += 32
        wsum = sb("wsum", [P, NT, 1], offset=o); o += 32
        hit = sb("hit", [P, NT, 2, NE], offset=o); o += NT * 2 * NE * 4
        mask = sb("mask", [P, NT, NE], offset=o); o += 64
        most = sb("most", [P, 1], offset=o); o += 32
        rounds_f = sb("rounds_f", [P, 1], offset=o); o += 32
        rounds = sb("rounds", [P, 1], I32, offset=o); o += 32
        assert o <= nc.sbuf_usable_end, o

        bank = [ctx.enter_context(nc.psum_tensor(f"bank{i}", [P, 512], F32)) for i in range(8)]

        def sem(name):
            return ctx.enter_context(nc.semaphore(name))

        chunk_in = [sem(f"chunk_in{i}") for i in range(RING)]
        hi_done = sem("hi_done")
        split_done = sem("split_done")
        split_used = sem("split_used")
        sp_turn = sem("sp_turn")
        first_in = sem("first_in")
        x_in = sem("x_in")
        gain_in = sem("gain_in")
        gain_used = sem("gain_used")
        bias_in = sem("bias_in")
        bias_used = sem("bias_used")
        consts = sem("consts")
        pool_step = sem("pool_step")
        mixer_in = sem("mixer_in")
        mixer_in2 = sem("mixer_in2")
        route_in = sem("route_in")
        c_mm = sem("c_mm")
        silu_c_done = sem("silu_c_done")
        ada_mm = sem("ada_mm")
        ada_out = sem("ada_out")
        ssq_done = sem("ssq_done")
        std_done = sem("std_done")
        h_done = sem("h_done")
        tr_mm = sem("tr_mm")
        tr_hi = sem("tr_hi")
        tr_lo = sem("tr_lo")
        z_out = sem("z_out")
        ws_mm = sem("ws_mm")
        ws_out = sem("ws_out")
        qk_mm = sem("qk_mm")
        qk_out_a = sem("qk_out_a")
        qk_out_v = sem("qk_out_v")
        vstat_done = sem("vstat_done")
        vstd_done = sem("vstd_done")
        v_done = sem("v_done")
        vm_mm = sem("vm_mm")
        ua_done = sem("ua_done")
        sc_mm = sem("sc_mm")
        negmax = sem("negmax")
        exp_done = sem("exp_done")
        a_done = sem("a_done")
        at_mm = sem("at_mm")
        at_out = sem("at_out")
        o_mm = sem("o_mm")
        o_out = sem("o_out")
        lam_dots = sem("lam_dots")
        lam_exps = sem("lam_exps")
        ostat_done = sem("ostat_done")
        ostd_done = sem("ostd_done")
        ob_done = sem("ob_done")
        x_step = sem("x_step")
        dve_step = sem("dve_step")
        act_step = sem("act_step")
        gu_mm = sem("gu_mm")
        silu_done = sem("silu_done")
        act_done = sem("act_done")
        fT_mm = sem("fT_mm")
        fT_hi_done = sem("fT_hi_done")
        fT_lo_done = sem("fT_lo_done")
        htok_split = sem("htok_split")
        r_mm = sem("r_mm")
        r_out = sem("r_out")
        logit_mm = sem("logit_mm")
        gap_done = sem("gap_done")
        gexp_done = sem("gexp_done")
        mask_done = sem("mask_done")
        count_mm = sem("count_mm")
        rounds_done = sem("rounds_done")
        pick_done = sem("pick_done")
        pick_mm = sem("pick_mm")
        put_done = sem("put_done")
        ga_mm = sem("ga_mm")
        ga_hi = sem("ga_hi")
        ga_lo = sem("ga_lo")
        m_sl = sem("m_sl")
        m_ac = sem("m_ac")
        m_tm = sem("m_tm")
        m_th = sem("m_th")
        m_tl = sem("m_tl")
        zero_mm = sem("zero_mm")
        m_yh = sem("m_yh")
        m_yl = sem("m_yl")
        m_sc = sem("m_sc")
        m_add = sem("m_add")
        out_ready = sem("out_ready")
        out_sent = sem("out_sent")

        def kview(ap):
            return ap.rearrange("(k p) n -> p k n", p=P)

        def chunk_source(c):
            kind, layer, j, half = c
            if kind == "ada":
                return kview(t["w_ada"][layer])[:, 4 * half:4 * half + 4, CB * j:CB * j + CB]
            if kind == "in":
                return kview(t["w_in"][layer])[:, 4 * half:4 * half + 4, CB * j:CB * j + CB]
            if kind == "out":
                return kview(t["w_out"][layer])[:, 4 * half:4 * half + 4, CB * j:CB * j + CB]
            if kind == "gate":
                return kview(t["ffn_w_gate"][0])[:, :, FB * j:FB * j + FB]
            if kind == "up":
                return kview(t["ffn_w_up"][0])[:, :, FB * j:FB * j + FB]
            return kview(t["ffn_w_down"][0])[:, 2 * j:2 * j + 2, :]

        def expert_source(e, kind, b):
            name = {"gate": "moe_w_gate", "up": "moe_w_up", "down": "moe_w_down"}[kind]
            v = t[name][0].rearrange("e (k p) n -> e p k n", p=P)
            if kind == "down":
                v = v[bass.ds(e, 1), :, 2 * b:2 * b + 2, :]
            else:
                v = v[bass.ds(e, 1), :, :, FB * b:FB * b + FB]
            return v.rearrange("a p k n -> (a p) k n")

        def ring_slot(n):
            s = n % RING
            return s

        def landed(n):
            return 16 * (n // RING + 1)

        def pair_slots(n):
            a, b = n % RING, (n + 1) % RING
            return min(a, b), max(a, b)

        def load_slot(kind, n):
            if kind == "gate":
                return pair_slots(n)[0]
            if kind == "up":
                return pair_slots(n - 1)[1]
            return n % RING

        def landed_in(slot, n):
            return 16 * (n // RING + 1)

        def slot_count(kind, n):
            slot = load_slot(kind, n)
            own = n if n % RING == slot else (n + 1 if kind == "gate" else n - 1)
            assert own % RING == slot
            return slot, 16 * (own // RING + 1)

        def taken(n, q):
            return 2 * n + q + 1

        def freed(n, kind):
            return taken(n + 1, 1) if kind == "gate" else taken(n, 1)

        def gu_raw(n, q):
            a, b = pair_slots(n)
            return raw[:, a:b + 1:b - a, 2 * q * FB:(2 * q + 2) * FB]

        def down_raw(n, c):
            return raw[:, n % RING, c * SUB:(c + 1) * SUB]

        blk = ctx.enter_context(nc.Block())

        @blk.sync
        def _(sp):
            sp.dma_start(c_rows[:, :], t["c"][0].rearrange("(k p) -> k p", p=P)).then_inc(first_in, 16)
            for n, c in enumerate(STREAM):
                if n >= RING:
                    ahead = n + 1 if c[0] == "gate" else n
                    sp.wait_ge(split_done, freed(ahead - RING, STREAM[ahead - RING][0]))
                slot, _ = slot_count(c[0], n)
                src = chunk_source(c)
                sp.dma_start(raw[:, slot, :].rearrange("p (k n) -> p k n", n=src.shape[2]), src)\
                  .then_inc(chunk_in[slot], 16)
                if n == 3:
                    sp.dma_start(x[:, :, :], t["x"][0].rearrange("(a p) d -> p a d", p=P)).then_inc(x_in, 16)

            def load_expert(e, turn):
                for j, (kind, b) in enumerate(EXPERT):
                    n = N0 + j
                    ahead = n + 1 if kind == "gate" else n
                    past = EXPERT[ahead - N0 - RING][0]
                    sp.wait_ge(split_done, turn * EXPERT_SPLITS + freed(ahead - RING, past))
                    sp.sem_inc(sp_turn, 1)
                    slot, _ = slot_count(kind, n)
                    src = expert_source(e, kind, b)
                    sp.dma_start(raw[:, slot, :].rearrange("p (k n) -> p k n", n=src.shape[2]), src)\
                      .then_inc(chunk_in[slot], 16)

            with sp.Fori(0, NE) as e:
                load_expert(e, e)
            sp.wait_ge(rounds_done, 1)
            n_turns = sp.value_load(rounds[0:1, 0:1], min_val=NE, max_val=2 * NE)
            with sp.If(n_turns > NE):
                with sp.Fori(0, NE) as e:
                    load_expert(e, e + NE)
            sp.wait_ge(out_ready, NT)
            sp.dma_start(out.rearrange("(a p) d -> p a d", p=P), h_tok[:, :, :]).then_inc(out_sent, 16)
            sp.wait_ge(out_sent, 16)

        @blk.gpsimd
        def _(pool):
            pool.memset(ada_bias[:, :], 0.0).then_inc(pool_step, 1)
            pool.memset(ones[:, :], 1.0).then_inc(pool_step, 1)
            pool.memset(ident[:, :], 0.0).then_inc(pool_step, 1)
            pool.memset(future[:, :], 0.0).then_inc(pool_step, 1)
            pool.memset(eps_col[:, :], EPS).then_inc(pool_step, 1)
            pool.iota(slot_int[:, :], pattern=[[1, P]], base=0, channel_multiplier=0).then_inc(pool_step, 1)
            pool.wait_ge(pool_step, 6)
            pool.affine_select(out=ident[:, :], in_=ident[:, :], compare_op=ALU.not_equal, fill=1.0,
                               base=0, pattern=[[-1, P]], channel_multiplier=1).then_inc(consts, 1)
            pool.affine_select(out=before[:, :], in_=ones[:, :], compare_op=ALU.is_gt, fill=0.0,
                               base=0, pattern=[[1, P]], channel_multiplier=-1).then_inc(consts, 1)
            pool.affine_select(out=upto[:, :], in_=ones[:, :], compare_op=ALU.is_ge, fill=0.0,
                               base=0, pattern=[[1, P]], channel_multiplier=-1).then_inc(consts, 1)
            pool.affine_select(out=future[:, :], in_=future[:, :], compare_op=ALU.is_ge, fill=NEG,
                               base=0, pattern=[[-1, P]], channel_multiplier=1).then_inc(consts, 1)
            pool.tensor_copy(slot_no[:, :], slot_int[:, :]).then_inc(consts, 1)

            def broadcast(dst, row, signal):
                pool.dma_start(dst, row.partition_broadcast(P)).then_inc(signal, 16)

            gains = [t["norm1_g"][0], t["norm2_g"][0], t["norm1_g"][1], t["norm2_g"][1], t["final_g"]]
            done = [0]

            def load_gain(i):
                if i:
                    pool.wait_ge(gain_used, 2 * i)
                broadcast(gain[:, :], gains[i], gain_in)

            def load_bias(upto_block):
                while done[0] < upto_block:
                    i = done[0]
                    layer, j = ADA[i]
                    if i:
                        pool.wait_ge(bias_used, i)
                    pool.dma_start(ada_bias[0:1, :], t["b_ada"][layer:layer + 1, CB * j:CB * j + CB])\
                        .then_inc(bias_in, 16)
                    done[0] += 1
                    if i and ADA[i - 1] in ((0, 3), (0, 9), (1, 3), (1, 9)):
                        following.append(1)
                        load_gain(len(following))

            following = []

            def load_mixer(layer):
                pool.dma_start(ws_raw[:, :, :], t["gmlp_ws"][layer].rearrange("g a b -> a g b")).then_inc(mixer_in, 16)
                pool.dma_start(bsT[:, :], t["gmlp_bs"][layer].rearrange("g a -> a g"), allow_slow_non_contiguous=True).then_inc(mixer_in, 16)
                broadcast(subln[:, :], t["diff_subln_g"][layer], mixer_in)

            def load_mixer_over_hT(layer):
                pool.wait_ge(split_used, S_OUT[layer])
                broadcast(vgain[:, :], t["gmlp_vnorm_g"][layer], mixer_in2)
                for i, name in enumerate(("lam_q1", "lam_k1", "lam_q2", "lam_k2")):
                    broadcast(lam_rows[:, i, :], t[name][layer], mixer_in2)

            load_gain(0)
            load_bias(4)
            load_mixer(0)
            load_bias(10)
            load_mixer_over_hT(0)
            load_bias(18)
            load_mixer(1)
            load_bias(24)
            load_mixer_over_hT(1)
            pool.wait_ge(split_used, S_MOE)
            pool.dma_start(w_route[:, :, :], t["w_router"][0].rearrange("(k p) e -> p k e", p=P)).then_inc(route_in, 16)

        @blk.scalar
        def _(act):
            steps = [0]

            def then(ins):
                steps[0] += 1
                ins.then_inc(act_step, 1)
                act.wait_ge(act_step, steps[0])

            def split_hi(s, src, like, base=0):
                if not (isinstance(base, int) and s < NB):
                    act.wait_ge(split_used, base + (s - NB + 1))
                act.activation(like(w_hi[:, s % NB, :]), src, ACT.Copy).then_inc(hi_done, 1)

            def flat(ap):
                return ap

            def pairs(ap):
                return ap.rearrange("p (g n) -> p g n", g=2)

            def wait_chunk(kind, n, base=0):
                slot, count = slot_count(kind, n)
                act.wait_ge(chunk_in[slot], base + count)

            def std_of_rows(i):
                for a in range(NT):
                    act.wait_ge(ssq_done, NT * i + a + 1)
                    act.activation(std[:, a:a + 1], ssq[:, a:a + 1], ACT.Sqrt, bias=eps_col[:, 0:1],
                                   scale=1.0 / D).then_inc(std_done, 1)

            def transposed_hi(dst, i):
                for a in range(NT):
                    for half in range(2):
                        n = 4 * i + 2 * a + half
                        act.wait_ge(tr_mm, n + 1)
                        act.activation(dst[:, 4 * half:4 * half + 4, P * a:P * a + P],
                                       bank[2 * a + half][:, :].rearrange("p (k n) -> p k n", k=4),
                                       ACT.Copy).then_inc(tr_hi, 1)

            act.wait_ge(c_mm, 1)
            act.activation(silu_c[:, :], bank[6][:, 0:KT], ACT.Silu).then_inc(silu_c_done, 1)
            act.wait_ge(consts, 5)
            for layer in range(DEPTH):
                std_of_rows(2 * layer)
                transposed_hi(hT_hi, 2 * layer if layer == 0 else 3)

                def z_block(j):
                    act.wait_ge(split_used, S_IN[layer] + 4 * (j + 1))
                    for a in range(NT):
                        act.activation(z[:, a, CB * j:CB * j + CB], bank[2 * (j % 2) + a][:, :],
                                       ACT.Gelu_apprx_tanh if j < 2 else ACT.Copy).then_inc(z_out, 1)

                for j in range(INW // CB):
                    for half in range(2):
                        n = WHERE[("in", layer, j, half)]
                        wait_chunk("in", n)
                        for q in range(2):
                            split_hi(S_IN[layer] + 4 * j + 2 * half + q,
                                     raw[:, n % RING, q * SUB:(q + 1) * SUB], flat)
                        if half == 0 and j:
                            z_block(j - 1)
                z_block(INW // CB - 1)

                for a in range(NT):
                    act.wait_ge(qk_mm, 4 * layer + a + 1)
                    act.activation(qT[:, :, P * a:P * a + P], bank[a][:, :].rearrange("p (h n) -> p h n", h=NH),
                                   ACT.Copy).then_inc(qk_out_a, 1)
                act.wait_ge(vstat_done, layer + 1)
                act.activation(gstat[:, 16:32], gstat[:, 0:16], ACT.Sqrt, bias=eps_col[:, 0:1],
                               scale=1.0 / GD).then_inc(vstd_done, 1)
                act.wait_ge(lam_dots, layer + 1)
                act.activation(lam_exp[:, :], lam_sum[:, :], ACT.Exp).then_inc(lam_exps, 1)
                for h in range(NH):
                    act.wait_ge(negmax, NH * layer + h + 1)
                    for m in range(2):
                        for a in range(NT):
                            cols = slice(0, P) if a == 0 else slice(P, 3 * P)
                            act.activation(prob[:, m, cols], bank[2 * (h % 2) + m][:, cols], ACT.Exp,
                                           bias=hstat[:, 4 + 2 * m + a:5 + 2 * m + a], scale=DH ** -0.5,
                                           accum_out=hstat[:, 8 + 2 * m + a:9 + 2 * m + a]).then_inc(exp_done, 1)
                    act.wait_ge(at_mm, NH * layer + h + 1)
                    act.activation(aT[:, :], bank[4 + h % 2][:, 0:3 * P], ACT.Copy).then_inc(at_out, 1)
                    act.wait_ge(o_mm, NH * layer + h + 1)
                    act.activation(z[:, :, 2 * GW + DV * h:2 * GW + DV * h + DV],
                                   bank[6][:, FB * (h % 2):FB * (h % 2) + FB].rearrange("p (a n) -> p a n", a=NT),
                                   ACT.Copy).then_inc(o_out, 1)
                act.wait_ge(ostat_done, layer + 1)
                act.activation(gstat[:, 40:48], gstat[:, 32:40], ACT.Sqrt, bias=eps_col[:, 0:1],
                               scale=1.0 / DV).then_inc(ostd_done, 1)

                transposed_hi(hT_hi, 1 if layer == 0 else 4)
                for j in range(D // CB):
                    for half in range(2):
                        n = WHERE[("out", layer, j, half)]
                        wait_chunk("out", n)
                        for q in range(2):
                            split_hi(S_OUT[layer] + 4 * j + 2 * half + q,
                                     raw[:, n % RING, q * SUB:(q + 1) * SUB], flat)

                std_of_rows(2 * layer + 1)
                if layer == 0:
                    transposed_hi(hT_hi, 2)
                    for b in range(NBLK + 1):
                        if b < NBLK:
                            n = WHERE[("gate", 0, b, 0)]
                            wait_chunk("gate", n)
                            wait_chunk("up", n + 1)
                            for q in range(4):
                                split_hi(S_FFN + split_in_block(b, q), gu_raw(n, q), pairs)
                        if b:
                            act.wait_ge(fT_mm, b)
                            act.activation(fT_hi[:, :, :], bank[6][:, :].rearrange("p (a n) -> p a n", a=NT),
                                           ACT.Copy).then_inc(fT_hi_done, 1)
                            n = WHERE[("down", 0, b - 1, 0)]
                            wait_chunk("down", n)
                            for c in range(2):
                                split_hi(S_FFN + down_split(b - 1, c), down_raw(n, c), flat)
                        if b < NBLK:
                            for a in range(NT):
                                if a == 0:
                                    act.wait_ge(gu_mm, b + 1)
                                else:
                                    act.wait_ge(split_used, S_FFN + split_in_block(b, 3) + 1)
                                act.activation(f_silu[:, a, :], bank[4 + a][:, 0:FB], ACT.Silu).then_inc(silu_done, 1)

            for a in range(NT):
                act.wait_ge(h_done, 2 * DEPTH * NT - NT + a + 1)
                act.activation(htok_hi[:, a, :], m_htok[:, a, :], ACT.Copy).then_inc(htok_split, 1)
            for a in range(NT):
                for half in range(2):
                    act.wait_ge(r_mm, 2 * a + half + 1)
                    act.activation(r_hT[:, 4 * half:4 * half + 4, P * a:P * a + P],
                                   bank[2 * a + half][:, :].rearrange("p (k n) -> p k n", k=4),
                                   ACT.Copy).then_inc(r_out, 1)
            act.wait_ge(gap_done, 1)
            act.activation(e2[:, :, :], gap[:, :, :], ACT.Exp).then_inc(gexp_done, 1)

            def gathered_hi(base):
                for half in range(2):
                    act.wait_ge(ga_mm, base * 4 + half + 1)
                    act.activation(hgT_hi[:, 4 * half:4 * half + 4, :],
                                   bank[2 + half][:, :].rearrange("p (k n) -> p k n", k=4),
                                   ACT.Copy).then_inc(ga_hi, 1)

            def expert_out_hi(turn):
                act.wait_ge(put_done, turn * 2 + 2)
                act.wait_ge(zero_mm, 1)
                act.wait_ge(split_used, turn * EXPERT_SPLITS + S_MOE)
                for half in range(2):
                    act.activation(y_hi[:, CB * half:CB * half + CB], bank[half][:, :], ACT.Copy,
                                   scale=slot_gate[:, 0:1]).then_inc(m_yh, 1)

            gathered_hi(0)
            act.wait_ge(m_add, 1)
            act.activation(put[:, :, :], m_acc[:, 0, 0:NT * P].rearrange("p (a n) -> p a n", a=NT), ACT.Copy)\
               .then_inc(put_done, 1)
            act.activation(slot_gate[:, :], eps_col[:, :], ACT.Copy).then_inc(put_done, 1)
            act.activation(e2[:, 0, :], eps_col[:, :], ACT.Silu).then_inc(act_step, 1)
            act.wait_ge(rounds_done, 1)
            n_turns = act.value_load(rounds[0:1, 0:1], min_val=NE, max_val=2 * NE)
            with act.Fori(0, n_turns) as i:
                ring = i * (16 * EXPERT_CHUNKS // RING)
                splits = i * EXPERT_SPLITS
                blocks = i * NBLK

                def silu_of(b):
                    act.wait_ge(split_used, splits + (S_MOE + split_in_block(b, 3) + 1))
                    act.activation(m_silu[:, :], bank[4 + b % 2][:, 0:FB], ACT.Silu).then_inc(m_sl, 1)

                def hidden_hi(b):
                    act.wait_ge(m_tm, blocks + (b + 1))
                    act.activation(mT_hi[:, :], bank[6][:, FB * (b % 2):FB * (b % 2) + FB], ACT.Copy).then_inc(m_th, 1)

                def down_hi(b):
                    n = N0 + EWHERE[("down", b)]
                    wait_chunk("down", n, ring)
                    for c in range(2):
                        split_hi(S_MOE + down_split(b, c), down_raw(n, c), flat, splits)

                for b in range(NBLK):
                    n = N0 + EWHERE[("gate", b)]
                    wait_chunk("gate", n, ring)
                    wait_chunk("up", n + 1, ring)
                    for q in range(4):
                        split_hi(S_MOE + split_in_block(b, q), gu_raw(n, q), pairs, splits)
                        if b and q == SILU_AFTER[b]:
                            silu_of(b - 1)
                        if b == 0 and q == 2:
                            expert_out_hi(i)
                    if b:
                        hidden_hi(b - 1)
                    if b == 2:
                        act.wait_ge(m_sc, i * 2 + 2)
                        act.wait_ge(pick_mm, i + 1)
                        act.activation(put[:, :, :], bank[7][:, 0:2 * P].rearrange("p (a n) -> p a n", a=NT),
                                       ACT.Copy).then_inc(put_done, 1)
                        act.activation(slot_gate[:, :], bank[7][:, 2 * P:2 * P + 1], ACT.Copy).then_inc(put_done, 1)
                    if b:
                        down_hi(b - 1)
                silu_of(NBLK - 1)
                down_hi(NBLK - 1)
                hidden_hi(NBLK - 1)
                gathered_hi(i + 1)
            expert_out_hi(n_turns)
            std_of_rows(2 * DEPTH)

        @blk.vector
        def _(dve):
            steps = [0]

            def then(ins):
                steps[0] += 1
                ins.then_inc(dve_step, 1)
                dve.wait_ge(dve_step, steps[0])

            def split_lo(s, count, src, like, splits=0):
                dve.wait_ge(hi_done, splits + (s + 1))
                dve.tensor_tensor(like(w_lo[:, s % NB, :]), src, like(w_hi[:, s % NB, :].bitcast(F32)),
                                  ALU.subtract).then_inc(split_done, 1)

            def flat(ap):
                return ap

            def pairs(ap):
                return ap.rearrange("p (g n) -> p g n", g=2)

            ada_no = [0]
            ada_evac = [0]

            def ada_out_block():
                i = ada_evac[0]
                ada_evac[0] += 1
                layer, j = ADA[i]
                piece, half = divmod(j, 2)
                dst = mod[:, piece, CB * half:CB * half + CB]
                dve.wait_ge(ada_mm, i + 1)
                if piece in (SC1, SC2):
                    if half == 0:
                        dve.wait_ge(gain_in, 16 * (2 * layer + (piece == SC2) + 1))
                    dve.scalar_tensor_tensor(out=dst, in0=bank[7][:, :], scalar=1.0,
                                             in1=gain[:, CB * half:CB * half + CB], op0=ALU.add,
                                             op1=ALU.mult).then_inc(ada_out, 1)
                    dve.wait_ge(ada_out, i + 1)
                    dve.sem_inc(gain_used, 1)
                else:
                    dve.tensor_copy(dst, bank[7][:, :]).then_inc(ada_out, 1)

            def ada_half(half):
                i = ada_no[0]
                layer, j = ADA[i]
                acc = ada_acc[:, i % 2, :]
                if half == 0:
                    if i >= 2:
                        dve.wait_ge(ada_mm, i - 1)
                    dve.wait_ge(bias_in, 16 * (i + 1))
                n = WHERE[("ada", layer, j, half)]
                dve.wait_ge(chunk_in[n % RING], landed(n))
                for q in range(4):
                    k = 4 * half + q
                    ins = dve.scalar_tensor_tensor(
                        out=acc, in0=raw[:, n % RING, CB * q:CB * q + CB], scalar=silu_c[:, k:k + 1],
                        in1=ada_bias[:, :] if k == 0 else acc, op0=ALU.mult, op1=ALU.add)
                    if k == 0:
                        ins.then_inc(bias_used, 1)
                        dve.wait_ge(bias_used, i + 1)
                    elif q < 3:
                        then(ins)
                    else:
                        ins.then_inc(split_done, 2)
                        dve.wait_ge(split_done, taken(n, 1))
                if half == 1:
                    ada_no[0] += 1
                    if ada_evac[0] < i:
                        ada_out_block()

            def ada_block():
                ada_half(0)
                ada_half(1)

            def ada_flush():
                while ada_evac[0] < ada_no[0]:
                    ada_out_block()

            def norm(i, a_piece, b_piece, dst):
                for a in range(NT):
                    dve.tensor_tensor_reduce(out=dst[:, a, :], in0=x[:, a, :], in1=x[:, a, :], scale=1.0,
                                             scalar=0.0, op0=ALU.mult, op1=ALU.add,
                                             accum_out=ssq[:, a:a + 1]).then_inc(ssq_done, 1)
                for a in range(NT):
                    dve.wait_ge(std_done, NT * i + a + 1)
                    then(dve.reciprocal(rstd[:, a:a + 1], std[:, a:a + 1]))
                    if b_piece is None:
                        dve.scalar_tensor_tensor(out=dst[:, a, :], in0=x[:, a, :], scalar=rstd[:, a:a + 1],
                                                 in1=gain[:, :], op0=ALU.mult, op1=ALU.mult).then_inc(out_ready, 1)
                        continue
                    then(dve.scalar_tensor_tensor(out=dst[:, a, :], in0=x[:, a, :], scalar=rstd[:, a:a + 1],
                                                  in1=mod[:, a_piece, :], op0=ALU.mult, op1=ALU.mult))
                    dve.tensor_tensor(dst[:, a, :], dst[:, a, :], mod[:, b_piece, :], ALU.add).then_inc(h_done, 1)

            def transposed_lo(hi, lo, i):
                for a in range(NT):
                    for half in range(2):
                        n = 4 * i + 2 * a + half
                        dve.wait_ge(tr_hi, n + 1)
                        dve.tensor_tensor(lo[:, 4 * half:4 * half + 4, P * a:P * a + P],
                                          bank[2 * a + half][:, :].rearrange("p (k n) -> p k n", k=4),
                                          hi[:, 4 * half:4 * half + 4, P * a:P * a + P].bitcast(F32),
                                          ALU.subtract).then_inc(tr_lo, 1)

            def add_scaled(src, piece, a, half, used, turn):
                dve.wait_ge(split_used, used)
                then(dve.tensor_tensor(y_scaled[:, turn % 2, :], src, mod[:, piece, CB * half:CB * half + CB], ALU.mult))
                xs = x[:, a, CB * half:CB * half + CB]
                dve.tensor_tensor(xs, xs, y_scaled[:, turn % 2, :], ALU.add).then_inc(x_step, 1)

            dve.wait_ge(silu_c_done, 1)
            dve.wait_ge(pool_step, 6)
            for _ in range(4):
                ada_block()
            ada_flush()
            dve.wait_ge(x_in, 16)
            dve.wait_ge(consts, 5)
            xcount = 0
            for layer in range(DEPTH):
                dve.wait_ge(ada_out, ada_evac[0])
                norm(2 * layer, SC1, SH1, h_tok)
                transposed_lo(hT_hi, hT_lo, 2 * layer if layer == 0 else 3)
                for j in range(INW // CB):
                    for half in range(2):
                        n = WHERE[("in", layer, j, half)]
                        for q in range(2):
                            split_lo(S_IN[layer] + 4 * j + 2 * half + q, taken(n, q),
                                     raw[:, n % RING, q * SUB:(q + 1) * SUB], flat)
                        ada_half(half)
                ada_flush()
                for half in range(2):
                    dve.wait_ge(ws_mm, 2 * layer + half + 1)
                    dve.tensor_tensor(wsT[:, 4 * half:4 * half + 4, :],
                                      bank[4 + half][:, :].rearrange("p (g n) -> p g n", g=4),
                                      upto[:, :].unsqueeze(1).to_broadcast([P, 4, P]), ALU.mult).then_inc(ws_out, 1)
                for a in range(NT):
                    dve.wait_ge(qk_mm, 4 * layer + NT + a + 1)
                    dve.tensor_copy(kT[:, :, P * a:P * a + P],
                                    bank[2 + a][:, :].rearrange("p (h n) -> p h n", h=NH)).then_inc(qk_out_v, 1)
                dve.wait_ge(z_out, NT * (INW // CB) * (layer + 1))
                for a in range(NT):
                    va = z[:, a, GW:2 * GW]
                    then(dve.tensor_tensor(vsq[:, :], va, va, ALU.mult))
                    then(dve.tensor_reduce(gstat[:, NG * a:NG * a + NG], vsq[:, :].rearrange("p (g n) -> p g n", g=NG),
                                           axis=AX.X, op=ALU.add))
                dve.sem_inc(vstat_done, 1)
                dve.wait_ge(mixer_in2, 80 * (layer + 1))
                for i in range(2):
                    then(dve.tensor_tensor(vsq[:, DH * i:DH * i + DH], lam_rows[:, 2 * i, :], lam_rows[:, 2 * i + 1, :], ALU.mult))
                then(dve.tensor_reduce(lam_sum[:, :], vsq[:, 0:2 * DH].rearrange("p (i n) -> p i n", i=2), axis=AX.X, op=ALU.add))
                dve.sem_inc(lam_dots, 1)
                lam_init = 0.8 - 0.6 * math.exp(-0.3 * layer)
                dve.wait_ge(vstd_done, layer + 1)
                then(dve.reciprocal(gstat[:, 0:16], gstat[:, 16:32]))
                for a in range(NT):
                    va = z[:, a, GW:2 * GW]
                    vg = va.rearrange("p (g n) -> p g n", g=NG)
                    then(dve.tensor_tensor(vg, vg, gstat[:, NG * a:NG * a + NG].unsqueeze(2).to_broadcast([P, NG, GD]), ALU.mult))
                    dve.tensor_tensor(va, va, vgain[:, :], ALU.mult).then_inc(v_done, 1)
                dve.wait_ge(lam_exps, layer + 1)
                then(dve.tensor_tensor(lam[:, :], lam_exp[:, 0:1], lam_exp[:, 1:2], ALU.subtract))
                then(dve.tensor_scalar(lam[:, :], lam[:, :], lam_init, None, ALU.add))

                def head_max(h):
                    dve.wait_ge(sc_mm, NH * layer + h + 1)
                    for m in range(2):
                        for a in range(NT):
                            cols = slice(0, P) if a == 0 else slice(P, 3 * P)
                            ins = dve.reduce_max(hstat[:, 2 * m + a:2 * m + a + 1], bank[2 * (h % 2) + m][:, cols], AX.X)
                            then(ins)
                    if h:
                        dve.wait_ge(exp_done, 4 * (NH * layer + h))
                    dve.tensor_scalar(hstat[:, 4:8], hstat[:, 0:4], -DH ** -0.5, None, ALU.mult).then_inc(negmax, 1)

                def head_maps(h):
                    dve.wait_ge(exp_done, 4 * (NH * layer + h + 1))
                    then(dve.reciprocal(hstat[:, 12:16], hstat[:, 8:12]))
                    then(dve.tensor_tensor(hstat[:, 14:16], hstat[:, 14:16], lam[:, 0:1].to_broadcast([P, 2]), ALU.mult))
                    for a in range(NT):
                        cols = slice(0, P) if a == 0 else slice(P, 3 * P)
                        then(dve.tensor_scalar(prob[:, 1, cols], prob[:, 1, cols], hstat[:, 14 + a:15 + a], None, ALU.mult))
                        then(dve.scalar_tensor_tensor(out=prob[:, 0, cols], in0=prob[:, 0, cols],
                                                      scalar=hstat[:, 12 + a:13 + a], in1=prob[:, 1, cols],
                                                      op0=ALU.mult, op1=ALU.subtract))
                    dve.sem_inc(a_done, 1)

                head_max(0)
                for half in range(2):
                    dve.wait_ge(vm_mm, 2 * layer + half + 1)
                    if half == 0:
                        dve.wait_ge(mixer_in, 48 * (layer + 1))
                    for g in range(4):
                        gg = 4 * half + g
                        ug = z[:, :, GD * gg:GD * gg + GD]
                        dve.scalar_tensor_tensor(out=ug, in0=bank[4 + half][:, 2 * GD * g:2 * GD * g + 2 * GD].rearrange("p (a n) -> p a n", a=NT),
                                                 scalar=bsT[:, gg:gg + 1], in1=ug, op0=ALU.add, op1=ALU.mult).then_inc(ua_done, 1)
                for h in range(NH):
                    head_maps(h)
                    if h + 1 < NH:
                        head_max(h + 1)
                dve.wait_ge(o_out, NH * (layer + 1))
                for a in range(NT):
                    oa = z[:, a, 2 * GW:3 * GW]
                    then(dve.tensor_tensor(vsq[:, :], oa, oa, ALU.mult))
                    then(dve.tensor_reduce(gstat[:, 32 + NH * a:32 + NH * a + NH], vsq[:, :].rearrange("p (h n) -> p h n", h=NH),
                                           axis=AX.X, op=ALU.add))
                dve.sem_inc(ostat_done, 1)
                dve.wait_ge(ostd_done, layer + 1)
                then(dve.reciprocal(gstat[:, 48:56], gstat[:, 40:48]))
                then(dve.tensor_scalar(gstat[:, 48:56], gstat[:, 48:56], 1.0 - lam_init, None, ALU.mult))
                for a in range(NT):
                    oh = z[:, a, 2 * GW:3 * GW].rearrange("p (h n) -> p h n", h=NH)
                    then(dve.tensor_tensor(oh, oh, gstat[:, 48 + NH * a:48 + NH * a + NH].unsqueeze(2).to_broadcast([P, NH, DV]), ALU.mult))
                    dve.tensor_tensor(oh, oh, subln[:, :].unsqueeze(1).to_broadcast([P, NH, DV]), ALU.mult).then_inc(ob_done, 1)
                transposed_lo(hT_hi, hT_lo, 1 if layer == 0 else 4)
                for j in range(D // CB):
                    for half in range(2):
                        n = WHERE[("out", layer, j, half)]
                        for q in range(2):
                            split_lo(S_OUT[layer] + 4 * j + 2 * half + q, taken(n, q),
                                     raw[:, n % RING, q * SUB:(q + 1) * SUB], flat)
                    if j == 0:
                        ada_block()
                ada_flush()
                dve.wait_ge(ada_out, ada_evac[0])
                for j in range(D // CB):
                    for a in range(NT):
                        add_scaled(bank[2 * (j % 2) + a][:, :], G1, a, j, S_OUT[layer] + 4 * (j + 1), a)
                        xcount += 1
                dve.wait_ge(x_step, xcount)
                if layer == 0:
                    norm(1, SC2, SH2, h_tok)
                    transposed_lo(hT_hi, hT_lo, 2)
                    for b in range(NBLK + 1):
                        if b < NBLK:
                            n = WHERE[("gate", 0, b, 0)]
                            for q in range(4):
                                split_lo(S_FFN + split_in_block(b, q), taken(n, q), gu_raw(n, q), pairs)
                        if BESIDE_FFN[b]:
                            ada_half(0)
                        if b:
                            dve.wait_ge(fT_hi_done, b)
                            dve.tensor_tensor(fT_lo[:, :, :], bank[6][:, :].rearrange("p (a n) -> p a n", a=NT),
                                              fT_hi[:, :, :].bitcast(F32), ALU.subtract).then_inc(fT_lo_done, 1)
                            n = WHERE[("down", 0, b - 1, 0)]
                            for c in range(2):
                                split_lo(S_FFN + down_split(b - 1, c), taken(n, c), down_raw(n, c), flat)
                        if b < NBLK:
                            for a in range(NT):
                                dve.wait_ge(silu_done, NT * b + a + 1)
                                dve.tensor_tensor(f_act[:, a, :], f_silu[:, a, :], bank[4 + a][:, FB:2 * FB],
                                                  ALU.mult).then_inc(act_done, 1)
                        if BESIDE_FFN[b]:
                            ada_half(1)
                        elif ada_evac[0] < ada_no[0]:
                            ada_flush()
                    dve.wait_ge(ada_out, ada_evac[0])
                    for a in range(NT):
                        for half in range(2):
                            add_scaled(bank[2 * a + half][:, :], G2, a, half, S_FFN + EXPERT_SPLITS, half)
                            xcount += 1
                    dve.wait_ge(x_step, xcount)
                else:
                    norm(3, SC2, SH2, m_htok)

            for a in range(NT):
                dve.wait_ge(htok_split, a + 1)
                then(dve.tensor_tensor(htok_lo[:, a, :], m_htok[:, a, :], htok_hi[:, a, :].bitcast(F32), ALU.subtract))
            dve.wait_ge(logit_mm, 1)
            then(dve.tensor_copy(logit[:, :, :], bank[4][:, 0:NT * NE].rearrange("p (a e) -> p a e", a=NT)))
            for a in range(NT):
                then(dve.max(top[:, a, :], logit[:, a, :]))
                then(dve.max_index(top_i[:, a, :], top[:, a, :], logit[:, a, :]))
            then(dve.tensor_copy(top_f[:, :, :], top_i[:, :, :]))
            dve.tensor_tensor(gap[:, :, :], top[:, :, 1:2], top[:, :, 0:1], ALU.subtract).then_inc(gap_done, 1)
            dve.wait_ge(gexp_done, 1)
            then(dve.tensor_scalar(wsum[:, :, :], e2[:, :, :], 1.0, None, ALU.add))
            then(dve.reciprocal(w1[:, :, :], wsum[:, :, :]))
            then(dve.tensor_tensor(w2[:, :, :], e2[:, :, :], w1[:, :, :], ALU.mult))
            for a in range(NT):
                for r in range(2):
                    then(dve.tensor_scalar(hit[:, a, r, :], slot_no[:, 0:NE], top_f[:, a, r:r + 1], None, ALU.is_equal))
                dve.tensor_tensor(mask[:, a, :], hit[:, a, 0, :], hit[:, a, 1, :], ALU.add).then_inc(mask_done, 1)
            dve.wait_ge(mask_done, NT)
            for a in range(NT):
                then(dve.tensor_scalar(hit[:, a, 1, :], hit[:, a, 1, :], w2[:, a, 0:1], None, ALU.mult))
                for again in range(2):
                    then(dve.scalar_tensor_tensor(out=gate_of[:, a, NE * again:NE * again + NE], in0=hit[:, a, 0, :],
                                                  scalar=w1[:, a, 0:1], in1=hit[:, a, 1, :], op0=ALU.mult, op1=ALU.add))
            then(dve.memset(slot_of[:, :, 2 * NE:2 * NE + 1], -1.0))
            then(dve.memset(gate_of[:, :, 2 * NE:2 * NE + 1], 0.0))
            dve.wait_ge(count_mm, 1)
            for a in range(NT):
                then(dve.scalar_tensor_tensor(out=slot_of[:, a, 0:NE], in0=bank[4][:, 32 + NE * a:32 + NE * a + NE],
                                              scalar=1.0, in1=mask[:, a, :], op0=ALU.add, op1=ALU.mult))
                then(dve.tensor_scalar(slot_of[:, a, NE:2 * NE], slot_of[:, a, 0:NE], -1.0 - P, None, ALU.add))
                then(dve.tensor_scalar(slot_of[:, a, 0:NE], slot_of[:, a, 0:NE], -1.0, None, ALU.add))
            then(dve.reduce_max(most[:, :], bank[4][:, 64:64 + NE], AX.X))
            then(dve.tensor_scalar(rounds_f[:, :], most[:, :], float(P), float(NE), ALU.is_gt, ALU.mult))
            then(dve.tensor_scalar(rounds_f[:, :], rounds_f[:, :], float(NE), None, ALU.add))
            dve.tensor_copy(rounds[:, :], rounds_f[:, :]).then_inc(rounds_done, 1)
            dve.memset(m_acc[:, :, :], 0.0).then_inc(m_add, 1)

            def make_pick(i, count):
                for a in range(NT):
                    dve.tensor_scalar(pick[:, a, :], slot_no[:, :], slot_of[:, a, i], None, ALU.is_equal)\
                       .then_inc(pick_done, 1)
                    dve.tensor_copy(gate_col[:, a:a + 1], gate_of[:, a, i]).then_inc(pick_done, 1)

            def gathered_lo(base):
                for half in range(2):
                    dve.wait_ge(ga_mm, base * 4 + (2 + half + 1))
                    dve.tensor_copy(hgT_lo[:, 4 * half:4 * half + 4, :],
                                    bank[(5, 7)[half]][:, :].rearrange("p (k n) -> p k n", k=4)).then_inc(ga_lo, 1)

            def expert_out_lo(turn):
                for half in range(2):
                    dve.wait_ge(m_yh, turn * 2 + (half + 1))
                    dve.scalar_tensor_tensor(out=y_lo[:, CB * half:CB * half + CB], in0=bank[half][:, :],
                                             scalar=slot_gate[:, 0:1], in1=y_hi[:, CB * half:CB * half + CB].bitcast(F32),
                                             op0=ALU.mult, op1=ALU.subtract).then_inc(m_yl, 1)

            def expert_add(turn):
                dve.wait_ge(m_add, turn * 4 + 1)
                for half in range(2):
                    dve.wait_ge(m_sc, turn * 2 + (half + 1))
                    for a in range(NT):
                        acc = m_acc[:, a, CB * half:CB * half + CB]
                        dve.tensor_tensor(acc, acc, bank[((2, 3), (5, 7))[half][a]][:, :], ALU.add).then_inc(m_add, 1)

            make_pick(slice(0, 1), 0)
            gathered_lo(0)
            dve.wait_ge(rounds_done, 1)
            n_turns = dve.value_load(rounds[0:1, 0:1], min_val=NE, max_val=2 * NE)
            with dve.Fori(0, n_turns) as i:
                splits = i * EXPERT_SPLITS
                blocks = i * NBLK

                def gated(b):
                    dve.wait_ge(m_sl, blocks + (b + 1))
                    dve.tensor_tensor(m_act[:, :], m_silu[:, :], bank[4 + b % 2][:, FB:2 * FB], ALU.mult)\
                       .then_inc(m_ac, 1)

                def hidden_lo(b):
                    dve.wait_ge(m_th, blocks + (b + 1))
                    dve.tensor_tensor(mT_lo[:, :], bank[6][:, FB * (b % 2):FB * (b % 2) + FB],
                                      mT_hi[:, :].bitcast(F32), ALU.subtract).then_inc(m_tl, 1)

                def down_lo(b):
                    n = N0 + EWHERE[("down", b)]
                    for c in range(2):
                        split_lo(S_MOE + down_split(b, c), taken(n, c), down_raw(n, c), flat, splits)

                for b in range(NBLK):
                    n = N0 + EWHERE[("gate", b)]
                    for q in range(4):
                        split_lo(S_MOE + split_in_block(b, q), taken(n, q), gu_raw(n, q), pairs, splits)
                        if b and q == SILU_AFTER[b]:
                            gated(b - 1)
                        if b == 0 and q == 2:
                            expert_out_lo(i)
                    if b == 0:
                        expert_add(i)
                    else:
                        hidden_lo(b - 1)
                        down_lo(b - 1)
                    if b == 5:
                        dve.wait_ge(pick_mm, i + 1)
                        make_pick(bass.ds(i + 1, 1), 0)
                gated(NBLK - 1)
                down_lo(NBLK - 1)
                hidden_lo(NBLK - 1)
                gathered_lo(i + 1)
            expert_out_lo(n_turns)
            expert_add(n_turns)
            dve.wait_ge(m_add, n_turns * 4 + 5)
            for a in range(NT):
                for half in range(2):
                    then(dve.tensor_tensor(f_scaled[:, half, :], m_acc[:, a, CB * half:CB * half + CB],
                                           mod[:, G2, CB * half:CB * half + CB], ALU.mult))
                    xs = x[:, a, CB * half:CB * half + CB]
                    then(dve.tensor_tensor(xs, xs, f_scaled[:, half, :], ALU.add))
            dve.wait_ge(gain_in, 16 * 5)
            norm(4, None, None, h_tok)

        @blk.tensor
        def _(pe):
            def three(dst, a_hi, a_lo, b_hi, b_lo, first, last):
                pe.matmul(dst, a_hi, b_hi, start=first, stop=False)
                pe.matmul(dst, a_lo, b_hi, start=False, stop=False)
                return pe.matmul(dst, a_hi, b_lo, start=False, stop=last)

            ada_no = [0]

            def ada_sum():
                i = ada_no[0]
                ada_no[0] += 1
                layer, j = ADA[i]
                pe.wait_ge(split_done, taken(WHERE[("ada", layer, j, 1)], 1))
                if i:
                    pe.wait_ge(ada_out, i)
                pe.matmul(bank[7][:, :], ones[:, :], ada_acc[:, i % 2, :], start=True, stop=True).then_inc(ada_mm, 1)

            def transposes(i, src, ready):
                for a in range(NT):
                    ready(a)
                    for half in range(2):
                        for k in range(4):
                            last = pe.transpose(bank[2 * a + half][:, P * k:P * k + P], src(a, 4 * half + k), ident[:, :])
                        last.then_inc(tr_mm, 1)

            def project(kind, layer, s0, blocks, evacuated):
                for j in range(blocks):
                    for sub in range(4):
                        if kind == "in" and sub == 2 and j:
                            ada_sum()
                        s = s0 + 4 * j + sub
                        pe.wait_ge(split_done, taken(WHERE[(kind, layer, j, sub // 2)], sub % 2))
                        if sub == 0:
                            evacuated(j)
                        for a in range(NT):
                            for kk in range(2):
                                k = 2 * sub + kk
                                cols = slice(CB * kk, CB * kk + CB)
                                last = three(bank[2 * (j % 2) + a][:, :], hT_hi[:, k, P * a:P * a + P],
                                             hT_lo[:, k, P * a:P * a + P], w_hi[:, s % NB, cols], w_lo[:, s % NB, cols],
                                             k == 0, k == KT - 1)
                        last.then_inc(split_used, 1)

            pe.wait_ge(consts, 5)
            pe.wait_ge(first_in, 16)
            pe.transpose(bank[6][:, 0:KT], c_rows[:, :], ident[0:KT, 0:KT]).then_inc(c_mm, 1)
            for _ in range(4):
                ada_sum()
            for layer in range(DEPTH):
                transposes(2 * layer if layer == 0 else 3, lambda a, k: h_tok[:, a, P * k:P * k + P],
                           lambda a: pe.wait_ge(h_done, 2 * NT * layer + a + 1))
                seen = 4 * ((2 * layer if layer == 0 else 3) + 1)
                pe.wait_ge(tr_lo, seen)

                def z_free(j):
                    if j >= 2:
                        pe.wait_ge(z_out, NT * ((INW // CB) * layer + j - 1))

                project("in", layer, S_IN[layer], INW // CB, z_free)
                ada_sum()
                pe.wait_ge(mixer_in, 48 * (layer + 1))
                for half in range(2):
                    for g in range(4):
                        last = pe.transpose(bank[4 + half][:, P * g:P * g + P], ws_raw[:, 4 * half + g, :], ident[:, :])
                    last.then_inc(ws_mm, 1)
                pe.wait_ge(z_out, NT * (INW // CB) * (layer + 1))
                for part in range(2):
                    for a in range(NT):
                        for h in range(NH):
                            c0 = 2 * GW + NH * DV * part + DV * h
                            last = pe.transpose(bank[2 * part + a][:, P * h:P * h + P], z[:, a, c0:c0 + DV], ident[:, :])
                        last.then_inc(qk_mm, 1)

                def scores(h):
                    for a in range(NT):
                        for m in range(2):
                            dst = bank[2 * (h % 2) + m]
                            cols = slice(0, P) if a == 0 else slice(P, 3 * P)
                            rows = slice(DH * m, DH * m + DH)
                            pe.matmul(dst[:, cols], qT[rows, h, P * a:P * a + P], kT[rows, h, 0:P * (a + 1)],
                                      start=(a == 0), stop=False, skip_group_check=True)
                    for a in range(NT):
                        for m in range(2):
                            cols = slice(P * 2 * a, P * 2 * a + P)
                            last = pe.matmul(bank[2 * (h % 2) + m][:, cols], ident[:, :], future[:, :],
                                             start=False, stop=True, skip_group_check=True)
                    last.then_inc(sc_mm, 1)

                pe.wait_ge(qk_out_a, NT * (layer + 1))
                pe.wait_ge(qk_out_v, NT * (layer + 1))
                scores(0)
                pe.wait_ge(ws_out, 2 * (layer + 1))
                pe.wait_ge(v_done, NT * (layer + 1))
                for half in range(2):
                    for g in range(4):
                        gg = 4 * half + g
                        last = pe.matmul(bank[4 + half][:, 2 * GD * g:2 * GD * g + 2 * GD].rearrange("p (a n) -> p a n", a=NT),
                                         wsT[:, gg, :], z[:, :, GW + GD * gg:GW + GD * gg + GD], start=True, stop=True)
                    last.then_inc(vm_mm, 1)
                scores(1)
                for h in range(NH):
                    pe.wait_ge(a_done, NH * layer + h + 1)
                    if h < 2:
                        pe.wait_ge(ua_done, 8 * layer + 4 * (h + 1))
                    for i in range(3):
                        last = pe.transpose(bank[4 + h % 2][:, P * i:P * i + P], prob[:, 0, P * i:P * i + P], ident[:, :])
                    last.then_inc(at_mm, 1)
                    if 1 <= h < NH - 1:
                        scores(h + 1)
                    pe.wait_ge(at_out, NH * layer + h + 1)
                    if h >= 2:
                        pe.wait_ge(o_out, NH * layer + h - 1)
                    v0 = 2 * GW + 2 * NH * DV + DV * h
                    dst = FB * (h % 2)
                    pe.matmul(bank[6][:, dst:dst + DV], aT[:, 0:P], z[:, 0, v0:v0 + DV], start=True, stop=True)
                    pe.matmul(bank[6][:, dst + DV:dst + 2 * DV], aT[:, P:2 * P], z[:, 0, v0:v0 + DV], start=True, stop=False)
                    pe.matmul(bank[6][:, dst + DV:dst + 2 * DV], aT[:, 2 * P:3 * P], z[:, 1, v0:v0 + DV],
                              start=False, stop=True).then_inc(o_mm, 1)

                def mix_tile(a, k):
                    c0 = P * k if k < 4 else 2 * GW + P * (k - 4)
                    return z[:, a, c0:c0 + P]

                transposes(1 if layer == 0 else 4, mix_tile, lambda a: pe.wait_ge(ob_done, NT * layer + a + 1))
                pe.wait_ge(tr_lo, 4 * ((1 if layer == 0 else 4) + 1))
                project("out", layer, S_OUT[layer], D // CB, lambda j: None)
                ada_sum()
                if layer == 0:
                    transposes(2, lambda a, k: h_tok[:, a, P * k:P * k + P], lambda a: pe.wait_ge(h_done, NT + a + 1))
                    pe.wait_ge(tr_lo, 4 * 3)
                    for b in range(NBLK + 1):
                        for q in range(4):
                            if q == 2 and b and BESIDE_FFN[b - 1]:
                                ada_sum()
                            if b < NBLK:
                                s = S_FFN + split_in_block(b, q)
                                pe.wait_ge(split_done, taken(WHERE[("gate", 0, b, 0)], q))
                                if q == 0 and b:
                                    pe.wait_ge(act_done, NT * b)
                                for a in range(NT):
                                    for kk in range(2):
                                        k = 2 * q + kk
                                        wh = w_hi[:, s % NB, :].rearrange("p (g k n) -> p g k n", g=2, k=2)[:, :, kk, :]
                                        wl = w_lo[:, s % NB, :].rearrange("p (g k n) -> p g k n", g=2, k=2)[:, :, kk, :]
                                        last = three(bank[4 + a][:, :].rearrange("p (g n) -> p g n", g=2),
                                                     hT_hi[:, k, P * a:P * a + P], hT_lo[:, k, P * a:P * a + P], wh, wl,
                                                     k == 0, k == KT - 1)
                                    if q == 3 and a == 0:
                                        last.then_inc(gu_mm, 1)
                                last.then_inc(split_used, 1)
                            if q == 1 and b:
                                for a in range(NT):
                                    pe.wait_ge(act_done, NT * (b - 1) + a + 1)
                                    for c in range(2):
                                        last = pe.transpose(bank[6][:, FB * a + P * c:FB * a + P * c + P],
                                                            f_act[:, a, P * c:P * c + P], ident[:, :])
                                last.then_inc(fT_mm, 1)
                        if b:
                            pe.wait_ge(fT_lo_done, b)
                            for c in range(2):
                                s = S_FFN + down_split(b - 1, c)
                                pe.wait_ge(split_done, taken(WHERE[("down", 0, b - 1, 0)], c))
                                for a in range(NT):
                                    for half in range(2):
                                        cols = slice(CB * half, CB * half + CB)
                                        last = three(bank[2 * a + half][:, :], fT_hi[:, a, P * c:P * c + P],
                                                     fT_lo[:, a, P * c:P * c + P], w_hi[:, s % NB, cols], w_lo[:, s % NB, cols],
                                                     b == 1 and c == 0, b == NBLK and c == 1)
                                last.then_inc(split_used, 1)

            for a in range(NT):
                pe.wait_ge(h_done, 3 * NT + a + 1)
                for half in range(2):
                    for k in range(4):
                        last = pe.transpose(bank[2 * a + half][:, P * k:P * k + P],
                                            m_htok[:, a, P * (4 * half + k):P * (4 * half + k) + P], ident[:, :])
                    last.then_inc(r_mm, 1)
            pe.wait_ge(route_in, 16)
            pe.wait_ge(r_out, 4)
            for a in range(NT):
                for k in range(KT):
                    last = pe.matmul(bank[4][:, NE * a:NE * a + NE], r_hT[:, k, P * a:P * a + P], w_route[:, k, :],
                                     start=(k == 0), stop=(k == KT - 1))
            last.then_inc(logit_mm, 1)
            pe.wait_ge(mask_done, NT)
            pe.matmul(bank[4][:, 32:32 + NE], before[:, :], mask[:, 0, :], start=True, stop=True)
            pe.matmul(bank[4][:, 40:40 + NE], ones[:, :], mask[:, 0, :], start=True, stop=False)
            pe.matmul(bank[4][:, 40:40 + NE], before[:, :], mask[:, 1, :], start=False, stop=True)
            pe.matmul(bank[4][:, 64:64 + NE], ones[:, :], mask[:, 0, :], start=True, stop=False)
            pe.matmul(bank[4][:, 64:64 + NE], ones[:, :], mask[:, 1, :], start=False, stop=True).then_inc(count_mm, 1)

            def gather():
                for g, src in enumerate((htok_hi, htok_lo)):
                    for half in range(2):
                        dst = bank[(2, 3, 5, 7)[2 * g + half]]
                        for k in range(4):
                            c0 = P * (4 * half + k)
                            for a in range(NT):
                                last = pe.matmul(dst[:, P * k:P * k + P], src[:, a, c0:c0 + P], pick[:, a, :],
                                                 start=(a == 0), stop=(a == NT - 1))
                        last.then_inc(ga_mm, 1)

            def scatter(turn):
                pe.wait_ge(put_done, turn * 2 + 2)
                pe.wait_ge(ga_hi, turn * 2 + 2)
                pe.wait_ge(ga_lo, turn * 2 + 2)
                for half in range(2):
                    cols = slice(CB * half, CB * half + CB)
                    pe.wait_ge(m_yl, turn * 2 + (half + 1))
                    for a in range(NT):
                        dst = bank[((2, 3), (5, 7))[half][a]][:, :]
                        pe.matmul(dst, put[:, a, :], y_hi[:, cols], start=True, stop=False)
                        last = pe.matmul(dst, put[:, a, :], y_lo[:, cols], start=False, stop=True)
                    last.then_inc(m_sc, 1)

            pe.wait_ge(pick_done, 4)
            gather()
            pe.wait_ge(m_add, 1)
            for half in range(2):
                last = pe.matmul(bank[half][:, :], ones[:, :], m_acc[:, 0, 0:CB], start=True, stop=True)
            last.then_inc(zero_mm, 1)
            pe.wait_ge(rounds_done, 1)
            n_turns = pe.value_load(rounds[0:1, 0:1], min_val=NE, max_val=2 * NE)
            with pe.Fori(0, n_turns) as i:
                splits = i * EXPERT_SPLITS
                blocks = i * NBLK
                pe.wait_ge(ga_hi, i * 2 + 2)
                pe.wait_ge(ga_lo, i * 2 + 2)
                for b in range(NBLK + 1):
                    if b == 1:
                        pe.wait_ge(m_add, i * 4 + 5)
                    for q in range(4):
                        if b < NBLK:
                            s = S_MOE + split_in_block(b, q)
                            pe.wait_ge(split_done, splits + taken(N0 + EWHERE[("gate", b)], q))
                            for kk in range(2):
                                k = 2 * q + kk
                                wh = w_hi[:, s % NB, :].rearrange("p (g k n) -> p g k n", g=2, k=2)[:, :, kk, :]
                                wl = w_lo[:, s % NB, :].rearrange("p (g k n) -> p g k n", g=2, k=2)[:, :, kk, :]
                                last = three(bank[4 + b % 2][:, :].rearrange("p (g n) -> p g n", g=2),
                                             hgT_hi[:, k, :], hgT_lo[:, k, :], wh, wl, k == 0, k == KT - 1)
                            last.then_inc(split_used, 1)
                        if q == 2 and b == 0:
                            scatter(i)
                        if b and q == 1 + SILU_AFTER[min(b, NBLK - 1)]:
                            pe.wait_ge(m_ac, blocks + b)
                            for c in range(2):
                                last = pe.transpose(bank[6][:, FB * ((b - 1) % 2) + P * c:FB * ((b - 1) % 2) + P * c + P],
                                                    m_act[:, P * c:P * c + P], ident[:, :])
                            last.then_inc(m_tm, 1)
                        if b == 2 and q == 1:
                            for a in range(NT):
                                pe.transpose(bank[7][:, P * a:P * a + P], pick[:, a, :].bitcast(F32), ident[:, :])
                            for a in range(NT):
                                last = pe.matmul(bank[7][:, 2 * P:2 * P + 1], pick[:, a, :].bitcast(F32), gate_col[:, a:a + 1],
                                                 start=(a == 0), stop=(a == NT - 1))
                            last.then_inc(pick_mm, 1)
                    if b == NBLK:
                        pe.wait_ge(pick_done, i * 4 + 8)
                        gather()
                    if b:
                        pe.wait_ge(m_tl, blocks + b)
                        for c in range(2):
                            s = S_MOE + down_split(b - 1, c)
                            pe.wait_ge(split_done, splits + taken(N0 + EWHERE[("down", b - 1)], c))
                            for half in range(2):
                                cols = slice(CB * half, CB * half + CB)
                                last = three(bank[half][:, :], mT_hi[:, P * c:P * c + P], mT_lo[:, P * c:P * c + P],
                                             w_hi[:, s % NB, cols], w_lo[:, s % NB, cols],
                                             b == 1 and c == 0, b == NBLK and c == 1)
                            last.then_inc(split_used, 1)
            scatter(n_turns)


_IN = ["x", "c", "w_ada", "b_ada", "norm1_g", "norm2_g", "w_in", "w_out", "gmlp_vnorm_g", "gmlp_ws", "gmlp_bs",
       "lam_q1", "lam_k1", "lam_q2", "lam_k2", "diff_subln_g", "ffn_w_gate", "ffn_w_up", "ffn_w_down",
       "w_router", "moe_w_gate", "moe_w_up", "moe_w_down", "final_g"]


def kernel(**inputs):
    import concourse.bacc as bacc
    from concourse.bass_utils import run_bass_kernel_spmd

    nc = bacc.Bacc("TRN2", target_bir_lowering=False, num_devices=1)
    arrays, tensors = {}, {}
    for name in _IN:
        a = np.ascontiguousarray(inputs[name])
        arrays["in_" + name] = a
        tensors[name] = nc.dram_tensor("in_" + name, a.shape, mybir.dt.from_np(a.dtype), kind="ExternalInput").ap()
    out = nc.dram_tensor("out", (SEQ, D), F32, kind="ExternalOutput").ap()
    trunk(nc, tensors, out)
    r = run_bass_kernel_spmd(nc, [arrays], core_ids=[0])
    return np.asarray(r.results[0]["out"]).reshape(1, SEQ, D)
```

```python
import math
from contextlib import ExitStack

import numpy as np
import concourse.bass as bass
from concourse import mybir
from concourse.alu_op_type import AluOpType as ALU

ACT = mybir.ActivationFunctionType
AX = mybir.AxisListType
F32 = mybir.dt.float32
F32R = mybir.dt.float32r
I32 = mybir.dt.int32
U32 = mybir.dt.uint32

P = 128
D = 1024
KT = D // P
SEQ = 256
NT = SEQ // P
DEPTH = 2
GW = 512
NG = 8
GD = GW // NG
NH = 4
DV = 128
DH = 64
INW = 2 * GW + 3 * NH * DV
FF = 2816
NE = 8
FB = 256
NBLK = FF // FB
CB = 512
EPS = 1e-6
NEG = -1e30
RING = 11
NB = 3
CHUNK = 2048
SUB = 1024
MOD_BLOCKS = 12
SPLITS_PER_BLOCK = 6
EXPERT_CHUNKS = 3 * NBLK
EXPERT_SPLITS = SPLITS_PER_BLOCK * NBLK
SILU_AFTER = [None, 1] + [0] * (NBLK - 2)
BY_HALF = [(0, 0), (1, 0), (0, 1), (1, 1)]
BY_TILE = [(0, 0), (0, 1), (1, 0), (1, 1)]
SH1, SC1, G1, SH2, SC2, G2 = range(6)


BESIDE_IN = [[(0, 4), (0, 5), (0, 6), (0, 7), (0, 8)], [(1, 6), (1, 7), (1, 8), (1, 9), (1, 10)]]
BESIDE_OUT = [(0, 9), (1, 11)]
BESIDE_FFN = [(0, 10), (0, 11), (1, 0), (1, 1), (1, 2), (1, 3), (1, 4), (1, 5), None, None, None, None]


def chunk_stream():
    s = [("ada", 0, j, half) for j in range(4) for half in range(2)]
    for layer in range(DEPTH):
        for j in range(INW // CB):
            for half in range(2):
                s.append(("in", layer, j, half))
                s.append(("ada", *BESIDE_IN[layer][j], half))
        for j in range(D // CB):
            s += [("out", layer, j, half) for half in range(2)]
            if j == 0:
                s += [("ada", *BESIDE_OUT[layer], half) for half in range(2)]
        if layer == 0:
            for b in range(NBLK + 1):
                if b < NBLK:
                    s += [("gate", 0, b, 0), ("up", 0, b, 0)]
                if BESIDE_FFN[b]:
                    s.append(("ada", *BESIDE_FFN[b], 0))
                if b >= 1:
                    s.append(("down", 0, b - 1, 0))
                if BESIDE_FFN[b]:
                    s.append(("ada", *BESIDE_FFN[b], 1))
    return s


def expert_chunks():
    s = []
    for b in range(NBLK + 1):
        if b < NBLK:
            s += [("gate", b), ("up", b)]
        if b >= 1:
            s.append(("down", b - 1))
    return s


def trunk(nc, t, out):
    STREAM = chunk_stream()
    WHERE = {c: n for n, c in enumerate(STREAM)}
    ADA = [(c[1], c[2]) for c in STREAM if c[0] == "ada" and c[3] == 0]
    N0 = len(STREAM)
    EXPERT = expert_chunks()
    EWHERE = {c: n for n, c in enumerate(EXPERT)}
    S_IN = [0, 0]
    S_OUT = [0, 0]
    S_IN[0] = 0
    S_OUT[0] = S_IN[0] + 4 * (INW // CB)
    S_FFN = S_OUT[0] + 4 * (D // CB)
    S_IN[1] = S_FFN + EXPERT_SPLITS
    S_OUT[1] = S_IN[1] + 4 * (INW // CB)
    S_MOE = S_OUT[1] + 4 * (D // CB)
    assert S_MOE % NB == 0 or True

    def split_in_block(b, q):
        return 0 + q if b == 0 else 4 + (b - 1) * 6 + q

    def down_split(b, c):
        return (4 + b * 6 + 4 + c) if b + 1 < NBLK else 4 + b * 6 + c

    ctx = ExitStack()
    with ctx:
        at = [(nc.sbuf_base + 63) // 64 * 64]

        def sb(name, shape, dt=F32, offset=None):
            size = int(np.prod(shape[1:])) * 4
            size = (size + 31) // 32 * 32
            where = at[0] if offset is None else offset
            assert where + size <= nc.sbuf_usable_end, (name, where + size)
            h = nc.alloc_sbuf_tensor_at(name, shape, dt, offset=where)
            if offset is None:
                at[0] += size
            return h

        raw = sb("raw", [P, RING, CHUNK])
        w_hi = sb("w_hi", [P, NB, SUB], F32R)
        w_lo = sb("w_lo", [P, NB, SUB], F32R)
        mod = sb("mod", [P, 6, D])
        x = sb("x", [P, NT, D])
        gain = sb("gain", [P, D])
        ident = sb("ident", [P, P])
        ones = sb("ones", [P, P])
        before = sb("before", [P, P])
        upto = sb("upto", [P, P])
        future = sb("future", [P, P])
        slot_no = sb("slot_no", [P, P])
        ada_acc = sb("ada_acc", [P, 2, CB])
        ada_bias = sb("ada_bias", [P, CB])
        b_rows = sb("b_rows", [P, CB])
        silu_c = sb("silu_c", [P, KT])
        c_rows = sb("c_rows", [KT, P])
        eps_col = sb("eps_col", [P, 1])
        ssq = sb("ssq", [P, NT])
        std = sb("std", [P, NT])
        rstd = sb("rstd", [P, NT])
        lam_sum = sb("lam_sum", [P, 2, DEPTH])
        lam_exp = sb("lam_exp", [P, 2, DEPTH])
        lam = sb("lam", [P, DEPTH])
        w_route = sb("w_route", [P, KT, NE])
        base = at[0]
        hT_hi = sb("hT_hi", [P, KT, SEQ], F32R)
        hT_lo = sb("hT_lo", [P, KT, SEQ], F32R)
        z = sb("z", [P, NT, INW])
        wsT = sb("wsT", [P, NG, P])
        ws_raw = sb("ws_raw", [P, NG, P])
        aT = sb("aT", [P, 3 * P], offset=at[0] - NG * P * 4)
        subln = sb("subln", [P, DV])
        gstat = sb("gstat", [P, 4 * NG * NT])
        hstat = sb("hstat", [P, 2, 16])
        vgain = sb("vgain", [P, GW])
        lam_rows = sb("lam_rows", [P, 4, DEPTH, DH], offset=base + 2 * KT * SEQ * 4 + NT * INW * 4)
        slot_int = sb("slot_int", [P, P], I32, offset=base)
        bsT = sb("bsT", [P, NG])
        o = base
        qT = sb("qT", [P, NH, SEQ], offset=o); o += NH * SEQ * 4
        kT = sb("kT", [P, NH, SEQ], offset=o); o += NH * SEQ * 4
        prob = sb("prob", [P, 2, 2, 3 * P], offset=o); o += 2 * 2 * 3 * P * 4
        vsq = sb("vsq", [P, GW], offset=o); o += GW * 4
        assert o <= base + 2 * KT * SEQ * 4
        zbase = base + 2 * KT * SEQ * 4
        h_tok = sb("h_tok", [P, NT, D], offset=zbase)
        y_scaled = sb("y_scaled", [P, 2, CB], offset=zbase + NT * D * 4)
        o = zbase + NT * D * 4 + 2 * CB * 4
        f_silu = sb("f_silu", [P, NT, FB], offset=o); o += NT * FB * 4
        f_act = sb("f_act", [P, NT, FB], offset=o); o += NT * FB * 4
        fT_hi = sb("fT_hi", [P, NT, FB], F32R, offset=o); o += NT * FB * 4
        fT_lo = sb("fT_lo", [P, NT, FB], F32R, offset=o); o += NT * FB * 4
        o = base
        htok_hi = sb("htok_hi", [P, NT, D], F32R, offset=o); o += NT * D * 4
        htok_lo = sb("htok_lo", [P, NT, D], F32R, offset=o); o += NT * D * 4
        f_scaled = sb("f_scaled", [P, 2, CB], offset=base)
        y_hi = sb("y_hi", [P, D], F32R, offset=o)
        m_htok = sb("m_htok", [P, NT, D], offset=o)
        o += D * 4
        y_lo = sb("y_lo", [P, D], F32R, offset=o); o += D * 4
        m_acc = sb("m_acc", [P, NT, D], offset=o)
        r_hT = sb("r_hT", [P, KT, SEQ], offset=o)
        o += NT * D * 4
        hgT_hi = sb("hgT_hi", [P, KT, P], F32R, offset=o); o += KT * P * 4
        hgT_lo = sb("hgT_lo", [P, KT, P], F32R, offset=o); o += KT * P * 4
        m_silu = sb("m_silu", [P, FB], offset=o); o += FB * 4
        m_act = sb("m_act", [P, FB], offset=o); o += FB * 4
        mT_hi = sb("mT_hi", [P, FB], F32R, offset=o); o += FB * 4
        mT_lo = sb("mT_lo", [P, FB], F32R, offset=o); o += FB * 4
        pick = sb("pick", [P, NT, P], F32R, offset=o); o += NT * P * 4
        put = sb("put", [P, NT, P], F32R, offset=o); o += NT * P * 4
        gate_col = sb("gate_col", [P, NT], offset=o); o += 32
        slot_gate = sb("slot_gate", [P, 1], offset=o); o += 32
        slot_of = sb("slot_of", [P, NT, 2 * NE + 1], offset=o); o += 160
        gate_of = sb("gate_of", [P, NT, 2 * NE + 1], offset=o); o += 160
        logit = sb("logit", [P, NT, NE], offset=o); o += 64
        top = sb("top", [P, NT, 8], offset=o); o += 64
        top_i = sb("top_i", [P, NT, 8], U32, offset=o); o += 64
        top_f = sb("top_f", [P, NT, 8], offset=o); o += 64
        gap = sb("gap", [P, NT, 1], offset=o); o += 32
        e2 = sb("e2", [P, NT, 1], offset=o); o += 32
        w12 = sb("w12", [P, NT, 2], offset=o); o += 32
        wsum = sb("wsum", [P, NT, 1], offset=o); o += 32
        hit = sb("hit", [P, NT, 2, NE], offset=o); o += NT * 2 * NE * 4
        mask = sb("mask", [P, NT, NE], offset=o); o += 64
        most = sb("most", [P, 1], offset=o); o += 32
        rounds_f = sb("rounds_f", [P, 1], offset=o); o += 32
        rounds = sb("rounds", [P, 1], I32, offset=o); o += 32
        assert o <= nc.sbuf_usable_end, o

        bank = [ctx.enter_context(nc.psum_tensor(f"bank{i}", [P, 512], F32)) for i in range(8)]

        def sem(name):
            return ctx.enter_context(nc.semaphore(name))

        chunk_in = [sem(f"chunk_in{i}") for i in range(RING)]
        hi_done = sem("hi_done")
        split_done = sem("split_done")
        split_used = sem("split_used")
        sp_turn = sem("sp_turn")
        first_in = sem("first_in")
        x_in = sem("x_in")
        gain0_in = sem("gain0_in")
        gain_in = sem("gain_in")
        gain_used = sem("gain_used")
        rows_in = sem("rows_in")
        bias_in = sem("bias_in")
        bias_used = sem("bias_used")
        consts = sem("consts")
        pool_step = sem("pool_step")
        mixer_in = sem("mixer_in")
        lam_in = sem("lam_in")
        route_in = sem("route_in")
        c_mm = sem("c_mm")
        silu_c_done = sem("silu_c_done")
        ada_mm = sem("ada_mm")
        ada_out = sem("ada_out")
        ssq_done = sem("ssq_done")
        std_done = sem("std_done")
        h_done = sem("h_done")
        tr_mm = sem("tr_mm")
        tr_hi = sem("tr_hi")
        tr_lo = sem("tr_lo")
        z_out = sem("z_out")
        ws_mm = sem("ws_mm")
        ws_out = sem("ws_out")
        qk_mm = sem("qk_mm")
        qk_out_a = sem("qk_out_a")
        qk_out_v = sem("qk_out_v")
        vstat_done = sem("vstat_done")
        vstd_done = sem("vstd_done")
        vrstd_done = sem("vrstd_done")
        v_done = sem("v_done")
        vm_mm = sem("vm_mm")
        ua_done = sem("ua_done")
        v_step = sem("v_step")
        v_step2 = sem("v_step2")
        sc_mm = sem("sc_mm")
        negmax = sem("negmax")
        exp_done = sem("exp_done")
        a_done = sem("a_done")
        at_mm = sem("at_mm")
        at_out = sem("at_out")
        o_mm = sem("o_mm")
        o_out = sem("o_out")
        lam_step = sem("lam_step")
        lam_dots = sem("lam_dots")
        lam_exps = sem("lam_exps")
        osq_done = sem("osq_done")
        ostd_done = sem("ostd_done")
        ob_done = sem("ob_done")
        ys_done = sem("ys_done")
        x_step = sem("x_step")
        dve_step = sem("dve_step")
        act_step = sem("act_step")
        gu_mm = sem("gu_mm")
        silu_done = sem("silu_done")
        act_done = sem("act_done")
        fT_mm = sem("fT_mm")
        fT_hi_done = sem("fT_hi_done")
        fT_lo_done = sem("fT_lo_done")
        htok_split = sem("htok_split")
        r_mm = sem("r_mm")
        r_out = sem("r_out")
        logit_mm = sem("logit_mm")
        gap_done = sem("gap_done")
        gexp_done = sem("gexp_done")
        mask_done = sem("mask_done")
        count_mm = sem("count_mm")
        rounds_done = sem("rounds_done")
        pick_done = sem("pick_done")
        pick_mm = sem("pick_mm")
        put_done = sem("put_done")
        ga_mm = sem("ga_mm")
        ga_hi = sem("ga_hi")
        ga_lo = sem("ga_lo")
        m_sl = sem("m_sl")
        m_ac = sem("m_ac")
        m_tm = sem("m_tm")
        m_th = sem("m_th")
        m_tl = sem("m_tl")
        zero_mm = sem("zero_mm")
        m_yh = sem("m_yh")
        m_yl = sem("m_yl")
        m_sc = sem("m_sc")
        m_add = sem("m_add")
        out_ready = sem("out_ready")
        out_sent = sem("out_sent")

        def kview(ap):
            return ap.rearrange("(k p) n -> p k n", p=P)

        def chunk_source(c):
            kind, layer, j, half = c
            if kind == "ada":
                return kview(t["w_ada"][layer])[:, 4 * half:4 * half + 4, CB * j:CB * j + CB]
            if kind == "in":
                return kview(t["w_in"][layer])[:, 4 * half:4 * half + 4, CB * j:CB * j + CB]
            if kind == "out":
                return kview(t["w_out"][layer])[:, 4 * half:4 * half + 4, CB * j:CB * j + CB]
            if kind == "gate":
                return kview(t["ffn_w_gate"][0])[:, :, FB * j:FB * j + FB]
            if kind == "up":
                return kview(t["ffn_w_up"][0])[:, :, FB * j:FB * j + FB]
            return kview(t["ffn_w_down"][0])[:, 2 * j:2 * j + 2, :]

        def expert_source(e, kind, b):
            name = {"gate": "moe_w_gate", "up": "moe_w_up", "down": "moe_w_down"}[kind]
            v = t[name][0].rearrange("e (k p) n -> e p k n", p=P)
            if kind == "down":
                v = v[bass.ds(e, 1), :, 2 * b:2 * b + 2, :]
            else:
                v = v[bass.ds(e, 1), :, :, FB * b:FB * b + FB]
            return v.rearrange("a p k n -> (a p) k n")

        def ring_slot(n):
            s = n % RING
            return s

        def landed(n):
            return 16 * (n // RING + 1)

        def pair_slots(n):
            a, b = n % RING, (n + 1) % RING
            return min(a, b), max(a, b)

        def load_slot(kind, n):
            if kind == "gate":
                return pair_slots(n)[0]
            if kind == "up":
                return pair_slots(n - 1)[1]
            return n % RING

        def landed_in(slot, n):
            return 16 * (n // RING + 1)

        def slot_count(kind, n):
            slot = load_slot(kind, n)
            own = n if n % RING == slot else (n + 1 if kind == "gate" else n - 1)
            assert own % RING == slot
            return slot, 16 * (own // RING + 1)

        def taken(n, q):
            return 2 * n + q + 1

        def freed(n, kind):
            return taken(n + 1, 1) if kind == "gate" else taken(n, 1)

        def gu_raw(n, q):
            a, b = pair_slots(n)
            return raw[:, a:b + 1:b - a, 2 * q * FB:(2 * q + 2) * FB]

        def down_raw(n, c):
            return raw[:, n % RING, c * SUB:(c + 1) * SUB]

        blk = ctx.enter_context(nc.Block())

        @blk.sync
        def _(sp):
            sp.dma_start(c_rows[:, :], t["c"][0].rearrange("(k p) -> k p", p=P)).then_inc(first_in, 16)
            sp.wait_ge(pool_step, 1)
            sp.dma_start(b_rows[0:DEPTH * MOD_BLOCKS, :], t["b_ada"].rearrange("l (j n) -> (l j) n", n=CB))\
              .then_inc(rows_in, 16)
            sp.dma_start(gain[:, :], t["norm1_g"][0].partition_broadcast(P)).then_inc(gain0_in, 16)
            for n, c in enumerate(STREAM):
                if n >= RING:
                    ahead = n + 1 if c[0] == "gate" else n
                    sp.wait_ge(split_done, freed(ahead - RING, STREAM[ahead - RING][0]))
                slot, _ = slot_count(c[0], n)
                src = chunk_source(c)
                sp.dma_start(raw[:, slot, :].rearrange("p (k n) -> p k n", n=src.shape[2]), src)\
                  .then_inc(chunk_in[slot], 16)
                if n == 3:
                    sp.dma_start(x[:, :, :], t["x"][0].rearrange("(a p) d -> p a d", p=P)).then_inc(x_in, 16)

            def load_expert(e, turn):
                for j, (kind, b) in enumerate(EXPERT):
                    n = N0 + j
                    ahead = n + 1 if kind == "gate" else n
                    past = EXPERT[ahead - N0 - RING][0]
                    sp.wait_ge(split_done, turn * EXPERT_SPLITS + freed(ahead - RING, past))
                    sp.sem_inc(sp_turn, 1)
                    slot, _ = slot_count(kind, n)
                    src = expert_source(e, kind, b)
                    sp.dma_start(raw[:, slot, :].rearrange("p (k n) -> p k n", n=src.shape[2]), src)\
                      .then_inc(chunk_in[slot], 16)

            with sp.Fori(0, NE) as e:
                load_expert(e, e)
            sp.wait_ge(rounds_done, 1)
            n_turns = sp.value_load(rounds[0:1, 0:1], min_val=NE, max_val=2 * NE)
            with sp.If(n_turns > NE):
                with sp.Fori(0, NE) as e:
                    load_expert(e, e + NE)
            sp.wait_ge(out_ready, NT)
            sp.dma_start(out.rearrange("(a p) d -> p a d", p=P), h_tok[:, :, :]).then_inc(out_sent, 16)
            sp.wait_ge(out_sent, 16)

        @blk.gpsimd
        def _(pool):
            pool.memset(b_rows[:, :], 0.0).then_inc(pool_step, 1)
            pool.memset(ones[:, :], 1.0).then_inc(pool_step, 1)
            pool.memset(ident[:, :], 0.0).then_inc(pool_step, 1)
            pool.memset(future[:, :], 0.0).then_inc(pool_step, 1)
            pool.memset(eps_col[:, :], EPS).then_inc(pool_step, 1)
            pool.iota(slot_int[:, :], pattern=[[1, P]], base=0, channel_multiplier=0).then_inc(pool_step, 1)
            pool.wait_ge(pool_step, 6)
            pool.affine_select(out=ident[:, :], in_=ident[:, :], compare_op=ALU.not_equal, fill=1.0,
                               base=0, pattern=[[-1, P]], channel_multiplier=1).then_inc(consts, 1)
            pool.affine_select(out=before[:, :], in_=ones[:, :], compare_op=ALU.is_gt, fill=0.0,
                               base=0, pattern=[[1, P]], channel_multiplier=-1).then_inc(consts, 1)
            pool.affine_select(out=upto[:, :], in_=ones[:, :], compare_op=ALU.is_ge, fill=0.0,
                               base=0, pattern=[[1, P]], channel_multiplier=-1).then_inc(consts, 1)
            pool.affine_select(out=future[:, :], in_=future[:, :], compare_op=ALU.is_ge, fill=NEG,
                               base=0, pattern=[[-1, P]], channel_multiplier=1).then_inc(consts, 1)
            pool.tensor_copy(slot_no[:, :], slot_int[:, :]).then_inc(consts, 1)

            def broadcast(dst, row, signal):
                pool.dma_start(dst, row.partition_broadcast(P)).then_inc(signal, 16)

            gains = [t["norm1_g"][0], t["norm2_g"][0], t["norm1_g"][1], t["norm2_g"][1], t["final_g"]]

            def load_gain(i):
                pool.wait_ge(gain_used, 2 * i)
                broadcast(gain[:, :], gains[i], gain_in)

            def bias(first, last):
                for i in range(first, last):
                    layer, j = ADA[i]
                    row = MOD_BLOCKS * layer + j
                    if i:
                        pool.wait_ge(bias_used, i)
                    pool.tensor_scalar(ada_bias[:, :], b_rows[:, :], ident[:, row:row + 1], 0.0, ALU.mult, ALU.add)\
                        .then_inc(bias_in, 1)

            def load_mixer(layer):
                pool.dma_start(ws_raw[:, :, :], t["gmlp_ws"][layer].rearrange("g a b -> a g b")).then_inc(mixer_in, 16)
                pool.dma_start(bsT[:, :], t["gmlp_bs"][layer].rearrange("g a -> a g"), allow_slow_non_contiguous=True)\
                    .then_inc(mixer_in, 16)
                broadcast(subln[:, :], t["diff_subln_g"][layer], mixer_in)
                broadcast(vgain[:, :], t["gmlp_vnorm_g"][layer], mixer_in)

            def v_squares(layer):
                pool.wait_ge(z_out, NT * ((INW // CB) * layer + 2))
                for a in range(NT):
                    va = z[:, a, GW:2 * GW]
                    pool.tensor_tensor(z[:, a, 4 * CB:5 * CB], va, va, ALU.mult).then_inc(v_step, 1)

            def v_scaled(layer):
                pool.wait_ge(vrstd_done, layer + 1)
                pool.wait_ge(mixer_in, 64 * (layer + 1))
                for a in range(NT):
                    va = z[:, a, GW:2 * GW]
                    vg = va.rearrange("p (g n) -> p g n", g=NG)
                    pool.tensor_tensor(vg, vg, gstat[:, NG * a:NG * a + NG].unsqueeze(2).to_broadcast([P, NG, GD]),
                                       ALU.mult).then_inc(v_step2, 1)
                    pool.wait_ge(v_step2, NT * layer + a + 1)
                    pool.tensor_tensor(va, va, vgain[:, :], ALU.mult).then_inc(v_done, 1)

            def add_to_x(stage, order, src):
                for n, (a, half) in enumerate(order):
                    pool.wait_ge(ys_done, 4 * stage + n + 1)
                    xs = x[:, a, CB * half:CB * half + CB]
                    pool.tensor_tensor(xs, xs, src[:, n % 2, :], ALU.add).then_inc(x_step, 1)

            pool.wait_ge(consts, 1)
            pool.wait_ge(rows_in, 16)
            bias(0, 1)
            for i, name in enumerate(("lam_q1", "lam_k1", "lam_q2", "lam_k2")):
                broadcast(lam_rows[:, i, :, :], t[name].rearrange("l n -> (l n)"), lam_in)
            load_mixer(0)
            pool.dma_start(w_route[:, :, :], t["w_router"][0].rearrange("(k p) e -> p k e", p=P)).then_inc(route_in, 16)
            bias(1, 5)
            load_gain(1)
            bias(5, 8)
            v_squares(0)
            bias(8, 10)
            v_scaled(0)
            bias(10, 11)
            add_to_x(0, BY_HALF, y_scaled)
            load_gain(2)
            bias(11, 18)
            load_mixer(1)
            load_gain(3)
            bias(18, 19)
            add_to_x(1, BY_TILE, y_scaled)
            bias(19, 22)
            v_squares(1)
            bias(22, 24)
            v_scaled(1)
            add_to_x(2, BY_HALF, y_scaled)
            load_gain(4)
            pool.wait_ge(logit_mm, 1)
            pool.memset(m_acc[:, :, :], 0.0).then_inc(m_add, 1)
            add_to_x(3, BY_TILE, f_scaled)

        @blk.scalar
        def _(act):
            steps = [0]

            def then(ins):
                steps[0] += 1
                ins.then_inc(act_step, 1)
                act.wait_ge(act_step, steps[0])

            def split_hi(s, src, like, base=0):
                if not (isinstance(base, int) and s < NB):
                    act.wait_ge(split_used, base + (s - NB + 1))
                act.activation(like(w_hi[:, s % NB, :]), src, ACT.Copy).then_inc(hi_done, 1)

            def flat(ap):
                return ap

            def pairs(ap):
                return ap.rearrange("p (g n) -> p g n", g=2)

            def wait_chunk(kind, n, base=0):
                slot, count = slot_count(kind, n)
                act.wait_ge(chunk_in[slot], base + count)

            def std_of_rows(i, junk):
                for a in range(NT):
                    if i == 0:
                        act.wait_ge(x_in, 16)
                    else:
                        order = BY_HALF if i % 2 else BY_TILE
                        act.wait_ge(x_step, 4 * (i - 1) + max(order.index((a, 0)), order.index((a, 1))) + 1)
                    act.activation(junk[:, a, :], x[:, a, :], ACT.Square, accum_out=ssq[:, a:a + 1]).then_inc(ssq_done, 1)
                    act.wait_ge(ssq_done, NT * i + a + 1)
                    act.activation(std[:, a:a + 1], ssq[:, a:a + 1], ACT.Sqrt, bias=eps_col[:, 0:1],
                                   scale=1.0 / D).then_inc(std_done, 1)

            def transposed_hi(dst, i):
                for a in range(NT):
                    for half in range(2):
                        n = 4 * i + 2 * a + half
                        act.wait_ge(tr_mm, n + 1)
                        act.activation(dst[:, 4 * half:4 * half + 4, P * a:P * a + P],
                                       bank[2 * a + half][:, :].rearrange("p (k n) -> p k n", k=4),
                                       ACT.Copy).then_inc(tr_hi, 1)

            act.wait_ge(c_mm, 1)
            act.activation(silu_c[:, :], bank[6][:, 0:KT], ACT.Silu).then_inc(silu_c_done, 1)
            act.wait_ge(consts, 5)
            for layer in range(DEPTH):
                std_of_rows(2 * layer, h_tok)
                transposed_hi(hT_hi, 2 * layer if layer == 0 else 3)

                def z_block(j):
                    act.wait_ge(split_used, S_IN[layer] + 4 * (j + 1))
                    if j == INW // CB - 1:
                        act.wait_ge(vstat_done, NT * (layer + 1))
                    for a in range(NT):
                        act.activation(z[:, a, CB * j:CB * j + CB], bank[2 * (j % 2) + a][:, :],
                                       ACT.Gelu_apprx_tanh if j < 2 else ACT.Copy).then_inc(z_out, 1)

                for j in range(INW // CB):
                    for half in range(2):
                        n = WHERE[("in", layer, j, half)]
                        wait_chunk("in", n)
                        for q in range(2):
                            split_hi(S_IN[layer] + 4 * j + 2 * half + q,
                                     raw[:, n % RING, q * SUB:(q + 1) * SUB], flat)
                        if half == 0 and j:
                            z_block(j - 1)
                        if half == 0 and j == INW // CB - 1:
                            act.wait_ge(vstat_done, NT * (layer + 1))
                            act.activation(gstat[:, 16:32], gstat[:, 0:16], ACT.Sqrt, bias=eps_col[:, 0:1],
                                           scale=1.0 / GD).then_inc(vstd_done, 1)
                z_block(INW // CB - 1)

                for a in range(NT):
                    act.wait_ge(qk_mm, 4 * layer + a + 1)
                    act.activation(qT[:, :, P * a:P * a + P], bank[a][:, :].rearrange("p (h n) -> p h n", h=NH),
                                   ACT.Copy).then_inc(qk_out_a, 1)
                if layer == 0:
                    act.wait_ge(lam_dots, 1)
                    act.activation(lam_exp[:, :, :], lam_sum[:, :, :], ACT.Exp).then_inc(lam_exps, 1)

                def exponentials(h):
                    st = hstat[:, h % 2, :]
                    act.wait_ge(negmax, NH * layer + h + 1)
                    for m in range(2):
                        for a in range(NT):
                            cols = slice(0, P) if a == 0 else slice(P, 3 * P)
                            act.activation(prob[:, h % 2, m, cols], bank[2 * (h % 2) + m][:, cols], ACT.Exp,
                                           bias=st[:, 4 + 2 * m + a:5 + 2 * m + a], scale=DH ** -0.5,
                                           accum_out=st[:, 8 + 2 * m + a:9 + 2 * m + a]).then_inc(exp_done, 1)

                exponentials(0)
                for h in range(NH):
                    if h + 1 < NH:
                        exponentials(h + 1)
                    act.wait_ge(at_mm, NH * layer + h + 1)
                    act.activation(aT[:, :], bank[4 + h % 2][:, 0:3 * P], ACT.Copy).then_inc(at_out, 1)
                    act.wait_ge(o_mm, NH * layer + h + 1)
                    act.activation(z[:, :, 2 * GW + DV * h:2 * GW + DV * h + DV],
                                   bank[6][:, FB * (h % 2):FB * (h % 2) + FB].rearrange("p (a n) -> p a n", a=NT),
                                   ACT.Copy).then_inc(o_out, 1)
                    for a in range(NT):
                        c0 = FB * (h % 2) + DV * a
                        act.activation(vsq[:, DV * a:DV * a + DV], bank[6][:, c0:c0 + DV], ACT.Square,
                                       accum_out=gstat[:, 32 + NH * a + h:33 + NH * a + h]).then_inc(osq_done, 1)
                act.wait_ge(osq_done, NT * NH * (layer + 1))
                act.activation(gstat[:, 40:48], gstat[:, 32:40], ACT.Sqrt, bias=eps_col[:, 0:1],
                               scale=1.0 / DV).then_inc(ostd_done, 1)
                transposed_hi(hT_hi, 1 if layer == 0 else 4)

                for j in range(D // CB):
                    for half in range(2):
                        n = WHERE[("out", layer, j, half)]
                        wait_chunk("out", n)
                        for q in range(2):
                            split_hi(S_OUT[layer] + 4 * j + 2 * half + q,
                                     raw[:, n % RING, q * SUB:(q + 1) * SUB], flat)

                std_of_rows(2 * layer + 1, h_tok if layer == 0 else m_htok)
                if layer == 0:
                    transposed_hi(hT_hi, 2)
                    for b in range(NBLK + 1):
                        if b < NBLK:
                            n = WHERE[("gate", 0, b, 0)]
                            wait_chunk("gate", n)
                            wait_chunk("up", n + 1)
                            for q in range(4):
                                split_hi(S_FFN + split_in_block(b, q), gu_raw(n, q), pairs)
                        if b:
                            act.wait_ge(fT_mm, b)
                            act.activation(fT_hi[:, :, :], bank[6][:, :].rearrange("p (a n) -> p a n", a=NT),
                                           ACT.Copy).then_inc(fT_hi_done, 1)
                            n = WHERE[("down", 0, b - 1, 0)]
                            wait_chunk("down", n)
                            for c in range(2):
                                split_hi(S_FFN + down_split(b - 1, c), down_raw(n, c), flat)
                        if b < NBLK:
                            for a in range(NT):
                                if a == 0:
                                    act.wait_ge(gu_mm, b + 1)
                                else:
                                    act.wait_ge(split_used, S_FFN + split_in_block(b, 3) + 1)
                                act.activation(f_silu[:, a, :], bank[4 + a][:, 0:FB], ACT.Silu).then_inc(silu_done, 1)

            for a in range(NT):
                for half in range(2):
                    act.wait_ge(r_mm, 2 * a + half + 1)
                    act.activation(r_hT[:, 4 * half:4 * half + 4, P * a:P * a + P],
                                   bank[2 * a + half][:, :].rearrange("p (k n) -> p k n", k=4),
                                   ACT.Copy).then_inc(r_out, 1)
                act.activation(htok_hi[:, a, :], m_htok[:, a, :], ACT.Copy).then_inc(htok_split, 1)
            act.wait_ge(gap_done, 1)
            act.activation(e2[:, :, :], gap[:, :, :], ACT.Exp).then_inc(gexp_done, 1)

            def gathered_hi(base):
                for half in range(2):
                    act.wait_ge(ga_mm, base * 4 + half + 1)
                    act.activation(hgT_hi[:, 4 * half:4 * half + 4, :],
                                   bank[2 + half][:, :].rearrange("p (k n) -> p k n", k=4),
                                   ACT.Copy).then_inc(ga_hi, 1)

            def expert_out_hi(turn):
                act.wait_ge(put_done, turn * 2 + 2)
                act.wait_ge(zero_mm, 1)
                act.wait_ge(split_used, turn * EXPERT_SPLITS + S_MOE)
                for half in range(2):
                    act.activation(y_hi[:, CB * half:CB * half + CB], bank[half][:, :], ACT.Copy,
                                   scale=slot_gate[:, 0:1]).then_inc(m_yh, 1)

            gathered_hi(0)
            act.wait_ge(m_add, 1)
            act.activation(put[:, :, :], m_acc[:, 0, 0:NT * P].rearrange("p (a n) -> p a n", a=NT), ACT.Copy)\
               .then_inc(put_done, 1)
            act.activation(slot_gate[:, :], eps_col[:, :], ACT.Copy).then_inc(put_done, 1)
            act.activation(e2[:, 0, :], eps_col[:, :], ACT.Silu).then_inc(act_step, 1)
            act.wait_ge(rounds_done, 1)
            n_turns = act.value_load(rounds[0:1, 0:1], min_val=NE, max_val=2 * NE)
            with act.Fori(0, n_turns) as i:
                ring = i * (16 * EXPERT_CHUNKS // RING)
                splits = i * EXPERT_SPLITS
                blocks = i * NBLK

                def silu_of(b):
                    act.wait_ge(split_used, splits + (S_MOE + split_in_block(b, 3) + 1))
                    act.activation(m_silu[:, :], bank[4 + b % 2][:, 0:FB], ACT.Silu).then_inc(m_sl, 1)

                def hidden_hi(b):
                    act.wait_ge(m_tm, blocks + (b + 1))
                    act.activation(mT_hi[:, :], bank[6][:, FB * (b % 2):FB * (b % 2) + FB], ACT.Copy).then_inc(m_th, 1)

                def down_hi(b):
                    n = N0 + EWHERE[("down", b)]
                    wait_chunk("down", n, ring)
                    for c in range(2):
                        split_hi(S_MOE + down_split(b, c), down_raw(n, c), flat, splits)

                for b in range(NBLK):
                    n = N0 + EWHERE[("gate", b)]
                    wait_chunk("gate", n, ring)
                    wait_chunk("up", n + 1, ring)
                    for q in range(4):
                        split_hi(S_MOE + split_in_block(b, q), gu_raw(n, q), pairs, splits)
                        if b and q == SILU_AFTER[b]:
                            silu_of(b - 1)
                        if b == 0 and q == 2:
                            expert_out_hi(i)
                    if b:
                        hidden_hi(b - 1)
                    if b == 2:
                        act.wait_ge(m_sc, i * 2 + 2)
                        act.wait_ge(pick_mm, i + 1)
                        act.activation(put[:, :, :], bank[7][:, 0:2 * P].rearrange("p (a n) -> p a n", a=NT),
                                       ACT.Copy).then_inc(put_done, 1)
                        act.activation(slot_gate[:, :], bank[7][:, 2 * P:2 * P + 1], ACT.Copy).then_inc(put_done, 1)
                    if b:
                        down_hi(b - 1)
                silu_of(NBLK - 1)
                down_hi(NBLK - 1)
                hidden_hi(NBLK - 1)
                gathered_hi(i + 1)
            expert_out_hi(n_turns)
            std_of_rows(2 * DEPTH, h_tok)

        @blk.vector
        def _(dve):
            steps = [0]

            def then(ins):
                steps[0] += 1
                ins.then_inc(dve_step, 1)
                dve.wait_ge(dve_step, steps[0])

            def split_lo(s, count, src, like, splits=0):
                dve.wait_ge(hi_done, splits + (s + 1))
                dve.tensor_tensor(like(w_lo[:, s % NB, :]), src, like(w_hi[:, s % NB, :].bitcast(F32)),
                                  ALU.subtract).then_inc(split_done, 1)

            def flat(ap):
                return ap

            def pairs(ap):
                return ap.rearrange("p (g n) -> p g n", g=2)

            ada_no = [0]
            ada_evac = [0]

            def ada_out_block():
                i = ada_evac[0]
                ada_evac[0] += 1
                layer, j = ADA[i]
                piece, half = divmod(j, 2)
                dst = mod[:, piece, CB * half:CB * half + CB]
                dve.wait_ge(ada_mm, i + 1)
                if piece in (SC1, SC2):
                    if half == 0:
                        norm_no = 2 * layer + (piece == SC2)
                        if norm_no == 0:
                            dve.wait_ge(gain0_in, 16)
                        else:
                            dve.wait_ge(gain_in, 16 * norm_no)
                    dve.scalar_tensor_tensor(out=dst, in0=bank[7][:, :], scalar=1.0,
                                             in1=gain[:, CB * half:CB * half + CB], op0=ALU.add,
                                             op1=ALU.mult).then_inc(ada_out, 1)
                    dve.wait_ge(ada_out, i + 1)
                    dve.sem_inc(gain_used, 1)
                else:
                    dve.tensor_copy(dst, bank[7][:, :]).then_inc(ada_out, 1)

            def ada_half(half):
                i = ada_no[0]
                layer, j = ADA[i]
                acc = ada_acc[:, i % 2, :]
                if half == 0:
                    if i >= 2:
                        dve.wait_ge(ada_mm, i - 1)
                    dve.wait_ge(bias_in, i + 1)
                n = WHERE[("ada", layer, j, half)]
                dve.wait_ge(chunk_in[n % RING], landed(n))
                for q in range(4):
                    k = 4 * half + q
                    ins = dve.scalar_tensor_tensor(
                        out=acc, in0=raw[:, n % RING, CB * q:CB * q + CB], scalar=silu_c[:, k:k + 1],
                        in1=ada_bias[:, :] if k == 0 else acc, op0=ALU.mult, op1=ALU.add)
                    if k == 0:
                        ins.then_inc(bias_used, 1)
                        dve.wait_ge(bias_used, i + 1)
                    elif q < 3:
                        then(ins)
                    else:
                        ins.then_inc(split_done, 2)
                        dve.wait_ge(split_done, taken(n, 1))
                if half == 1:
                    ada_no[0] += 1
                    if ada_evac[0] < i:
                        ada_out_block()

            def ada_block():
                ada_half(0)
                ada_half(1)

            def ada_flush():
                while ada_evac[0] < ada_no[0]:
                    ada_out_block()

            def norm(i, a_piece, b_piece, dst):
                for a in range(NT):
                    dve.wait_ge(std_done, NT * i + a + 1)
                    then(dve.reciprocal(rstd[:, a:a + 1], std[:, a:a + 1]))
                    if b_piece is None:
                        dve.scalar_tensor_tensor(out=dst[:, a, :], in0=x[:, a, :], scalar=rstd[:, a:a + 1],
                                                 in1=gain[:, :], op0=ALU.mult, op1=ALU.mult).then_inc(out_ready, 1)
                        continue
                    then(dve.scalar_tensor_tensor(out=dst[:, a, :], in0=x[:, a, :], scalar=rstd[:, a:a + 1],
                                                  in1=mod[:, a_piece, :], op0=ALU.mult, op1=ALU.mult))
                    dve.tensor_tensor(dst[:, a, :], dst[:, a, :], mod[:, b_piece, :], ALU.add).then_inc(h_done, 1)

            def transposed_lo(hi, lo, i):
                for a in range(NT):
                    for half in range(2):
                        n = 4 * i + 2 * a + half
                        dve.wait_ge(tr_hi, n + 1)
                        dve.tensor_tensor(lo[:, 4 * half:4 * half + 4, P * a:P * a + P],
                                          bank[2 * a + half][:, :].rearrange("p (k n) -> p k n", k=4),
                                          hi[:, 4 * half:4 * half + 4, P * a:P * a + P].bitcast(F32),
                                          ALU.subtract).then_inc(tr_lo, 1)

            def scale_updates(stage, order, src, piece, ready, dst):
                for n, (a, half) in enumerate(order):
                    ready(a, half)
                    if 4 * stage + n >= 2:
                        dve.wait_ge(x_step, 4 * stage + n - 1)
                    dve.tensor_tensor(dst[:, n % 2, :], src(a, half), mod[:, piece, CB * half:CB * half + CB],
                                      ALU.mult).then_inc(ys_done, 1)

            dve.wait_ge(silu_c_done, 1)
            dve.wait_ge(pool_step, 6)
            for _ in range(4):
                ada_block()
            ada_flush()
            dve.wait_ge(consts, 5)
            for layer in range(DEPTH):
                dve.wait_ge(ada_out, ada_evac[0])
                norm(2 * layer, SC1, SH1, h_tok)
                transposed_lo(hT_hi, hT_lo, 2 * layer if layer == 0 else 3)
                for j in range(INW // CB):
                    for half in range(2):
                        n = WHERE[("in", layer, j, half)]
                        for q in range(2):
                            split_lo(S_IN[layer] + 4 * j + 2 * half + q, taken(n, q),
                                     raw[:, n % RING, q * SUB:(q + 1) * SUB], flat)
                        ada_half(half)
                        if (j, half) == (0, 1) and layer == 0:
                            dve.wait_ge(lam_in, 64)
                            for i in range(2):
                                then(dve.tensor_tensor(lam_rows[:, 2 * i, :, :], lam_rows[:, 2 * i, :, :],
                                                       lam_rows[:, 2 * i + 1, :, :], ALU.mult))
                                dve.tensor_reduce(lam_sum[:, i, :], lam_rows[:, 2 * i, :, :], axis=AX.X, op=ALU.add)\
                                   .then_inc(lam_step, 1)
                            dve.wait_ge(lam_step, 2)
                            dve.sem_inc(lam_dots, 1)
                        if (j, half) == (1, 1):
                            for g in range(2):
                                dve.wait_ge(ws_mm, 2 * layer + g + 1)
                                dve.tensor_tensor(wsT[:, 4 * g:4 * g + 4, :],
                                                  bank[4 + g][:, :].rearrange("p (g n) -> p g n", g=4),
                                                  upto[:, :].unsqueeze(1).to_broadcast([P, 4, P]), ALU.mult).then_inc(ws_out, 1)
                            dve.wait_ge(mixer_in, 64 * (layer + 1))
                            lam_init = 0.8 - 0.6 * math.exp(-0.3 * layer)
                            then(dve.tensor_scalar(subln[:, :], subln[:, :], 1.0 - lam_init, None, ALU.mult))
                        if (j, half) == (3, 1):
                            for a in range(NT):
                                dve.wait_ge(v_step, NT * layer + a + 1)
                                dve.tensor_reduce(gstat[:, NG * a:NG * a + NG],
                                                  z[:, a, 4 * CB:5 * CB].rearrange("p (g n) -> p g n", g=NG),
                                                  axis=AX.X, op=ALU.add).then_inc(vstat_done, 1)
                        if (j, half) == (INW // CB - 1, 0):
                            dve.wait_ge(vstd_done, layer + 1)
                            dve.reciprocal(gstat[:, 0:16], gstat[:, 16:32]).then_inc(vrstd_done, 1)
                ada_flush()
                for a in range(NT):
                    dve.wait_ge(qk_mm, 4 * layer + NT + a + 1)
                    dve.tensor_copy(kT[:, :, P * a:P * a + P],
                                    bank[2 + a][:, :].rearrange("p (h n) -> p h n", h=NH)).then_inc(qk_out_v, 1)

                def head_max(h):
                    st = hstat[:, h % 2, :]
                    dve.wait_ge(sc_mm, NH * layer + h + 1)
                    for m in range(2):
                        for a in range(NT):
                            cols = slice(0, P) if a == 0 else slice(P, 3 * P)
                            ins = dve.reduce_max(st[:, 2 * m + a:2 * m + a + 1], bank[2 * (h % 2) + m][:, cols], AX.X)
                            if m + a == 2:
                                then(ins)
                    dve.tensor_scalar(st[:, 4:8], st[:, 0:4], -DH ** -0.5, None, ALU.mult).then_inc(negmax, 1)

                def head_maps(h):
                    st = hstat[:, h % 2, :]
                    p1, p2 = prob[:, h % 2, 0, :], prob[:, h % 2, 1, :]
                    dve.wait_ge(exp_done, 4 * (NH * layer + h + 1))
                    then(dve.reciprocal(st[:, 12:16], st[:, 8:12]))
                    then(dve.tensor_tensor(st[:, 14:16], st[:, 14:16], lam[:, layer:layer + 1].to_broadcast([P, 2]), ALU.mult))
                    parts = [slice(0, P), slice(P, 3 * P)]
                    for a in range(NT):
                        ins = dve.tensor_scalar(p2[:, parts[a]], p2[:, parts[a]], st[:, 14 + a:15 + a], None, ALU.mult)
                        if a:
                            then(ins)
                    for a in range(NT):
                        ins = dve.scalar_tensor_tensor(out=p1[:, parts[a]], in0=p1[:, parts[a]],
                                                       scalar=st[:, 12 + a:13 + a], in1=p2[:, parts[a]],
                                                       op0=ALU.mult, op1=ALU.subtract)
                    ins.then_inc(a_done, 1)

                if layer == 0:
                    dve.wait_ge(lam_exps, 1)
                    then(dve.tensor_tensor(lam[:, :], lam_exp[:, 0, :], lam_exp[:, 1, :], ALU.subtract))
                    for i in range(DEPTH):
                        then(dve.tensor_scalar(lam[:, i:i + 1], lam[:, i:i + 1], 0.8 - 0.6 * math.exp(-0.3 * i), None, ALU.add))
                head_max(0)
                head_max(1)
                for half in range(2):
                    dve.wait_ge(vm_mm, 2 * layer + half + 1)
                    for g in range(4):
                        gg = 4 * half + g
                        ug = z[:, :, GD * gg:GD * gg + GD]
                        dve.scalar_tensor_tensor(out=ug, in0=bank[4 + half][:, 2 * GD * g:2 * GD * g + 2 * GD].rearrange("p (a n) -> p a n", a=NT),
                                                 scalar=bsT[:, gg:gg + 1], in1=ug, op0=ALU.add, op1=ALU.mult).then_inc(ua_done, 1)
                for h in range(NH):
                    head_maps(h)
                    if h + 2 < NH:
                        head_max(h + 2)
                dve.wait_ge(ostd_done, layer + 1)
                then(dve.reciprocal(gstat[:, 48:56], gstat[:, 40:48]))
                for a in range(NT):
                    for h in range(NH):
                        oh = z[:, a, 2 * GW + DV * h:2 * GW + DV * h + DV]
                        dve.scalar_tensor_tensor(out=oh, in0=oh, scalar=gstat[:, 48 + NH * a + h:49 + NH * a + h],
                                                 in1=subln[:, :], op0=ALU.mult, op1=ALU.mult).then_inc(ob_done, 1)
                transposed_lo(hT_hi, hT_lo, 1 if layer == 0 else 4)
                for j in range(D // CB):
                    for half in range(2):
                        n = WHERE[("out", layer, j, half)]
                        for q in range(2):
                            split_lo(S_OUT[layer] + 4 * j + 2 * half + q, taken(n, q),
                                     raw[:, n % RING, q * SUB:(q + 1) * SUB], flat)
                    if j == 0:
                        ada_block()
                ada_flush()
                dve.wait_ge(ada_out, ada_evac[0])
                scale_updates(2 * layer, BY_HALF, lambda a, half: bank[2 * half + a][:, :], G1,
                              lambda a, half: dve.wait_ge(split_used, S_OUT[layer] + 4 * (half + 1)), y_scaled)
                if layer == 0:
                    norm(1, SC2, SH2, h_tok)
                    transposed_lo(hT_hi, hT_lo, 2)
                    for b in range(NBLK + 1):
                        if b < NBLK:
                            n = WHERE[("gate", 0, b, 0)]
                            for q in range(4):
                                split_lo(S_FFN + split_in_block(b, q), taken(n, q), gu_raw(n, q), pairs)
                        if BESIDE_FFN[b]:
                            ada_half(0)
                        if b:
                            dve.wait_ge(fT_hi_done, b)
                            dve.tensor_tensor(fT_lo[:, :, :], bank[6][:, :].rearrange("p (a n) -> p a n", a=NT),
                                              fT_hi[:, :, :].bitcast(F32), ALU.subtract).then_inc(fT_lo_done, 1)
                            n = WHERE[("down", 0, b - 1, 0)]
                            for c in range(2):
                                split_lo(S_FFN + down_split(b - 1, c), taken(n, c), down_raw(n, c), flat)
                        if b < NBLK:
                            for a in range(NT):
                                dve.wait_ge(silu_done, NT * b + a + 1)
                                dve.tensor_tensor(f_act[:, a, :], f_silu[:, a, :], bank[4 + a][:, FB:2 * FB],
                                                  ALU.mult).then_inc(act_done, 1)
                        if BESIDE_FFN[b]:
                            ada_half(1)
                        elif ada_evac[0] < ada_no[0]:
                            ada_flush()
                    dve.wait_ge(ada_out, ada_evac[0])
                    scale_updates(1, BY_TILE, lambda a, half: bank[2 * a + half][:, :], G2,
                                  lambda a, half: dve.wait_ge(split_used, S_FFN + EXPERT_SPLITS), y_scaled)
                else:
                    norm(3, SC2, SH2, m_htok)

            for a in range(NT):
                dve.wait_ge(htok_split, a + 1)
                then(dve.tensor_tensor(htok_lo[:, a, :], m_htok[:, a, :], htok_hi[:, a, :].bitcast(F32), ALU.subtract))
            dve.wait_ge(logit_mm, 1)
            then(dve.tensor_copy(logit[:, :, :], bank[4][:, 0:NT * NE].rearrange("p (a e) -> p a e", a=NT)))
            for a in range(NT):
                then(dve.max(top[:, a, :], logit[:, a, :]))
                then(dve.max_index(top_i[:, a, :], top[:, a, :], logit[:, a, :]))
            dve.tensor_tensor(gap[:, :, :], top[:, :, 1:2], top[:, :, 0:1], ALU.subtract).then_inc(gap_done, 1)
            then(dve.tensor_copy(top_f[:, :, :], top_i[:, :, :]))
            then(dve.tensor_tensor(hit[:, :, :, :], slot_no[:, 0:NE].unsqueeze(1).unsqueeze(1).to_broadcast([P, NT, 2, NE]),
                                   top_f[:, :, 0:2].unsqueeze(3).to_broadcast([P, NT, 2, NE]), ALU.is_equal))
            dve.tensor_tensor(mask[:, :, :], hit[:, :, 0, :], hit[:, :, 1, :], ALU.add).then_inc(mask_done, 1)
            dve.wait_ge(gexp_done, 1)
            then(dve.tensor_scalar(wsum[:, :, :], e2[:, :, :], 1.0, None, ALU.add))
            then(dve.reciprocal(w12[:, :, 0:1], wsum[:, :, :]))
            then(dve.tensor_tensor(w12[:, :, 1:2], e2[:, :, :], w12[:, :, 0:1], ALU.mult))
            dve.wait_ge(mask_done, 1)
            then(dve.tensor_tensor(hit[:, :, :, :], hit[:, :, :, :], w12[:, :, :].unsqueeze(3).to_broadcast([P, NT, 2, NE]), ALU.mult))
            then(dve.memset(gate_of[:, :, 2 * NE:2 * NE + 1], 0.0))
            for again in range(2):
                then(dve.tensor_tensor(gate_of[:, :, NE * again:NE * again + NE], hit[:, :, 0, :], hit[:, :, 1, :], ALU.add))
            then(dve.memset(slot_of[:, :, 2 * NE:2 * NE + 1], -1.0))
            dve.wait_ge(count_mm, 1)
            then(dve.scalar_tensor_tensor(out=slot_of[:, :, 0:NE],
                                          in0=bank[4][:, 32:32 + NT * NE].rearrange("p (a e) -> p a e", a=NT),
                                          scalar=1.0, in1=mask[:, :, :], op0=ALU.add, op1=ALU.mult))
            then(dve.tensor_scalar(slot_of[:, :, NE:2 * NE], slot_of[:, :, 0:NE], -1.0 - P, None, ALU.add))
            then(dve.tensor_scalar(slot_of[:, :, 0:NE], slot_of[:, :, 0:NE], -1.0, None, ALU.add))

            def make_pick(i, count):
                for a in range(NT):
                    dve.tensor_scalar(pick[:, a, :], slot_no[:, :], slot_of[:, a, i], None, ALU.is_equal)\
                       .then_inc(pick_done, 1)
                    dve.tensor_copy(gate_col[:, a:a + 1], gate_of[:, a, i]).then_inc(pick_done, 1)

            def gathered_lo(base):
                for half in range(2):
                    dve.wait_ge(ga_mm, base * 4 + (2 + half + 1))
                    dve.tensor_copy(hgT_lo[:, 4 * half:4 * half + 4, :],
                                    bank[(5, 7)[half]][:, :].rearrange("p (k n) -> p k n", k=4)).then_inc(ga_lo, 1)

            def expert_out_lo(turn):
                for half in range(2):
                    dve.wait_ge(m_yh, turn * 2 + (half + 1))
                    dve.scalar_tensor_tensor(out=y_lo[:, CB * half:CB * half + CB], in0=bank[half][:, :],
                                             scalar=slot_gate[:, 0:1], in1=y_hi[:, CB * half:CB * half + CB].bitcast(F32),
                                             op0=ALU.mult, op1=ALU.subtract).then_inc(m_yl, 1)

            def expert_add(turn):
                dve.wait_ge(m_add, turn * 4 + 1)
                for half in range(2):
                    dve.wait_ge(m_sc, turn * 2 + (half + 1))
                    for a in range(NT):
                        acc = m_acc[:, a, CB * half:CB * half + CB]
                        dve.tensor_tensor(acc, acc, bank[((2, 3), (5, 7))[half][a]][:, :], ALU.add).then_inc(m_add, 1)

            make_pick(slice(0, 1), 0)
            then(dve.reduce_max(most[:, :], bank[4][:, 64:64 + NE], AX.X))
            then(dve.tensor_scalar(rounds_f[:, :], most[:, :], float(P), float(NE), ALU.is_gt, ALU.mult))
            then(dve.tensor_scalar(rounds_f[:, :], rounds_f[:, :], float(NE), None, ALU.add))
            dve.tensor_copy(rounds[:, :], rounds_f[:, :]).then_inc(rounds_done, 1)
            gathered_lo(0)
            dve.wait_ge(rounds_done, 1)
            n_turns = dve.value_load(rounds[0:1, 0:1], min_val=NE, max_val=2 * NE)
            with dve.Fori(0, n_turns) as i:
                splits = i * EXPERT_SPLITS
                blocks = i * NBLK

                def gated(b):
                    dve.wait_ge(m_sl, blocks + (b + 1))
                    dve.tensor_tensor(m_act[:, :], m_silu[:, :], bank[4 + b % 2][:, FB:2 * FB], ALU.mult)\
                       .then_inc(m_ac, 1)

                def hidden_lo(b):
                    dve.wait_ge(m_th, blocks + (b + 1))
                    dve.tensor_tensor(mT_lo[:, :], bank[6][:, FB * (b % 2):FB * (b % 2) + FB],
                                      mT_hi[:, :].bitcast(F32), ALU.subtract).then_inc(m_tl, 1)

                def down_lo(b):
                    n = N0 + EWHERE[("down", b)]
                    for c in range(2):
                        split_lo(S_MOE + down_split(b, c), taken(n, c), down_raw(n, c), flat, splits)

                for b in range(NBLK):
                    n = N0 + EWHERE[("gate", b)]
                    for q in range(4):
                        split_lo(S_MOE + split_in_block(b, q), taken(n, q), gu_raw(n, q), pairs, splits)
                        if b and q == SILU_AFTER[b]:
                            gated(b - 1)
                        if b == 0 and q == 2:
                            expert_out_lo(i)
                    if b == 0:
                        expert_add(i)
                    else:
                        hidden_lo(b - 1)
                        down_lo(b - 1)
                    if b == 5:
                        dve.wait_ge(pick_mm, i + 1)
                        make_pick(bass.ds(i + 1, 1), 0)
                gated(NBLK - 1)
                down_lo(NBLK - 1)
                hidden_lo(NBLK - 1)
                gathered_lo(i + 1)
            expert_out_lo(n_turns)
            expert_add(n_turns)
            dve.wait_ge(m_add, n_turns * 4 + 5)
            scale_updates(3, BY_TILE, lambda a, half: m_acc[:, a, CB * half:CB * half + CB], G2,
                          lambda a, half: None, f_scaled)
            dve.wait_ge(gain_in, 16 * 4)
            norm(4, None, None, h_tok)

        @blk.tensor
        def _(pe):
            def three(dst, a_hi, a_lo, b_hi, b_lo, first, last):
                pe.matmul(dst, a_hi, b_hi, start=first, stop=False)
                pe.matmul(dst, a_lo, b_hi, start=False, stop=False)
                return pe.matmul(dst, a_hi, b_lo, start=False, stop=last)

            ada_no = [0]

            def ada_sum():
                i = ada_no[0]
                ada_no[0] += 1
                layer, j = ADA[i]
                pe.wait_ge(split_done, taken(WHERE[("ada", layer, j, 1)], 1))
                if i:
                    pe.wait_ge(ada_out, i)
                pe.matmul(bank[7][:, :], ones[:, :], ada_acc[:, i % 2, :], start=True, stop=True).then_inc(ada_mm, 1)

            def transposes(i, src, ready):
                for a in range(NT):
                    ready(a)
                    for half in range(2):
                        for k in range(4):
                            last = pe.transpose(bank[2 * a + half][:, P * k:P * k + P], src(a, 4 * half + k), ident[:, :])
                        last.then_inc(tr_mm, 1)

            def project(kind, layer, s0, blocks, evacuated):
                for j in range(blocks):
                    for sub in range(4):
                        if kind == "in" and sub == 2 and j:
                            ada_sum()
                        if kind == "in" and sub == 2 and j == 0:
                            pe.wait_ge(mixer_in, 64 * (layer + 1))
                            for half in range(2):
                                for g in range(4):
                                    last = pe.transpose(bank[4 + half][:, P * g:P * g + P], ws_raw[:, 4 * half + g, :], ident[:, :])
                                last.then_inc(ws_mm, 1)
                        s = s0 + 4 * j + sub
                        pe.wait_ge(split_done, taken(WHERE[(kind, layer, j, sub // 2)], sub % 2))
                        if sub == 0:
                            evacuated(j)
                        for a in range(NT):
                            for kk in range(2):
                                k = 2 * sub + kk
                                cols = slice(CB * kk, CB * kk + CB)
                                last = three(bank[2 * (j % 2) + a][:, :], hT_hi[:, k, P * a:P * a + P],
                                             hT_lo[:, k, P * a:P * a + P], w_hi[:, s % NB, cols], w_lo[:, s % NB, cols],
                                             k == 0, k == KT - 1)
                        last.then_inc(split_used, 1)

            pe.wait_ge(consts, 5)
            pe.wait_ge(first_in, 16)
            pe.transpose(bank[6][:, 0:KT], c_rows[:, :], ident[0:KT, 0:KT]).then_inc(c_mm, 1)
            for _ in range(4):
                ada_sum()
            for layer in range(DEPTH):
                transposes(2 * layer if layer == 0 else 3, lambda a, k: h_tok[:, a, P * k:P * k + P],
                           lambda a: pe.wait_ge(h_done, 2 * NT * layer + a + 1))
                seen = 4 * ((2 * layer if layer == 0 else 3) + 1)
                pe.wait_ge(tr_lo, seen)

                def z_free(j):
                    if j >= 2:
                        pe.wait_ge(z_out, NT * ((INW // CB) * layer + j - 1))

                project("in", layer, S_IN[layer], INW // CB, z_free)
                ada_sum()
                pe.wait_ge(z_out, NT * (INW // CB) * (layer + 1))
                for part in range(2):
                    for a in range(NT):
                        for h in range(NH):
                            c0 = 2 * GW + NH * DV * part + DV * h
                            last = pe.transpose(bank[2 * part + a][:, P * h:P * h + P], z[:, a, c0:c0 + DV], ident[:, :])
                        last.then_inc(qk_mm, 1)

                def scores(h):
                    for a in range(NT):
                        for m in range(2):
                            dst = bank[2 * (h % 2) + m]
                            cols = slice(0, P) if a == 0 else slice(P, 3 * P)
                            rows = slice(DH * m, DH * m + DH)
                            pe.matmul(dst[:, cols], qT[rows, h, P * a:P * a + P], kT[rows, h, 0:P * (a + 1)],
                                      start=(a == 0), stop=False, skip_group_check=True)
                    for a in range(NT):
                        for m in range(2):
                            cols = slice(P * 2 * a, P * 2 * a + P)
                            last = pe.matmul(bank[2 * (h % 2) + m][:, cols], ident[:, :], future[:, :],
                                             start=False, stop=True, skip_group_check=True)
                    last.then_inc(sc_mm, 1)

                pe.wait_ge(qk_out_a, NT * (layer + 1))
                pe.wait_ge(qk_out_v, NT * (layer + 1))
                scores(0)
                scores(1)
                pe.wait_ge(ws_out, 2 * (layer + 1))
                pe.wait_ge(v_done, NT * (layer + 1))
                for half in range(2):
                    for g in range(4):
                        gg = 4 * half + g
                        last = pe.matmul(bank[4 + half][:, 2 * GD * g:2 * GD * g + 2 * GD].rearrange("p (a n) -> p a n", a=NT),
                                         wsT[:, gg, :], z[:, :, GW + GD * gg:GW + GD * gg + GD], start=True, stop=True)
                    last.then_inc(vm_mm, 1)
                for h in range(NH):
                    pe.wait_ge(a_done, NH * layer + h + 1)
                    if h < 2:
                        pe.wait_ge(ua_done, 8 * layer + 4 * (h + 1))
                    for i in range(3):
                        last = pe.transpose(bank[4 + h % 2][:, P * i:P * i + P], prob[:, h % 2, 0, P * i:P * i + P], ident[:, :])
                    last.then_inc(at_mm, 1)
                    if h + 2 < NH:
                        scores(h + 2)
                    pe.wait_ge(at_out, NH * layer + h + 1)
                    if h:
                        pe.wait_ge(osq_done, NT * (NH * layer + h))
                    v0 = 2 * GW + 2 * NH * DV + DV * h
                    dst = FB * (h % 2)
                    pe.matmul(bank[6][:, dst:dst + DV], aT[:, 0:P], z[:, 0, v0:v0 + DV], start=True, stop=True)
                    pe.matmul(bank[6][:, dst + DV:dst + 2 * DV], aT[:, P:2 * P], z[:, 0, v0:v0 + DV], start=True, stop=False)
                    pe.matmul(bank[6][:, dst + DV:dst + 2 * DV], aT[:, 2 * P:3 * P], z[:, 1, v0:v0 + DV],
                              start=False, stop=True).then_inc(o_mm, 1)

                def mix_tile(a, k):
                    c0 = P * k if k < 4 else 2 * GW + P * (k - 4)
                    return z[:, a, c0:c0 + P]

                transposes(1 if layer == 0 else 4, mix_tile, lambda a: pe.wait_ge(ob_done, NH * (NT * layer + a + 1)))
                pe.wait_ge(tr_lo, 4 * ((1 if layer == 0 else 4) + 1))
                project("out", layer, S_OUT[layer], D // CB, lambda j: None)
                ada_sum()
                if layer == 0:
                    transposes(2, lambda a, k: h_tok[:, a, P * k:P * k + P], lambda a: pe.wait_ge(h_done, NT + a + 1))
                    pe.wait_ge(tr_lo, 4 * 3)
                    for b in range(NBLK + 1):
                        for q in range(4):
                            if q == 2 and b and BESIDE_FFN[b - 1]:
                                ada_sum()
                            if b < NBLK:
                                s = S_FFN + split_in_block(b, q)
                                pe.wait_ge(split_done, taken(WHERE[("gate", 0, b, 0)], q))
                                if q == 0 and b:
                                    pe.wait_ge(act_done, NT * b)
                                for a in range(NT):
                                    for kk in range(2):
                                        k = 2 * q + kk
                                        wh = w_hi[:, s % NB, :].rearrange("p (g k n) -> p g k n", g=2, k=2)[:, :, kk, :]
                                        wl = w_lo[:, s % NB, :].rearrange("p (g k n) -> p g k n", g=2, k=2)[:, :, kk, :]
                                        last = three(bank[4 + a][:, :].rearrange("p (g n) -> p g n", g=2),
                                                     hT_hi[:, k, P * a:P * a + P], hT_lo[:, k, P * a:P * a + P], wh, wl,
                                                     k == 0, k == KT - 1)
                                    if q == 3 and a == 0:
                                        last.then_inc(gu_mm, 1)
                                last.then_inc(split_used, 1)
                            if q == 1 and b:
                                for a in range(NT):
                                    pe.wait_ge(act_done, NT * (b - 1) + a + 1)
                                    for c in range(2):
                                        last = pe.transpose(bank[6][:, FB * a + P * c:FB * a + P * c + P],
                                                            f_act[:, a, P * c:P * c + P], ident[:, :])
                                last.then_inc(fT_mm, 1)
                        if b:
                            pe.wait_ge(fT_lo_done, b)
                            for c in range(2):
                                s = S_FFN + down_split(b - 1, c)
                                pe.wait_ge(split_done, taken(WHERE[("down", 0, b - 1, 0)], c))
                                for a in range(NT):
                                    for half in range(2):
                                        cols = slice(CB * half, CB * half + CB)
                                        last = three(bank[2 * a + half][:, :], fT_hi[:, a, P * c:P * c + P],
                                                     fT_lo[:, a, P * c:P * c + P], w_hi[:, s % NB, cols], w_lo[:, s % NB, cols],
                                                     b == 1 and c == 0, b == NBLK and c == 1)
                                last.then_inc(split_used, 1)

            for a in range(NT):
                pe.wait_ge(h_done, 3 * NT + a + 1)
                for half in range(2):
                    for k in range(4):
                        last = pe.transpose(bank[2 * a + half][:, P * k:P * k + P],
                                            m_htok[:, a, P * (4 * half + k):P * (4 * half + k) + P], ident[:, :])
                    last.then_inc(r_mm, 1)
            pe.wait_ge(route_in, 16)
            pe.wait_ge(r_out, 4)
            for a in range(NT):
                for k in range(KT):
                    last = pe.matmul(bank[4][:, NE * a:NE * a + NE], r_hT[:, k, P * a:P * a + P], w_route[:, k, :],
                                     start=(k == 0), stop=(k == KT - 1))
            last.then_inc(logit_mm, 1)
            pe.wait_ge(mask_done, 1)
            pe.matmul(bank[4][:, 32:32 + NE], before[:, :], mask[:, 0, :], start=True, stop=True)
            pe.matmul(bank[4][:, 40:40 + NE], ones[:, :], mask[:, 0, :], start=True, stop=False)
            pe.matmul(bank[4][:, 40:40 + NE], before[:, :], mask[:, 1, :], start=False, stop=True)
            pe.matmul(bank[4][:, 64:64 + NE], ones[:, :], mask[:, 0, :], start=True, stop=False)
            pe.matmul(bank[4][:, 64:64 + NE], ones[:, :], mask[:, 1, :], start=False, stop=True).then_inc(count_mm, 1)

            def gather():
                for g, src in enumerate((htok_hi, htok_lo)):
                    for half in range(2):
                        dst = bank[(2, 3, 5, 7)[2 * g + half]]
                        for k in range(4):
                            c0 = P * (4 * half + k)
                            for a in range(NT):
                                last = pe.matmul(dst[:, P * k:P * k + P], src[:, a, c0:c0 + P], pick[:, a, :],
                                                 start=(a == 0), stop=(a == NT - 1))
                        last.then_inc(ga_mm, 1)

            def scatter(turn):
                pe.wait_ge(put_done, turn * 2 + 2)
                pe.wait_ge(ga_hi, turn * 2 + 2)
                pe.wait_ge(ga_lo, turn * 2 + 2)
                for half in range(2):
                    cols = slice(CB * half, CB * half + CB)
                    pe.wait_ge(m_yl, turn * 2 + (half + 1))
                    for a in range(NT):
                        dst = bank[((2, 3), (5, 7))[half][a]][:, :]
                        pe.matmul(dst, put[:, a, :], y_hi[:, cols], start=True, stop=False)
                        last = pe.matmul(dst, put[:, a, :], y_lo[:, cols], start=False, stop=True)
                    last.then_inc(m_sc, 1)

            pe.wait_ge(pick_done, 4)
            gather()
            pe.wait_ge(m_add, 1)
            for half in range(2):
                last = pe.matmul(bank[half][:, :], ones[:, :], m_acc[:, 0, 0:CB], start=True, stop=True)
            last.then_inc(zero_mm, 1)
            pe.wait_ge(rounds_done, 1)
            n_turns = pe.value_load(rounds[0:1, 0:1], min_val=NE, max_val=2 * NE)
            with pe.Fori(0, n_turns) as i:
                splits = i * EXPERT_SPLITS
                blocks = i * NBLK
                pe.wait_ge(ga_hi, i * 2 + 2)
                pe.wait_ge(ga_lo, i * 2 + 2)
                for b in range(NBLK + 1):
                    if b == 1:
                        pe.wait_ge(m_add, i * 4 + 5)
                    for q in range(4):
                        if b < NBLK:
                            s = S_MOE + split_in_block(b, q)
                            pe.wait_ge(split_done, splits + taken(N0 + EWHERE[("gate", b)], q))
                            for kk in range(2):
                                k = 2 * q + kk
                                wh = w_hi[:, s % NB, :].rearrange("p (g k n) -> p g k n", g=2, k=2)[:, :, kk, :]
                                wl = w_lo[:, s % NB, :].rearrange("p (g k n) -> p g k n", g=2, k=2)[:, :, kk, :]
                                last = three(bank[4 + b % 2][:, :].rearrange("p (g n) -> p g n", g=2),
                                             hgT_hi[:, k, :], hgT_lo[:, k, :], wh, wl, k == 0, k == KT - 1)
                            last.then_inc(split_used, 1)
                        if q == 2 and b == 0:
                            scatter(i)
                        if b and q == 1 + SILU_AFTER[min(b, NBLK - 1)]:
                            pe.wait_ge(m_ac, blocks + b)
                            for c in range(2):
                                last = pe.transpose(bank[6][:, FB * ((b - 1) % 2) + P * c:FB * ((b - 1) % 2) + P * c + P],
                                                    m_act[:, P * c:P * c + P], ident[:, :])
                            last.then_inc(m_tm, 1)
                        if b == 2 and q == 1:
                            for a in range(NT):
                                pe.transpose(bank[7][:, P * a:P * a + P], pick[:, a, :].bitcast(F32), ident[:, :])
                            for a in range(NT):
                                last = pe.matmul(bank[7][:, 2 * P:2 * P + 1], pick[:, a, :].bitcast(F32), gate_col[:, a:a + 1],
                                                 start=(a == 0), stop=(a == NT - 1))
                            last.then_inc(pick_mm, 1)
                    if b == NBLK:
                        pe.wait_ge(pick_done, i * 4 + 8)
                        gather()
                    if b:
                        pe.wait_ge(m_tl, blocks + b)
                        for c in range(2):
                            s = S_MOE + down_split(b - 1, c)
                            pe.wait_ge(split_done, splits + taken(N0 + EWHERE[("down", b - 1)], c))
                            for half in range(2):
                                cols = slice(CB * half, CB * half + CB)
                                last = three(bank[half][:, :], mT_hi[:, P * c:P * c + P], mT_lo[:, P * c:P * c + P],
                                             w_hi[:, s % NB, cols], w_lo[:, s % NB, cols],
                                             b == 1 and c == 0, b == NBLK and c == 1)
                            last.then_inc(split_used, 1)
            scatter(n_turns)


_IN = ["x", "c", "w_ada", "b_ada", "norm1_g", "norm2_g", "w_in", "w_out", "gmlp_vnorm_g", "gmlp_ws", "gmlp_bs",
       "lam_q1", "lam_k1", "lam_q2", "lam_k2", "diff_subln_g", "ffn_w_gate", "ffn_w_up", "ffn_w_down",
       "w_router", "moe_w_gate", "moe_w_up", "moe_w_down", "final_g"]


def kernel(**inputs):
    import concourse.bacc as bacc
    from concourse.bass_utils import run_bass_kernel_spmd

    nc = bacc.Bacc("TRN2", target_bir_lowering=False, num_devices=1)
    arrays, tensors = {}, {}
    for name in _IN:
        a = np.ascontiguousarray(inputs[name])
        arrays["in_" + name] = a
        tensors[name] = nc.dram_tensor("in_" + name, a.shape, mybir.dt.from_np(a.dtype), kind="ExternalInput").ap()
    out = nc.dram_tensor("out", (SEQ, D), F32, kind="ExternalOutput").ap()
    trunk(nc, tensors, out)
    r = run_bass_kernel_spmd(nc, [arrays], core_ids=[0])
    return np.asarray(r.results[0]["out"]).reshape(1, SEQ, D)
```

```python
import math
from contextlib import ExitStack

import numpy as np
import concourse.bass as bass
from concourse import mybir
from concourse.alu_op_type import AluOpType as ALU

ACT = mybir.ActivationFunctionType
AX = mybir.AxisListType
F32 = mybir.dt.float32
F32R = mybir.dt.float32r
I32 = mybir.dt.int32
U32 = mybir.dt.uint32

P = 128
D = 1024
KT = D // P
SEQ = 256
NT = SEQ // P
DEPTH = 2
GW = 512
NG = 8
GD = GW // NG
NH = 4
DV = 128
DH = 64
INW = 2 * GW + 3 * NH * DV
FF = 2816
NE = 8
FB = 256
NBLK = FF // FB
CB = 512
EPS = 1e-6
NEG = -1e30
RING = 11
NB = 3
NB_MOE = 6
CHUNK = 2048
SUB = 1024
MOD_BLOCKS = 12
SPLITS_PER_BLOCK = 6
EXPERT_CHUNKS = 3 * NBLK
EXPERT_SPLITS = SPLITS_PER_BLOCK * NBLK
SILU_AFTER = [None, 3] + [0] * (NBLK - 2)
SCATTERED = [(1, 1, 6), (0, 1, 7), (0, 0, 2), (1, 0, 3)]
BY_HALF = [(0, 0), (1, 0), (0, 1), (1, 1)]
BY_TILE = [(0, 0), (0, 1), (1, 0), (1, 1)]
SH1, SC1, G1, SH2, SC2, G2 = range(6)


BESIDE_IN = [[(0, 4), (0, 5), (0, 6), (0, 7), (0, 8)], [None, (1, 7), (1, 8), (1, 9), (1, 10)]]
BESIDE_OUT = [(0, 9), (1, 11)]
BESIDE_FFN = [(0, 10), (0, 11), (1, 0), (1, 1), (1, 2), (1, 3), (1, 4), (1, 5), (1, 6), None, None, None]
FIRST_ADA = [2, 0, 3, 1]


WARM_HEAD, WARM_MIX, WARM_NORM = 8, 16, 24


def chunk_stream():
    s = [("ada", 0, j, half) for j in FIRST_ADA for half in range(2)]
    for layer in range(DEPTH):
        for j in range(INW // CB):
            for half in range(2):
                s.append(("in", layer, j, half))
                if BESIDE_IN[layer][j]:
                    s.append(("ada", *BESIDE_IN[layer][j], half))
        s += [("out", layer, 0, 0), ("out", layer, 1, 0)]
        for half in range(2):
            s += [("ada", *BESIDE_OUT[layer], half), ("out", layer, half, 1)]
        if layer == 0:
            for b in range(NBLK + 1):
                if b < NBLK:
                    s += [("gate", 0, b, 0), ("up", 0, b, 0)]
                if BESIDE_FFN[b]:
                    s.append(("ada", *BESIDE_FFN[b], 0))
                if b >= 1:
                    s.append(("down", 0, b - 1, 0))
                if BESIDE_FFN[b]:
                    s.append(("ada", *BESIDE_FFN[b], 1))
    return s


def expert_chunks():
    s = []
    for b in range(NBLK + 1):
        if b < NBLK:
            s += [("gate", b), ("up", b)]
        if b >= 1:
            s.append(("down", b - 1))
    return s


def trunk(nc, t, out):
    STREAM = chunk_stream()
    WHERE = {c: n for n, c in enumerate(STREAM)}
    ADA = [(c[1], c[2]) for c in STREAM if c[0] == "ada" and c[3] == 0]
    N0 = len(STREAM)
    EXPERT = expert_chunks()
    EWHERE = {c: n for n, c in enumerate(EXPERT)}
    S_IN = [0, 0]
    S_OUT = [0, 0]
    S_IN[0] = 0
    S_OUT[0] = S_IN[0] + 4 * (INW // CB)
    S_FFN = S_OUT[0] + 4 * (D // CB)
    S_IN[1] = S_FFN + EXPERT_SPLITS
    S_OUT[1] = S_IN[1] + 4 * (INW // CB)
    S_MOE = S_OUT[1] + 4 * (D // CB)
    assert EXPERT_SPLITS % NB_MOE == 0 and NB_MOE == 2 * NB

    def split_in_block(b, q):
        return 0 + q if b == 0 else 4 + (b - 1) * 6 + q

    def down_split(b, c):
        return (4 + b * 6 + 4 + c) if b + 1 < NBLK else 4 + b * 6 + c

    ctx = ExitStack()
    with ctx:
        at = [(nc.sbuf_base + 63) // 64 * 64]

        def sb(name, shape, dt=F32, offset=None):
            size = int(np.prod(shape[1:])) * 4
            size = (size + 31) // 32 * 32
            where = at[0] if offset is None else offset
            assert where + size <= nc.sbuf_usable_end, (name, where + size)
            h = nc.alloc_sbuf_tensor_at(name, shape, dt, offset=where)
            if offset is None:
                at[0] += size
            return h

        raw = sb("raw", [P, RING, CHUNK])
        w_hi = sb("w_hi", [P, NB, SUB], F32R)
        w_lo = sb("w_lo", [P, NB, SUB], F32R)
        mod = sb("mod", [P, 6, D])
        at_mod = at[0] - 6 * D * 4
        x = sb("x", [P, NT, D])
        gain = sb("gain", [P, D])
        ones_r = sb("ones_r", [P, P], F32R)
        ident_r = sb("ident_r", [P, P], F32R)
        ident = ident_r[:, :].bitcast(F32)
        upto = sb("upto", [P, P])
        future = sb("future", [P, P], F32R)
        at_ada = at[0]
        ada_bias = sb("ada_bias", [P, CB])
        ada_lo = sb("ada_lo", [P, CB], F32R)
        ada_acc = sb("ada_acc", [P, 2, CB])
        ada_hi = sb("ada_hi", [P, CB], F32R)
        at_rows = at[0]
        b_rows = sb("b_rows", [P, CB])
        silu_c = sb("silu_c", [P, KT])
        eps_col = sb("eps_col", [P, 1])
        ssq = sb("ssq", [P, 2, NT])
        mean0 = sb("mean0", [P, NT])
        std = sb("std", [P, NT])
        rstd = sb("rstd", [P, NT])
        lam_sum = sb("lam_sum", [P, 2, DEPTH])
        lam_exp = sb("lam_exp", [P, 2, DEPTH])
        lam = sb("lam", [P, DEPTH])
        w_route = sb("w_route", [P, KT, NE])
        base = at[0]
        hT_hi = sb("hT_hi", [P, KT, SEQ], F32R)
        hT_lo = sb("hT_lo", [P, KT, SEQ], F32R)
        z = sb("z", [P, NT, INW])
        wsT = sb("wsT", [P, NG, P])
        ws_raw = sb("ws_raw", [P, NG, P])
        at_ws = at[0] - NG * P * 4
        aT = sb("aT", [P, 3 * P], offset=at_ws)
        subln = sb("subln", [P, DV])
        gstat = sb("gstat", [P, 4 * NG * NT])
        hstat = sb("hstat", [P, 2, 16])
        vgain = sb("vgain", [P, GW], offset=at_ws + NG * P * 2)
        lam_rows = sb("lam_rows", [P, 4, DEPTH, DH], offset=base + 2 * KT * SEQ * 4 + NT * INW * 4)
        raw_ones = sb("raw_ones", [P, P], offset=base + P * 4)
        raw_future = sb("raw_future", [P, P], offset=base + 2 * P * 4)
        raw_ident = sb("raw_ident", [P, P], offset=base + 3 * P * 4)
        c_rows = sb("c_rows", [KT, P], offset=base + 4 * P * 4)
        bsT = sb("bsT", [P, NG])
        o = base
        qT = sb("qT", [P, NH, SEQ], offset=o); o += NH * SEQ * 4
        kT = sb("kT", [P, NH, SEQ], offset=o); o += NH * SEQ * 4
        prob = sb("prob", [P, 2, 2, 3 * P], offset=o); o += 2 * 2 * 3 * P * 4
        vsq = sb("vsq", [P, GW], offset=o); o += GW * 4
        assert o <= base + 2 * KT * SEQ * 4
        zbase = base + 2 * KT * SEQ * 4
        h_tok = sb("h_tok", [P, NT, D], offset=zbase)
        y_scaled = sb("y_scaled", [P, 2, CB], offset=zbase + NT * D * 4)
        silu_b = sb("silu_b", [P, 2, 2, P], offset=zbase + NT * D * 4)
        o = zbase + NT * D * 4 + 2 * CB * 4
        f_silu = sb("f_silu", [P, NT, FB], offset=o); o += NT * FB * 4
        f_act = sb("f_act", [P, NT, FB], offset=o); o += NT * FB * 4
        fT_hi = sb("fT_hi", [P, NT, FB], F32R, offset=o); o += NT * FB * 4
        fT_lo = sb("fT_lo", [P, NT, FB], F32R, offset=o); o += NT * FB * 4
        more_hi = sb("more_hi", [P, NB, SUB], F32R, offset=at_mod)
        more_lo = sb("more_lo", [P, 2, SUB], F32R, offset=at_mod + NB * SUB * 4)
        more_lo2 = sb("more_lo2", [P, SUB], F32R, offset=at_ada + 2 * NT * P * 4)
        assert (NB + 2) * SUB <= G2 * D and 2 * NT * P + SUB <= 5 * CB
        o = base
        htok_hi = sb("htok_hi", [P, NT, D], F32R, offset=o); o += NT * D * 4
        htok_lo = sb("htok_lo", [P, NT, D], F32R, offset=o); o += NT * D * 4
        f_scaled = sb("f_scaled", [P, 2, CB], offset=base)
        y_hi = sb("y_hi", [P, D], F32R, offset=o)
        m_htok = sb("m_htok", [P, NT, D], offset=o)
        o += D * 4
        y_lo = sb("y_lo", [P, D], F32R, offset=o); o += D * 4
        m_acc = sb("m_acc", [P, NT, D], offset=o)
        r_hT = sb("r_hT", [P, KT, SEQ], offset=o)
        o += NT * D * 4
        hgT_hi = sb("hgT_hi", [P, KT, P], F32R, offset=o); o += KT * P * 4
        hgT_lo = sb("hgT_lo", [P, KT, P], F32R, offset=o); o += KT * P * 4
        slot_int = sb("slot_int", [P, P], I32, offset=o)
        raw_before = sb("raw_before", [P, P], offset=o + P * 4)
        before = sb("before", [P, P], offset=o + FB * 4)
        m_silu = sb("m_silu", [P, FB], offset=o); o += FB * 4
        m_act = sb("m_act", [P, FB], offset=o); o += FB * 4
        mT_hi = sb("mT_hi", [P, FB], F32R, offset=o); o += FB * 4
        mT_lo = sb("mT_lo", [P, FB], F32R, offset=o); o += FB * 4
        pick = sb("pick", [P, NT, P], F32R, offset=at_ada)
        put = sb("put", [P, NT, P], F32R, offset=at_ada + NT * P * 4)
        gate_col = sb("gate_col", [P, NT], offset=o); o += 32
        slot_gate = sb("slot_gate", [P, 1], offset=o); o += 32
        slot_of = sb("slot_of", [P, NT, 2 * NE + 1], offset=o); o += 160
        gate_of = sb("gate_of", [P, NT, 2 * NE + 1], offset=o); o += 160
        logit = sb("logit", [P, NT, NE], offset=o); o += 64
        top = sb("top", [P, NT, 8], offset=o); o += 64
        top_i = sb("top_i", [P, NT, 8], U32, offset=o); o += 64
        top_f = sb("top_f", [P, NT, 8], offset=o); o += 64
        gap = sb("gap", [P, NT, 1], offset=o); o += 32
        e2 = sb("e2", [P, NT, 1], offset=o); o += 32
        w12 = sb("w12", [P, NT, 2], offset=o); o += 32
        wsum = sb("wsum", [P, NT, 1], offset=o); o += 32
        hit = sb("hit", [P, NT, 2, NE], offset=o); o += NT * 2 * NE * 4
        mask = sb("mask", [P, NT, NE], offset=o); o += 64
        most = sb("most", [P, 1], offset=o); o += 32
        rounds_f = sb("rounds_f", [P, 1], offset=o); o += 32
        rounds = sb("rounds", [P, 1], I32, offset=o); o += 32
        slot_no = sb("slot_no", [P, P], offset=at_rows)
        assert o <= nc.sbuf_usable_end, o

        def hi_of(s):
            if s < S_MOE:
                return w_hi[:, s % NB, :]
            b = (s - S_MOE) % NB_MOE
            return more_hi[:, b, :] if b < NB else w_hi[:, (s - NB_MOE) % NB, :]

        def lo_of(s):
            if s < S_MOE:
                return w_lo[:, s % NB, :]
            b = (s - S_MOE) % NB_MOE
            if b < NB:
                return more_lo[:, b, :] if b < 2 else more_lo2[:, :]
            return w_lo[:, (s - NB_MOE) % NB, :]

        bank = [ctx.enter_context(nc.psum_tensor(f"bank{i}", [P, 512], F32)) for i in range(8)]

        def wait_quarter(engine, sems, stage, n):
            engine.wait_ge(sems[n % 2], 2 * stage + n // 2 + 1)

        def is_scale(i):
            return ADA[i][1] // 2 in (SC1, SC2)

        def mod_block(i):
            piece, half = divmod(ADA[i][1], 2)
            return mod[:, piece, CB * half:CB * half + CB]

        def score_bank(h, m):
            return bank[2 * ((h + 1) % 2) + m]

        def qk_bank(part, a):
            return bank[(4, 5, 6, 2)[2 * part + a]]

        def tr_bank(i, half, a):
            return bank[2 + a] if half == 0 else bank[(0 if i == 2 else 4) + a]

        def sem(name):
            return ctx.enter_context(nc.semaphore(name))

        chunk_in = [sem(f"chunk_in{i}") for i in range(RING)]
        hi_done = sem("hi_done")
        split_done = sem("split_done")
        split_used = sem("split_used")
        sp_turn = sem("sp_turn")
        first_in = sem("first_in")
        x_in = sem("x_in")
        gain0_in = sem("gain0_in")
        gain_in = sem("gain_in")
        gain_used = sem("gain_used")
        rows_in = sem("rows_in")
        bias_in = sem("bias_in")
        bias_used = sem("bias_used")
        start_read = sem("start_read")
        silu_b_done = sem("silu_b_done")
        ada_hi_done = sem("ada_hi_done")
        ada_split = sem("ada_split")
        consts = sem("consts")
        pool_step = sem("pool_step")
        mixer_in = sem("mixer_in")
        vgain_in = sem("vgain_in")
        lam_in = sem("lam_in")
        route_in = sem("route_in")
        c_mm = sem("c_mm")
        silu_c_done = sem("silu_c_done")
        ada_mm = sem("ada_mm")
        ada_out = sem("ada_out")
        ssq_done = sem("ssq_done")
        std_done = sem("std_done")
        h_scaled = sem("h_scaled")
        h_done = sem("h_done")
        h_own = sem("h_own")
        tr_mm = sem("tr_mm")
        tr_hi = sem("tr_hi")
        tr_lo = sem("tr_lo")
        z_out = sem("z_out")
        ws_mm = sem("ws_mm")
        ws_out = sem("ws_out")
        qk_mm = sem("qk_mm")
        qk_out_a = sem("qk_out_a")
        qk_out_v = sem("qk_out_v")
        vstat_done = sem("vstat_done")
        vstd_done = sem("vstd_done")
        vrstd_done = sem("vrstd_done")
        v_done = sem("v_done")
        vm_mm = sem("vm_mm")
        ua_done = sem("ua_done")
        v_step = sem("v_step")
        v_step2 = sem("v_step2")
        sc_mm = sem("sc_mm")
        negmax = sem("negmax")
        exp_done = sem("exp_done")
        a_done = sem("a_done")
        at_mm = sem("at_mm")
        at_out = sem("at_out")
        o_mm = sem("o_mm")
        o_out = sem("o_out")
        lam_step = sem("lam_step")
        lam_dots = sem("lam_dots")
        lam_exps = sem("lam_exps")
        osq_done = sem("osq_done")
        ostd_done = sem("ostd_done")
        ob_done = sem("ob_done")
        ys_done = sem("ys_done")
        x_step = sem("x_step")
        x_own = sem("x_own")
        dve_step = sem("dve_step")
        act_step = sem("act_step")
        gu_mm = sem("gu_mm")
        silu_done = sem("silu_done")
        act_done = sem("act_done")
        fT_mm = sem("fT_mm")
        fT_hi_done = sem("fT_hi_done")
        fT_lo_done = sem("fT_lo_done")
        htok_split = sem("htok_split")
        r_mm = sem("r_mm")
        r_out = sem("r_out")
        logit_mm = sem("logit_mm")
        gap_done = sem("gap_done")
        gexp_done = sem("gexp_done")
        mask_done = sem("mask_done")
        count_mm = sem("count_mm")
        rounds_done = sem("rounds_done")
        pick_done = sem("pick_done")
        pick_mm = sem("pick_mm")
        put_done = sem("put_done")
        ga_mm = sem("ga_mm")
        ga_hi = sem("ga_hi")
        ga_lo = sem("ga_lo")
        m_sl = sem("m_sl")
        m_ac = sem("m_ac")
        m_tm = sem("m_tm")
        m_th = sem("m_th")
        m_tl = sem("m_tl")
        zero_mm = sem("zero_mm")
        m_yh = sem("m_yh")
        m_yl = sem("m_yl")
        m_sc = sem("m_sc")
        m_add = sem("m_add")
        out_ready = sem("out_ready")
        out_sent = [sem(f"out_sent{a}") for a in range(NT)]

        def kview(ap):
            return ap.rearrange("(k p) n -> p k n", p=P)

        def chunk_source(c):
            kind, layer, j, half = c
            if kind == "ada":
                return kview(t["w_ada"][layer])[:, 4 * half:4 * half + 4, CB * j:CB * j + CB]
            if kind == "in":
                return kview(t["w_in"][layer])[:, 4 * half:4 * half + 4, CB * j:CB * j + CB]
            if kind == "out":
                return kview(t["w_out"][layer])[:, 4 * half:4 * half + 4, CB * j:CB * j + CB]
            if kind == "gate":
                return kview(t["ffn_w_gate"][0])[:, :, FB * j:FB * j + FB]
            if kind == "up":
                return kview(t["ffn_w_up"][0])[:, :, FB * j:FB * j + FB]
            return kview(t["ffn_w_down"][0])[:, 2 * j:2 * j + 2, :]

        def expert_source(e, kind, b):
            name = {"gate": "moe_w_gate", "up": "moe_w_up", "down": "moe_w_down"}[kind]
            v = t[name][0].rearrange("e (k p) n -> e p k n", p=P)
            if kind == "down":
                v = v[bass.ds(e, 1), :, 2 * b:2 * b + 2, :]
            else:
                v = v[bass.ds(e, 1), :, :, FB * b:FB * b + FB]
            return v.rearrange("a p k n -> (a p) k n")

        def ring_slot(n):
            s = n % RING
            return s

        def landed(n):
            return 16 * (n // RING + 1)

        def pair_slots(n):
            a, b = n % RING, (n + 1) % RING
            return min(a, b), max(a, b)

        def load_slot(kind, n):
            if kind == "gate":
                return pair_slots(n)[0]
            if kind == "up":
                return pair_slots(n - 1)[1]
            return n % RING

        def landed_in(slot, n):
            return 16 * (n // RING + 1)

        def slot_count(kind, n):
            slot = load_slot(kind, n)
            own = n if n % RING == slot else (n + 1 if kind == "gate" else n - 1)
            assert own % RING == slot
            return slot, 16 * (own // RING + 1)

        def taken(n, q):
            return 2 * n + q + 1

        def freed(n, kind):
            return taken(n + 1, 1) if kind == "gate" else taken(n, 1)

        def gu_raw(n, q):
            a, b = pair_slots(n)
            return raw[:, a:b + 1:b - a, 2 * q * FB:(2 * q + 2) * FB]

        def down_raw(n, c):
            return raw[:, n % RING, c * SUB:(c + 1) * SUB]

        blk = ctx.enter_context(nc.Block())

        @blk.sync
        def _(sp):
            sp.dma_start(c_rows[:, :], t["c"][0].rearrange("(k p) -> k p", p=P)).then_inc(first_in, 16)
            sp.wait_ge(pool_step, 1)
            sp.dma_start(b_rows[0:DEPTH * MOD_BLOCKS, :], t["b_ada"].rearrange("l (j n) -> (l j) n", n=CB))\
              .then_inc(rows_in, 16)
            sp.dma_start(gain[:, :], t["norm1_g"][0].partition_broadcast(P)).then_inc(gain0_in, 16)
            for n, c in enumerate(STREAM):
                if n >= RING:
                    ahead = n + 1 if c[0] == "gate" else n
                    sp.wait_ge(split_done, freed(ahead - RING, STREAM[ahead - RING][0]))
                    for past in STREAM[max(n - RING, 0):ahead - RING + 1]:
                        if past[0] == "ada" and (past[1], past[2]) in ADA[:4]:
                            sp.wait_ge(start_read, 2 * ADA.index((past[1], past[2])) + past[3] + 1)
                slot, _ = slot_count(c[0], n)
                src = chunk_source(c)
                sp.dma_start(raw[:, slot, :].rearrange("p (k n) -> p k n", n=src.shape[2]), src)\
                  .then_inc(chunk_in[slot], 16)
                if n == 1:
                    sp.dma_start(x[:, :, :], t["x"][0].rearrange("(a p) d -> p a d", p=P)).then_inc(x_in, 16)

            def load_expert(e, turn):
                for j, (kind, b) in enumerate(EXPERT):
                    n = N0 + j
                    ahead = n + 1 if kind == "gate" else n
                    past = EXPERT[ahead - N0 - RING][0]
                    sp.wait_ge(split_done, turn * EXPERT_SPLITS + freed(ahead - RING, past))
                    sp.sem_inc(sp_turn, 1)
                    slot, _ = slot_count(kind, n)
                    src = expert_source(e, kind, b)
                    sp.dma_start(raw[:, slot, :].rearrange("p (k n) -> p k n", n=src.shape[2]), src)\
                      .then_inc(chunk_in[slot], 16)

            with sp.Fori(0, NE) as e:
                load_expert(e, e)
            sp.wait_ge(rounds_done, 1)
            n_turns = sp.value_load(rounds[0:1, 0:1], min_val=NE, max_val=2 * NE)
            with sp.If(n_turns > NE):
                with sp.Fori(0, NE) as e:
                    load_expert(e, e + NE)
            for a in range(NT):
                sp.wait_ge(out_ready, 2 * a + 2)
                sp.dma_start(out.rearrange("(a p) d -> p a d", p=P)[:, a, :], h_tok[:, a, :]).then_inc(out_sent[a], 16)
            for a in range(NT):
                sp.wait_ge(out_sent[a], 16)

        @blk.gpsimd
        def _(pool):
            pool.memset(b_rows[:, :], 0.0).then_inc(pool_step, 1)
            pool.memset(raw_ones[:, :], 1.0).then_inc(pool_step, 1)
            pool.memset(raw_ident[:, :], 0.0).then_inc(pool_step, 1)
            pool.memset(raw_future[:, :], 0.0).then_inc(pool_step, 1)
            pool.memset(eps_col[:, :], EPS).then_inc(pool_step, 1)
            pool.wait_ge(pool_step, 5)
            pool.affine_select(out=raw_ident[:, :], in_=raw_ident[:, :], compare_op=ALU.not_equal, fill=1.0,
                               base=0, pattern=[[-1, P]], channel_multiplier=1).then_inc(consts, 1)
            pool.affine_select(out=upto[:, :], in_=raw_ones[:, :], compare_op=ALU.is_ge, fill=0.0,
                               base=0, pattern=[[1, P]], channel_multiplier=-1).then_inc(consts, 1)
            pool.affine_select(out=raw_future[:, :], in_=raw_future[:, :], compare_op=ALU.is_ge, fill=NEG,
                               base=0, pattern=[[-1, P]], channel_multiplier=1).then_inc(consts, 1)
            pool.tensor_copy(ones_r[:, :], raw_ones[:, :]).then_inc(consts, 1)
            pool.wait_ge(consts, 3)
            pool.tensor_copy(ident_r[:, :], raw_ident[:, :]).then_inc(consts, 1)
            pool.tensor_copy(future[:, :], raw_future[:, :]).then_inc(consts, 1)

            def broadcast(dst, row, signal):
                pool.dma_start(dst, row.partition_broadcast(P)).then_inc(signal, 16)

            gains = [t["norm1_g"][0], t["norm2_g"][0], t["norm1_g"][1], t["norm2_g"][1], t["final_g"]]

            def load_gain(i):
                pool.wait_ge(gain_used, 2 * i)
                broadcast(gain[:, :], gains[i], gain_in)

            def bias(first, last):
                for i in range(first, last):
                    layer, j = ADA[i]
                    row = MOD_BLOCKS * layer + j
                    if i:
                        pool.wait_ge(bias_used, i)
                    pool.tensor_scalar(ada_bias[:, :], b_rows[:, :], ident[:, row:row + 1], 0.0, ALU.mult, ALU.add)\
                        .then_inc(bias_in, 1)

            def modulate(first, last):
                for i in range(first, last):
                    if i + 1 < len(ADA):
                        bias(i + 1, i + 2)
                    pool.wait_ge(ada_hi_done, i - 3)
                    pool.tensor_tensor(ada_lo[:, :], ada_acc[:, i % 2, :], ada_hi[:, :].bitcast(F32), ALU.subtract)\
                        .then_inc(ada_split, 1)

            def shift_h(i, dst, piece, quarters=(0, 2)):
                for n in quarters:
                    a, half = BY_HALF[n]
                    pool.wait_ge(h_scaled, 4 * i + n + 1)
                    cols = slice(CB * half, CB * half + CB)
                    pool.tensor_tensor(dst[:, a, cols], dst[:, a, cols], mod[:, piece, cols], ALU.add).then_inc(h_done, 1)

            def load_mixer(layer):
                pool.dma_start(ws_raw[:, :, :], t["gmlp_ws"][layer].rearrange("g a b -> a g b")).then_inc(mixer_in, 16)
                pool.dma_start(bsT[:, :], t["gmlp_bs"][layer].rearrange("g a -> a g"), allow_slow_non_contiguous=True)\
                    .then_inc(mixer_in, 16)
                broadcast(subln[:, :], t["diff_subln_g"][layer], mixer_in)

            def load_vgain(layer):
                pool.wait_ge(ws_mm, 2 * (layer + 1))
                broadcast(vgain[:, :], t["gmlp_vnorm_g"][layer], vgain_in)

            def v_squares(layer):
                pool.wait_ge(z_out, NT * ((INW // CB) * layer + 2))
                for a in range(NT):
                    va = z[:, a, GW:2 * GW]
                    pool.tensor_tensor(z[:, a, 4 * CB:5 * CB], va, va, ALU.mult).then_inc(v_step, 1)

            def v_scaled(layer):
                pool.wait_ge(vrstd_done, layer + 1)
                pool.wait_ge(vgain_in, 16 * (layer + 1))
                for a in range(NT):
                    va = z[:, a, GW:2 * GW]
                    vg = va.rearrange("p (g n) -> p g n", g=NG)
                    pool.tensor_tensor(vg, vg, gstat[:, NG * a:NG * a + NG].unsqueeze(2).to_broadcast([P, NG, GD]),
                                       ALU.mult).then_inc(v_step2, 1)
                    pool.wait_ge(v_step2, NT * layer + a + 1)
                    pool.tensor_tensor(va, va, vgain[:, :], ALU.mult).then_inc(v_done, 1)

            def add_to_x(stage, order, src):
                for n in (0, 2):
                    a, half = order[n]
                    pool.wait_ge(ys_done, 4 * stage + n + 1)
                    xs = x[:, a, CB * half:CB * half + CB]
                    pool.tensor_tensor(xs, xs, src[:, 0, :], ALU.add).then_inc(x_step, 1)

            pool.wait_ge(consts, 6)
            pool.wait_ge(rows_in, 16)
            bias(0, 1)
            for i, name in enumerate(("lam_q1", "lam_k1", "lam_q2", "lam_k2")):
                broadcast(lam_rows[:, i, :, :], t[name].rearrange("l n -> (l n)"), lam_in)
            load_mixer(0)
            pool.dma_start(w_route[:, :, :], t["w_router"][0].rearrange("(k p) e -> p k e", p=P)).then_inc(route_in, 16)
            bias(1, 4)
            shift_h(0, h_tok, SH1, (0,))
            bias(4, 5)
            shift_h(0, h_tok, SH1, (2,))
            load_gain(1)
            load_vgain(0)
            modulate(4, 6)
            v_squares(0)
            modulate(6, 8)
            v_scaled(0)
            modulate(8, 10)
            add_to_x(0, BY_HALF, y_scaled)
            shift_h(1, h_tok, SH2)
            load_gain(2)
            modulate(10, 14)
            load_mixer(1)
            modulate(14, 18)
            load_gain(3)
            modulate(18, 19)
            add_to_x(1, BY_TILE, y_scaled)
            shift_h(2, h_tok, SH1)
            load_vgain(1)
            modulate(19, 20)
            v_squares(1)
            modulate(20, 22)
            v_scaled(1)
            modulate(22, 24)
            add_to_x(2, BY_HALF, y_scaled)
            shift_h(3, m_htok, SH2)
            pool.memset(raw_before[:, :], 1.0).then_inc(pool_step, 1)
            pool.iota(slot_int[:, :], pattern=[[1, P]], base=0, channel_multiplier=0).then_inc(pool_step, 1)
            pool.wait_ge(pool_step, 7)
            pool.affine_select(out=before[:, :], in_=raw_before[:, :], compare_op=ALU.is_gt, fill=0.0,
                               base=0, pattern=[[1, P]], channel_multiplier=-1).then_inc(consts, 1)
            pool.tensor_copy(slot_no[:, :], slot_int[:, :]).then_inc(consts, 1)
            load_gain(4)
            pool.wait_ge(logit_mm, 1)
            pool.memset(m_acc[:, :, :], 0.0).then_inc(m_add, 1)
            add_to_x(3, BY_TILE, f_scaled)

        @blk.scalar
        def _(act):
            steps = [0]

            def then(ins):
                steps[0] += 1
                ins.then_inc(act_step, 1)
                act.wait_ge(act_step, steps[0])

            def split_hi(s, src, like, base=0):
                buffers = NB if s < S_MOE else NB_MOE
                if s >= NB:
                    act.wait_ge(split_used, base + (s - buffers + 1))
                act.activation(like(hi_of(s)), src, ACT.Copy).then_inc(hi_done, 1)

            def flat(ap):
                return ap

            def pairs(ap):
                return ap.rearrange("p (g n) -> p g n", g=2)

            def wait_chunk(kind, n, base=0):
                slot, count = slot_count(kind, n)
                act.wait_ge(chunk_in[slot], base + count)

            def std_of_rows(i, junk):
                order = BY_HALF if i % 2 else BY_TILE
                for n, (a, half) in enumerate(order):
                    if i == 0:
                        act.wait_ge(x_in, 16)
                    else:
                        wait_quarter(act, (x_step, x_own), i - 1, n)
                    cols = slice(CB * half, CB * half + CB)
                    then(act.activation(junk[:, a, cols], x[:, a, cols], ACT.Square, accum_out=ssq[:, half, a:a + 1]))
                    if half == 0:
                        then(act.activation(mean0[:, a:a + 1], ssq[:, 0, a:a + 1], ACT.Identity,
                                            bias=eps_col[:, 0:1], scale=1.0 / D))
                    else:
                        act.activation(std[:, a:a + 1], ssq[:, 1, a:a + 1], ACT.Sqrt, bias=mean0[:, a:a + 1],
                                       scale=1.0 / D).then_inc(std_done, 1)

            def transposed_hi(dst, i, half):
                for a in range(NT):
                    act.wait_ge(tr_mm, 4 * i + 2 * half + a + 1)
                    act.activation(dst[:, 4 * half:4 * half + 4, P * a:P * a + P],
                                   tr_bank(i, half, a)[:, :].rearrange("p (k n) -> p k n", k=4),
                                   ACT.Copy).then_inc(tr_hi, 1)

            ada_no = [4]
            ada_seen = [4]

            def modulation_out(before_block=None):
                upto_block = ada_no[0] if before_block is None else before_block
                for i in range(ada_seen[0], upto_block):
                    if not is_scale(i):
                        act.wait_ge(ada_mm, i + 1)
                        act.activation(mod_block(i), bank[7][:, :], ACT.Copy).then_inc(ada_out, 1)
                ada_seen[0] = max(ada_seen[0], upto_block)

            def modulation_hi():
                i = ada_no[0]
                ada_no[0] += 1
                act.wait_ge(split_done, taken(WHERE[("ada", *ADA[i], 1)], 1))
                modulation_out(i)
                act.wait_ge(ada_mm, i)
                act.activation(ada_hi[:, :], ada_acc[:, i % 2, :], ACT.Copy).then_inc(ada_hi_done, 1)

            def beside(i, piece):
                if piece in (1, 2):
                    transposed_hi(hT_hi, i, piece - 1)

            act.wait_ge(c_mm, 1)
            act.activation(silu_c[:, :], bank[6][:, 0:KT], ACT.Silu).then_inc(silu_c_done, 1)
            act.wait_ge(silu_c_done, 1)
            act.activation(silu_b[:, :, :, :], silu_c[:, :].rearrange("p (h k) -> p h k", h=2)[:, :, 0:2]
                           .unsqueeze(3).to_broadcast([P, 2, 2, P]), ACT.Copy).then_inc(silu_b_done, 1)
            act.wait_ge(consts, 5)
            for layer in range(DEPTH):
                std_of_rows(2 * layer, h_tok)

                def z_block(j):
                    act.wait_ge(split_used, S_IN[layer] + 4 * (j + 1))
                    if j == INW // CB - 1:
                        act.wait_ge(vstat_done, NT * (layer + 1))
                    for a in range(NT):
                        act.activation(z[:, a, CB * j:CB * j + CB], bank[2 * (j % 2) + a][:, :],
                                       ACT.Gelu_apprx_tanh if j < 2 else ACT.Copy).then_inc(z_out, 1)

                for j in range(INW // CB):
                    for half in range(2):
                        n = WHERE[("in", layer, j, half)]
                        wait_chunk("in", n)
                        for q in range(2):
                            split_hi(S_IN[layer] + 4 * j + 2 * half + q,
                                     raw[:, n % RING, q * SUB:(q + 1) * SUB], flat)
                            beside(3 * layer, 4 * j + 2 * half + q)
                        if half == 0 and j:
                            if BESIDE_IN[layer][j - 1]:
                                modulation_hi()
                            z_block(j - 1)
                        if half == 0 and j == INW // CB - 1:
                            act.wait_ge(vstat_done, NT * (layer + 1))
                            act.activation(gstat[:, 16:32], gstat[:, 0:16], ACT.Sqrt, bias=eps_col[:, 0:1],
                                           scale=1.0 / GD).then_inc(vstd_done, 1)
                modulation_hi()
                act.wait_ge(split_used, S_IN[layer] + 4 * (INW // CB))
                for a in range(NT):
                    act.wait_ge(qk_mm, 4 * layer + a + 1)
                    act.activation(qT[:, :, P * a:P * a + P], qk_bank(0, a)[:, :].rearrange("p (h n) -> p h n", h=NH),
                                   ACT.Copy).then_inc(qk_out_a, 1)
                z_block(INW // CB - 1)
                if layer == 0:
                    act.wait_ge(lam_dots, 1)
                    act.activation(lam_exp[:, :, :], lam_sum[:, :, :], ACT.Exp).then_inc(lam_exps, 1)

                def exponentials(h):
                    st = hstat[:, h % 2, :]
                    act.wait_ge(negmax, NH * layer + h + 1)
                    for m in range(2):
                        for a in range(NT):
                            cols = slice(0, P) if a == 0 else slice(P, 3 * P)
                            act.activation(prob[:, h % 2, m, cols], score_bank(h, m)[:, cols], ACT.Exp,
                                           bias=st[:, 4 + 2 * m + a:5 + 2 * m + a], scale=DH ** -0.5,
                                           accum_out=st[:, 8 + 2 * m + a:9 + 2 * m + a]).then_inc(exp_done, 1)

                def head_out(h):
                    act.wait_ge(at_mm, NH * layer + h + 1)
                    act.activation(aT[:, :], bank[4 + h % 2][:, 0:3 * P], ACT.Copy).then_inc(at_out, 1)

                def head_sums(h):
                    act.wait_ge(o_mm, NH * layer + h + 1)
                    act.activation(z[:, :, 2 * GW + DV * h:2 * GW + DV * h + DV],
                                   bank[6][:, FB * (h % 2):FB * (h % 2) + FB].rearrange("p (a n) -> p a n", a=NT),
                                   ACT.Copy).then_inc(o_out, 1)
                    for a in range(NT):
                        c0 = FB * (h % 2) + DV * a
                        act.activation(vsq[:, DV * a:DV * a + DV], bank[6][:, c0:c0 + DV], ACT.Square,
                                       accum_out=gstat[:, 32 + NH * a + h:33 + NH * a + h]).then_inc(osq_done, 1)

                def out_hi(piece):
                    j, half = (piece // 2) % 2, piece // 4
                    n = WHERE[("out", layer, j, half)]
                    wait_chunk("out", n)
                    q = piece % 2
                    split_hi(S_OUT[layer] + piece, raw[:, n % RING, q * SUB:(q + 1) * SUB], flat)

                exponentials(0)
                exponentials(1)
                modulation_out()
                head_out(0)
                exponentials(2)
                head_sums(0)
                head_out(1)
                exponentials(3)
                head_sums(1)
                transposed_hi(hT_hi, 3 * layer + 1, 0)
                head_out(2)
                act.activation(gstat[:, 56:57], eps_col[:, :], ACT.Sqrt)
                head_sums(2)
                out_hi(0)
                head_out(3)
                head_sums(3)
                act.wait_ge(osq_done, NT * NH * (layer + 1))
                act.activation(gstat[:, 40:48], gstat[:, 32:40], ACT.Sqrt, bias=eps_col[:, 0:1],
                               scale=1.0 / DV).then_inc(ostd_done, 1)
                for piece in range(1, 8):
                    out_hi(piece)
                    if piece == 3:
                        transposed_hi(hT_hi, 3 * layer + 1, 1)
                    if piece == 6:
                        modulation_hi()
                modulation_out()
                std_of_rows(2 * layer + 1, h_tok if layer == 0 else m_htok)
                if layer == 0:
                    for b in range(NBLK + 1):
                        if b < NBLK:
                            n = WHERE[("gate", 0, b, 0)]
                            wait_chunk("gate", n)
                            wait_chunk("up", n + 1)
                            for q in range(4):
                                split_hi(S_FFN + split_in_block(b, q), gu_raw(n, q), pairs)
                                beside(2, 4 * b + q)
                                if q == 1 and b and BESIDE_FFN[b - 1]:
                                    modulation_hi()
                                elif q == 1:
                                    modulation_out()
                        if b:
                            act.wait_ge(fT_mm, b)
                            act.activation(fT_hi[:, :, :], bank[6][:, :].rearrange("p (a n) -> p a n", a=NT),
                                           ACT.Copy).then_inc(fT_hi_done, 1)
                            n = WHERE[("down", 0, b - 1, 0)]
                            wait_chunk("down", n)
                            for c in range(2):
                                split_hi(S_FFN + down_split(b - 1, c), down_raw(n, c), flat)
                        if b < NBLK:
                            for a in range(NT):
                                if a == 0:
                                    act.wait_ge(gu_mm, b + 1)
                                else:
                                    act.wait_ge(split_used, S_FFN + split_in_block(b, 3) + 1)
                                act.activation(f_silu[:, a, :], bank[4 + a][:, 0:FB], ACT.Silu).then_inc(silu_done, 1)

            for half in range(2):
                for a in range(NT):
                    act.wait_ge(r_mm, 2 * half + a + 1)
                    act.activation(r_hT[:, 4 * half:4 * half + 4, P * a:P * a + P],
                                   bank[2 * a + half][:, :].rearrange("p (k n) -> p k n", k=4),
                                   ACT.Copy).then_inc(r_out, 1)
            for a in range(NT):
                act.activation(htok_hi[:, a, :], m_htok[:, a, :], ACT.Copy).then_inc(htok_split, 1)
            act.wait_ge(gap_done, 1)
            act.activation(e2[:, :, :], gap[:, :, :], ACT.Exp).then_inc(gexp_done, 1)

            def gathered_hi(base):
                for half in range(2):
                    act.wait_ge(ga_mm, base * 4 + half + 1)
                    act.activation(hgT_hi[:, 4 * half:4 * half + 4, :],
                                   bank[2 + half][:, :].rearrange("p (k n) -> p k n", k=4),
                                   ACT.Copy).then_inc(ga_hi, 1)

            def expert_out_hi(turn):
                act.wait_ge(put_done, turn * 2 + 2)
                act.wait_ge(zero_mm, 1)
                act.wait_ge(split_used, turn * EXPERT_SPLITS + S_MOE)
                for half in range(2):
                    act.activation(y_hi[:, CB * half:CB * half + CB], bank[half][:, :], ACT.Copy,
                                   scale=slot_gate[:, 0:1]).then_inc(m_yh, 1)

            gathered_hi(0)
            act.wait_ge(m_add, 1)
            act.activation(put[:, :, :], m_acc[:, 0, 0:NT * P].rearrange("p (a n) -> p a n", a=NT), ACT.Copy)\
               .then_inc(put_done, 1)
            act.activation(slot_gate[:, :], eps_col[:, :], ACT.Copy).then_inc(put_done, 1)
            then(act.activation(e2[:, 0, :], eps_col[:, :], ACT.Silu))
            act.wait_ge(rounds_done, 1)
            n_turns = act.value_load(rounds[0:1, 0:1], min_val=NE, max_val=2 * NE)
            with act.Fori(0, n_turns) as i:
                ring = i * (16 * EXPERT_CHUNKS // RING)
                splits = i * EXPERT_SPLITS
                blocks = i * NBLK

                def silu_of(b):
                    act.wait_ge(split_used, splits + (S_MOE + split_in_block(b, 3) + 1))
                    act.activation(m_silu[:, :], bank[4 + b % 2][:, 0:FB], ACT.Silu).then_inc(m_sl, 1)

                def hidden_hi(b):
                    act.wait_ge(m_tm, blocks + (b + 1))
                    act.activation(mT_hi[:, :], bank[6][:, FB * (b % 2):FB * (b % 2) + FB], ACT.Copy).then_inc(m_th, 1)

                def down_hi(b):
                    n = N0 + EWHERE[("down", b)]
                    wait_chunk("down", n, ring)
                    for c in range(2):
                        split_hi(S_MOE + down_split(b, c), down_raw(n, c), flat, splits)

                for b in range(NBLK):
                    n = N0 + EWHERE[("gate", b)]
                    wait_chunk("gate", n, ring)
                    wait_chunk("up", n + 1, ring)
                    for q in range(4):
                        split_hi(S_MOE + split_in_block(b, q), gu_raw(n, q), pairs, splits)
                        if b and q == SILU_AFTER[b]:
                            silu_of(b - 1)
                        if b == 0 and q == 2:
                            expert_out_hi(i)
                    if b:
                        down_hi(b - 1)
                        hidden_hi(b - 1)
                    if b == 2:
                        act.wait_ge(m_sc, i * 2 + 2)
                        act.wait_ge(pick_mm, i + 1)
                        act.activation(put[:, :, :], bank[7][:, 0:2 * P].rearrange("p (a n) -> p a n", a=NT),
                                       ACT.Copy).then_inc(put_done, 1)
                        act.activation(slot_gate[:, :], bank[7][:, 2 * P:2 * P + 1], ACT.Copy).then_inc(put_done, 1)
                silu_of(NBLK - 1)
                down_hi(NBLK - 1)
                hidden_hi(NBLK - 1)
                gathered_hi(i + 1)
            expert_out_hi(n_turns)
            then(act.activation(e2[:, 0, :], eps_col[:, :], ACT.Sqrt))
            std_of_rows(2 * DEPTH, h_tok)

        @blk.vector
        def _(dve):
            steps = [0]

            def then(ins):
                steps[0] += 1
                ins.then_inc(dve_step, 1)
                dve.wait_ge(dve_step, steps[0])

            def split_lo(s, count, src, like, splits=0):
                dve.wait_ge(hi_done, splits + (s + 1))
                dve.tensor_tensor(like(lo_of(s)), src, like(hi_of(s).bitcast(F32)),
                                  ALU.subtract).then_inc(split_done, 1)

            def flat(ap):
                return ap

            def pairs(ap):
                return ap.rearrange("p (g n) -> p g n", g=2)

            ada_no = [0]
            ada_seen = [0]

            def modulation_out(upto_block=None):
                upto_block = ada_no[0] if upto_block is None else upto_block
                for i in range(ada_seen[0], upto_block):
                    layer, j = ADA[i]
                    src = bank[7 - i % 2] if i < 4 else bank[7]
                    if is_scale(i):
                        dve.wait_ge(ada_mm, i + 1)
                        norm_no = 2 * layer + (j // 2 == SC2)
                        if norm_no == 0:
                            dve.wait_ge(gain0_in, 16)
                        else:
                            dve.wait_ge(gain_in, 16 * norm_no)
                        half = j % 2
                        dve.scalar_tensor_tensor(out=mod_block(i), in0=src[:, :], scalar=1.0,
                                                 in1=gain[:, CB * half:CB * half + CB], op0=ALU.add,
                                                 op1=ALU.mult).then_inc(ada_out, 1)
                        dve.wait_ge(ada_out, i + 1)
                        dve.sem_inc(gain_used, 1)
                    elif i < 4:
                        dve.wait_ge(ada_mm, i + 1)
                        dve.tensor_copy(mod_block(i), src[:, :]).then_inc(ada_out, 1)
                ada_seen[0] = max(ada_seen[0], upto_block)

            def ada_half(half, tiles=range(4)):
                i = ada_no[0]
                layer, j = ADA[i]
                acc = ada_acc[:, i % 2, :]
                start = 2 if i < 4 else 0
                if half == 0 and tiles[0] == start:
                    if 2 <= i < 6:
                        dve.wait_ge(ada_mm, i - 1)
                    if i >= 6:
                        dve.wait_ge(ada_split, i - 5)
                    dve.wait_ge(bias_in, i + 1)
                n = WHERE[("ada", layer, j, half)]
                dve.wait_ge(chunk_in[n % RING], landed(n))
                for q in tiles:
                    k = 4 * half + q
                    first = half == 0 and q == start
                    ins = dve.scalar_tensor_tensor(
                        out=acc, in0=raw[:, n % RING, CB * q:CB * q + CB], scalar=silu_c[:, k:k + 1],
                        in1=ada_bias[:, :] if first else acc, op0=ALU.mult, op1=ALU.add)
                    if first:
                        ins.then_inc(bias_used, 1)
                        dve.wait_ge(bias_used, i + 1)
                    elif q < 3:
                        then(ins)
                    else:
                        ins.then_inc(split_done, 2)
                        dve.wait_ge(split_done, taken(n, 1))
                if half == 1 and tiles[-1] == 3:
                    ada_no[0] += 1

            def norm(i, a_piece, b_piece, dst, quarters=range(4)):
                order = BY_HALF if a_piece is not None else BY_TILE
                for n in quarters:
                    a, half = order[n]
                    if half == 0:
                        dve.wait_ge(std_done, NT * i + a + 1)
                        then(dve.reciprocal(rstd[:, a:a + 1], std[:, a:a + 1]))
                    cols = slice(CB * half, CB * half + CB)
                    by = gain[:, cols] if a_piece is None else mod[:, a_piece, cols]
                    dve.scalar_tensor_tensor(out=dst[:, a, cols], in0=x[:, a, cols], scalar=rstd[:, a:a + 1],
                                             in1=by, op0=ALU.mult, op1=ALU.mult)\
                       .then_inc(out_ready if a_piece is None else h_scaled, 1)
                    if b_piece is not None and n % 2:
                        dve.wait_ge(h_scaled, 4 * i + n + 1)
                        dve.tensor_tensor(dst[:, a, cols], dst[:, a, cols], mod[:, b_piece, cols], ALU.add).then_inc(h_own, 1)

            def transposed_lo(hi, lo, i, half):
                for a in range(NT):
                    dve.wait_ge(tr_hi, 4 * i + 2 * half + a + 1)
                    dve.tensor_tensor(lo[:, 4 * half:4 * half + 4, P * a:P * a + P],
                                      tr_bank(i, half, a)[:, :].rearrange("p (k n) -> p k n", k=4),
                                      hi[:, 4 * half:4 * half + 4, P * a:P * a + P].bitcast(F32),
                                      ALU.subtract).then_inc(tr_lo, 1)

            def beside(i, piece):
                if piece in (0, 1):
                    transposed_lo(hT_hi, hT_lo, i, piece)

            def scale_updates(stage, order, src, piece, ready, dst):
                for n, (a, half) in enumerate(order):
                    ready(a, half)
                    if 2 * stage + n // 2:
                        wait_quarter(dve, (x_step, x_own), 0, 4 * stage + n - 2)
                    dve.tensor_tensor(dst[:, n % 2, :], src(a, half), mod[:, piece, CB * half:CB * half + CB],
                                      ALU.mult).then_inc(ys_done, 1)
                    if n % 2:
                        dve.wait_ge(ys_done, 4 * stage + n + 1)
                        xs = x[:, a, CB * half:CB * half + CB]
                        dve.tensor_tensor(xs, xs, dst[:, 1, :], ALU.add).then_inc(x_own, 1)

            dve.wait_ge(silu_c_done, 1)
            dve.wait_ge(pool_step, 5)
            for n in range(4):
                for half in range(2):
                    ada_half(half, (2, 3))
                modulation_out(n)
                if n == 2:
                    dve.wait_ge(ada_out, 2)
                    norm(0, SC1, SH1, h_tok, range(2))
            modulation_out()
            dve.wait_ge(consts, 6)
            for layer in range(DEPTH):
                dve.wait_ge(ada_out, ada_no[0])
                norm(2 * layer, SC1, SH1, h_tok, range(4) if layer else range(2, 4))
                for j in range(INW // CB):
                    for half in range(2):
                        n = WHERE[("in", layer, j, half)]
                        for q in range(2):
                            split_lo(S_IN[layer] + 4 * j + 2 * half + q, taken(n, q),
                                     raw[:, n % RING, q * SUB:(q + 1) * SUB], flat)
                            beside(3 * layer, 4 * j + 2 * half + q)
                            if q == 0 and half == 0 and j and BESIDE_IN[layer][j - 1]:
                                modulation_out(ada_no[0] - 1)
                            if BESIDE_IN[layer][j]:
                                ada_half(half, (2 * q, 2 * q + 1))
                        if (j, half) == (0, 1) and layer == 0:
                            dve.wait_ge(lam_in, 64)
                            for i in range(2):
                                then(dve.tensor_tensor(lam_rows[:, 2 * i, :, :], lam_rows[:, 2 * i, :, :],
                                                       lam_rows[:, 2 * i + 1, :, :], ALU.mult))
                                dve.tensor_reduce(lam_sum[:, i, :], lam_rows[:, 2 * i, :, :], axis=AX.X, op=ALU.add)\
                                   .then_inc(lam_step, 1)
                            dve.wait_ge(lam_step, 2)
                            dve.sem_inc(lam_dots, 1)
                        if (j, half) == (1, 1):
                            for g in range(2):
                                dve.wait_ge(ws_mm, 2 * layer + g + 1)
                                dve.tensor_tensor(wsT[:, 4 * g:4 * g + 4, :],
                                                  bank[4 + g][:, :].rearrange("p (g n) -> p g n", g=4),
                                                  upto[:, :].unsqueeze(1).to_broadcast([P, 4, P]), ALU.mult).then_inc(ws_out, 1)
                            dve.wait_ge(mixer_in, 48 * (layer + 1))
                            lam_init = 0.8 - 0.6 * math.exp(-0.3 * layer)
                            then(dve.tensor_scalar(subln[:, :], subln[:, :], 1.0 - lam_init, None, ALU.mult))
                        if (j, half) == (3, 1):
                            for a in range(NT):
                                dve.wait_ge(v_step, NT * layer + a + 1)
                                dve.tensor_reduce(gstat[:, NG * a:NG * a + NG],
                                                  z[:, a, 4 * CB:5 * CB].rearrange("p (g n) -> p g n", g=NG),
                                                  axis=AX.X, op=ALU.add).then_inc(vstat_done, 1)
                        if (j, half) == (INW // CB - 1, 0):
                            dve.wait_ge(vstd_done, layer + 1)
                            dve.reciprocal(gstat[:, 0:16], gstat[:, 16:32]).then_inc(vrstd_done, 1)
                modulation_out(ada_no[0] - 1)
                dve.wait_ge(split_used, S_IN[layer] + 4 * (INW // CB))
                for a in range(NT):
                    dve.wait_ge(qk_mm, 4 * layer + NT + a + 1)
                    dve.tensor_copy(kT[:, :, P * a:P * a + P],
                                    qk_bank(1, a)[:, :].rearrange("p (h n) -> p h n", h=NH)).then_inc(qk_out_v, 1)

                def head_max(h):
                    st = hstat[:, h % 2, :]
                    dve.wait_ge(sc_mm, NH * layer + h + 1)
                    for m in range(2):
                        for a in range(NT):
                            cols = slice(0, P) if a == 0 else slice(P, 3 * P)
                            ins = dve.reduce_max(st[:, 2 * m + a:2 * m + a + 1], score_bank(h, m)[:, cols], AX.X)
                            if m + a == 2:
                                then(ins)
                    dve.tensor_scalar(st[:, 4:8], st[:, 0:4], -DH ** -0.5, None, ALU.mult).then_inc(negmax, 1)

                def head_maps(h):
                    st = hstat[:, h % 2, :]
                    p1, p2 = prob[:, h % 2, 0, :], prob[:, h % 2, 1, :]
                    dve.wait_ge(exp_done, 4 * (NH * layer + h + 1))
                    then(dve.reciprocal(st[:, 12:16], st[:, 8:12]))
                    then(dve.tensor_tensor(st[:, 14:16], st[:, 14:16], lam[:, layer:layer + 1].to_broadcast([P, 2]), ALU.mult))
                    parts = [slice(0, P), slice(P, 3 * P)]
                    for a in range(NT):
                        ins = dve.tensor_scalar(p2[:, parts[a]], p2[:, parts[a]], st[:, 14 + a:15 + a], None, ALU.mult)
                        if a:
                            then(ins)
                    for a in range(NT):
                        ins = dve.scalar_tensor_tensor(out=p1[:, parts[a]], in0=p1[:, parts[a]],
                                                       scalar=st[:, 12 + a:13 + a], in1=p2[:, parts[a]],
                                                       op0=ALU.mult, op1=ALU.subtract)
                    ins.then_inc(a_done, 1)

                if layer == 0:
                    dve.wait_ge(lam_exps, 1)
                    then(dve.tensor_tensor(lam[:, :], lam_exp[:, 0, :], lam_exp[:, 1, :], ALU.subtract))
                    for i in range(DEPTH):
                        then(dve.tensor_scalar(lam[:, i:i + 1], lam[:, i:i + 1], 0.8 - 0.6 * math.exp(-0.3 * i), None, ALU.add))
                head_max(0)
                head_max(1)
                for half in range(2):
                    dve.wait_ge(vm_mm, 2 * layer + half + 1)
                    for g in range(4):
                        gg = 4 * half + g
                        ug = z[:, :, GD * gg:GD * gg + GD]
                        dve.scalar_tensor_tensor(out=ug, in0=bank[4 + half][:, 2 * GD * g:2 * GD * g + 2 * GD].rearrange("p (a n) -> p a n", a=NT),
                                                 scalar=bsT[:, gg:gg + 1], in1=ug, op0=ALU.add, op1=ALU.mult).then_inc(ua_done, 1)
                def out_lo(piece):
                    j, half = (piece // 2) % 2, piece // 4
                    n = WHERE[("out", layer, j, half)]
                    q = piece % 2
                    split_lo(S_OUT[layer] + piece, taken(n, q), raw[:, n % RING, q * SUB:(q + 1) * SUB], flat)

                modulation_out()
                head_maps(0)
                head_max(2)
                head_maps(1)
                head_max(3)
                head_maps(2)
                head_maps(3)
                dve.wait_ge(at_mm, NH * (layer + 1))
                transposed_lo(hT_hi, hT_lo, 3 * layer + 1, 0)
                out_lo(0)
                out_lo(1)
                dve.wait_ge(ostd_done, layer + 1)
                then(dve.reciprocal(gstat[:, 48:56], gstat[:, 40:48]))
                for a in range(NT):
                    for h in range(NH):
                        oh = z[:, a, 2 * GW + DV * h:2 * GW + DV * h + DV]
                        dve.scalar_tensor_tensor(out=oh, in0=oh, scalar=gstat[:, 48 + NH * a + h:49 + NH * a + h],
                                                 in1=subln[:, :], op0=ALU.mult, op1=ALU.mult).then_inc(ob_done, 1)
                out_lo(2)
                out_lo(3)
                ada_half(0, (0, 1))
                transposed_lo(hT_hi, hT_lo, 3 * layer + 1, 1)
                ada_half(0, (2, 3))
                out_lo(4)
                ada_half(1, (0, 1))
                out_lo(5)
                ada_half(1, (2, 3))
                out_lo(6)
                out_lo(7)
                modulation_out()
                dve.wait_ge(ada_out, ada_no[0])
                scale_updates(2 * layer, BY_HALF, lambda a, half: bank[2 * half + a][:, :], G1,
                              lambda a, half: dve.wait_ge(split_used, S_OUT[layer] + 6 + 2 * half), y_scaled)
                if layer == 0:
                    norm(1, SC2, SH2, h_tok)
                    for b in range(NBLK + 1):
                        if b < NBLK:
                            n = WHERE[("gate", 0, b, 0)]
                            for q in range(4):
                                split_lo(S_FFN + split_in_block(b, q), taken(n, q), gu_raw(n, q), pairs)
                                beside(2, 4 * b + q)
                                if q == 1 and b:
                                    modulation_out(ada_no[0] - 1 if BESIDE_FFN[b - 1] else None)
                                if q >= 2 and BESIDE_FFN[b]:
                                    ada_half(0, (2 * q - 4, 2 * q - 3))
                        if b:
                            dve.wait_ge(fT_hi_done, b)
                            dve.tensor_tensor(fT_lo[:, :, :], bank[6][:, :].rearrange("p (a n) -> p a n", a=NT),
                                              fT_hi[:, :, :].bitcast(F32), ALU.subtract).then_inc(fT_lo_done, 1)
                            n = WHERE[("down", 0, b - 1, 0)]
                            for c in range(2):
                                split_lo(S_FFN + down_split(b - 1, c), taken(n, c), down_raw(n, c), flat)
                                if c == 0 and BESIDE_FFN[b]:
                                    ada_half(1, (0, 1))
                        if b < NBLK:
                            for a in range(NT):
                                dve.wait_ge(silu_done, NT * b + a + 1)
                                dve.tensor_tensor(f_act[:, a, :], f_silu[:, a, :], bank[4 + a][:, FB:2 * FB],
                                                  ALU.mult).then_inc(act_done, 1)
                        if BESIDE_FFN[b]:
                            ada_half(1, (2, 3) if b else range(4))
                    dve.wait_ge(ada_out, ada_no[0])
                    scale_updates(1, BY_TILE, lambda a, half: bank[2 * a + half][:, :], G2,
                                  lambda a, half: dve.wait_ge(split_used, S_FFN + EXPERT_SPLITS), y_scaled)
                else:
                    norm(3, SC2, SH2, m_htok)

            for a in range(NT):
                dve.wait_ge(htok_split, a + 1)
                then(dve.tensor_tensor(htok_lo[:, a, :], m_htok[:, a, :], htok_hi[:, a, :].bitcast(F32), ALU.subtract))
            dve.wait_ge(logit_mm, 1)
            then(dve.tensor_copy(logit[:, :, :], bank[4][:, 0:NT * NE].rearrange("p (a e) -> p a e", a=NT)))
            for a in range(NT):
                then(dve.max(top[:, a, :], logit[:, a, :]))
                then(dve.max_index(top_i[:, a, :], top[:, a, :], logit[:, a, :]))
            dve.tensor_tensor(gap[:, :, :], top[:, :, 1:2], top[:, :, 0:1], ALU.subtract).then_inc(gap_done, 1)
            then(dve.tensor_copy(top_f[:, :, :], top_i[:, :, :]))
            dve.wait_ge(consts, 8)
            then(dve.tensor_tensor(hit[:, :, :, :], slot_no[:, 0:NE].unsqueeze(1).unsqueeze(1).to_broadcast([P, NT, 2, NE]),
                                   top_f[:, :, 0:2].unsqueeze(3).to_broadcast([P, NT, 2, NE]), ALU.is_equal))
            dve.tensor_tensor(mask[:, :, :], hit[:, :, 0, :], hit[:, :, 1, :], ALU.add).then_inc(mask_done, 1)
            dve.wait_ge(gexp_done, 1)
            then(dve.tensor_scalar(wsum[:, :, :], e2[:, :, :], 1.0, None, ALU.add))
            then(dve.reciprocal(w12[:, :, 0:1], wsum[:, :, :]))
            then(dve.tensor_tensor(w12[:, :, 1:2], e2[:, :, :], w12[:, :, 0:1], ALU.mult))
            dve.wait_ge(mask_done, 1)
            then(dve.tensor_tensor(hit[:, :, :, :], hit[:, :, :, :], w12[:, :, :].unsqueeze(3).to_broadcast([P, NT, 2, NE]), ALU.mult))
            then(dve.memset(gate_of[:, :, 2 * NE:2 * NE + 1], 0.0))
            for again in range(2):
                then(dve.tensor_tensor(gate_of[:, :, NE * again:NE * again + NE], hit[:, :, 0, :], hit[:, :, 1, :], ALU.add))
            then(dve.memset(slot_of[:, :, 2 * NE:2 * NE + 1], -1.0))
            dve.wait_ge(count_mm, 1)
            then(dve.scalar_tensor_tensor(out=slot_of[:, :, 0:NE],
                                          in0=bank[4][:, 32:32 + NT * NE].rearrange("p (a e) -> p a e", a=NT),
                                          scalar=1.0, in1=mask[:, :, :], op0=ALU.add, op1=ALU.mult))
            then(dve.tensor_scalar(slot_of[:, :, NE:2 * NE], slot_of[:, :, 0:NE], -1.0 - P, None, ALU.add))
            then(dve.tensor_scalar(slot_of[:, :, 0:NE], slot_of[:, :, 0:NE], -1.0, None, ALU.add))

            def make_pick(i, count):
                for a in range(NT):
                    dve.tensor_scalar(pick[:, a, :], slot_no[:, :], slot_of[:, a, i], None, ALU.is_equal)\
                       .then_inc(pick_done, 1)
                    dve.tensor_copy(gate_col[:, a:a + 1], gate_of[:, a, i]).then_inc(pick_done, 1)

            def gathered_lo(base):
                for half in range(2):
                    dve.wait_ge(ga_mm, base * 4 + (2 + half + 1))
                    dve.tensor_copy(hgT_lo[:, 4 * half:4 * half + 4, :],
                                    bank[(5, 7)[half]][:, :].rearrange("p (k n) -> p k n", k=4)).then_inc(ga_lo, 1)

            def expert_out_lo(turn):
                for half in range(2):
                    dve.wait_ge(m_yh, turn * 2 + (half + 1))
                    dve.scalar_tensor_tensor(out=y_lo[:, CB * half:CB * half + CB], in0=bank[half][:, :],
                                             scalar=slot_gate[:, 0:1], in1=y_hi[:, CB * half:CB * half + CB].bitcast(F32),
                                             op0=ALU.mult, op1=ALU.subtract).then_inc(m_yl, 1)

            def expert_add(turn, n):
                a, half, b = SCATTERED[n]
                dve.wait_ge(m_sc, turn * 2 + (half + 1))
                acc = m_acc[:, a, CB * half:CB * half + CB]
                dve.tensor_tensor(acc, acc, bank[b][:, :], ALU.add).then_inc(m_add, 1)

            make_pick(slice(0, 1), 0)
            then(dve.reduce_max(most[:, :], bank[4][:, 64:64 + NE], AX.X))
            then(dve.tensor_scalar(rounds_f[:, :], most[:, :], float(P), float(NE), ALU.is_gt, ALU.mult))
            then(dve.tensor_scalar(rounds_f[:, :], rounds_f[:, :], float(NE), None, ALU.add))
            dve.tensor_copy(rounds[:, :], rounds_f[:, :]).then_inc(rounds_done, 1)
            gathered_lo(0)
            dve.wait_ge(rounds_done, 1)
            n_turns = dve.value_load(rounds[0:1, 0:1], min_val=NE, max_val=2 * NE)
            with dve.Fori(0, n_turns) as i:
                splits = i * EXPERT_SPLITS
                blocks = i * NBLK

                def gated(b):
                    dve.wait_ge(m_sl, blocks + (b + 1))
                    dve.tensor_tensor(m_act[:, :], m_silu[:, :], bank[4 + b % 2][:, FB:2 * FB], ALU.mult)\
                       .then_inc(m_ac, 1)

                def hidden_lo(b):
                    dve.wait_ge(m_th, blocks + (b + 1))
                    dve.tensor_tensor(mT_lo[:, :], bank[6][:, FB * (b % 2):FB * (b % 2) + FB],
                                      mT_hi[:, :].bitcast(F32), ALU.subtract).then_inc(m_tl, 1)

                def down_lo(b):
                    n = N0 + EWHERE[("down", b)]
                    for c in range(2):
                        split_lo(S_MOE + down_split(b, c), taken(n, c), down_raw(n, c), flat, splits)

                for b in range(NBLK):
                    n = N0 + EWHERE[("gate", b)]
                    for q in range(4):
                        split_lo(S_MOE + split_in_block(b, q), taken(n, q), gu_raw(n, q), pairs, splits)
                        if b and q == SILU_AFTER[b]:
                            gated(b - 1)
                        if b == 0 and q == 2:
                            expert_out_lo(i)
                        if b == 1 and q in (0, 2):
                            expert_add(i, q // 2)
                        if b == 2 and q in (0, 2):
                            expert_add(i, 2 + q // 2)
                    if b:
                        down_lo(b - 1)
                        hidden_lo(b - 1)
                    if b == 5:
                        dve.wait_ge(pick_mm, i + 1)
                        make_pick(bass.ds(i + 1, 1), 0)
                gated(NBLK - 1)
                down_lo(NBLK - 1)
                hidden_lo(NBLK - 1)
                gathered_lo(i + 1)
            expert_out_lo(n_turns)
            for n in (2, 3, 1, 0):
                expert_add(n_turns, n)
            dve.wait_ge(m_add, n_turns * 4 + 5)
            scale_updates(3, BY_TILE, lambda a, half: m_acc[:, a, CB * half:CB * half + CB], G2,
                          lambda a, half: None, f_scaled)
            dve.wait_ge(gain_in, 16 * 4)
            norm(4, None, None, h_tok)

        @blk.tensor
        def _(pe):
            def three(dst, a_hi, a_lo, b_hi, b_lo, first, last):
                pe.matmul(dst, a_hi, b_hi, start=first, stop=False)
                pe.matmul(dst, a_lo, b_hi, start=False, stop=False)
                return pe.matmul(dst, a_hi, b_lo, start=False, stop=last)

            ada_no = [4]

            def ada_first(i, half):
                dst = bank[7 - i % 2][:, :]
                if half == 0 and i >= 2:
                    pe.wait_ge(ada_out, i - 1)
                n = WHERE[("ada", *ADA[i], half)]
                pe.wait_ge(chunk_in[n % RING], landed(n))
                for q in range(2):
                    last = pe.matmul(dst, silu_b[:, half, q, :], raw[:, n % RING, CB * q:CB * q + CB],
                                     start=(half == 0 and q == 0), stop=False)
                last.then_inc(start_read, 1)
                if half == 1:
                    pe.wait_ge(split_done, taken(n, 1))
                    pe.matmul(dst, ones_r[:, :].bitcast(F32), ada_acc[:, i % 2, :], start=False, stop=True).then_inc(ada_mm, 1)

            def ada_sum():
                i = ada_no[0]
                ada_no[0] += 1
                layer, j = ADA[i]
                pe.wait_ge(ada_split, i - 3)
                pe.wait_ge(ada_out, i)
                pe.matmul(bank[7][:, :], ones_r[:, :], ada_hi[:, :], start=True, stop=False)
                pe.matmul(bank[7][:, :], ones_r[:, :], ada_lo[:, :], start=False, stop=True).then_inc(ada_mm, 1)

            def keep_warm(n, b=7):
                for _ in range(n):
                    pe.matmul(bank[b][:, :].rearrange("p (g n) -> p g n", g=4), ones_r[:, :],
                              ones_r[:, :].unsqueeze(1).to_broadcast([P, 4, P]), start=True, stop=True)

            def transposes(i, half, src, ready):
                for a in range(NT):
                    ready(a)
                    for k in range(4):
                        last = pe.transpose(tr_bank(i, half, a)[:, P * k:P * k + P], src(a, 4 * half + k), ident[:, :])
                    last.then_inc(tr_mm, 1)

            def h_transposes(i, norm_no, half):
                transposes(i, half, lambda a, k: h_tok[:, a, P * k:P * k + P],
                           lambda a: wait_quarter(pe, (h_done, h_own), norm_no, 2 * half + a))

            def qk_transposes(layer):
                pe.wait_ge(z_out, NT * ((INW // CB) * layer + 4))
                for part in range(2):
                    for a in range(NT):
                        for h in range(NH):
                            c0 = 2 * GW + NH * DV * part + DV * h
                            last = pe.transpose(qk_bank(part, a)[:, P * h:P * h + P], z[:, a, c0:c0 + DV], ident[:, :])
                        last.then_inc(qk_mm, 1)

            def project(kind, layer, s0, blocks, evacuated, i, more):
                for j in range(blocks):
                    for sub in range(4):
                        if j == 0 and sub in (0, 2):
                            pe.wait_ge(tr_lo, 4 * i + 2 + sub)
                        if j == 0 and sub == 1:
                            more()
                        if kind == "in" and sub == 3 and j == blocks - 1:
                            qk_transposes(layer)
                        if kind == "in" and sub == 3 and j and BESIDE_IN[layer][j - 1]:
                            ada_sum()
                        if kind == "in" and sub == 2 and j == 0:
                            pe.wait_ge(mixer_in, 48 * (layer + 1))
                            for half in range(2):
                                for g in range(4):
                                    last = pe.transpose(bank[4 + half][:, P * g:P * g + P], ws_raw[:, 4 * half + g, :], ident[:, :])
                                last.then_inc(ws_mm, 1)
                        s = s0 + 4 * j + sub
                        pe.wait_ge(split_done, taken(WHERE[(kind, layer, j, sub // 2)], sub % 2))
                        if sub == 0:
                            evacuated(j)
                        for a in range(NT):
                            for kk in range(2):
                                k = 2 * sub + kk
                                cols = slice(CB * kk, CB * kk + CB)
                                last = three(bank[2 * (j % 2) + a][:, :], hT_hi[:, k, P * a:P * a + P],
                                             hT_lo[:, k, P * a:P * a + P], hi_of(s)[:, cols], lo_of(s)[:, cols],
                                             k == 0, k == KT - 1)
                        last.then_inc(split_used, 1)

            pe.wait_ge(consts, 6)
            pe.wait_ge(first_in, 16)
            pe.transpose(bank[6][:, 0:KT], c_rows[:, :], ident[0:KT, 0:KT]).then_inc(c_mm, 1)
            pe.wait_ge(silu_b_done, 1)
            for n in range(4):
                for half in range(2):
                    if (n, half) == (3, 1):
                        h_transposes(0, 0, 0)
                    ada_first(n, half)
            for layer in range(DEPTH):
                if layer:
                    keep_warm(WARM_NORM, 6)
                    h_transposes(3, 2, 0)

                def z_free(j):
                    if j >= 2:
                        pe.wait_ge(z_out, NT * ((INW // CB) * layer + j - 1))

                project("in", layer, S_IN[layer], INW // CB, z_free, 3 * layer, lambda: h_transposes(3 * layer, 2 * layer, 1))
                ada_sum()

                def scores(h):
                    for a in range(NT):
                        for m in range(2):
                            dst = score_bank(h, m)
                            cols = slice(0, P) if a == 0 else slice(P, 3 * P)
                            rows = slice(DH * m, DH * m + DH)
                            pe.matmul(dst[:, cols], qT[rows, h, P * a:P * a + P], kT[rows, h, 0:P * (a + 1)],
                                      start=(a == 0), stop=False, skip_group_check=True)
                    for a in range(NT):
                        for m in range(2):
                            cols = slice(P * 2 * a, P * 2 * a + P)
                            last = pe.matmul(score_bank(h, m)[:, cols], ident_r[:, :], future[:, :],
                                             start=False, stop=True, skip_group_check=True)
                    last.then_inc(sc_mm, 1)

                pe.wait_ge(qk_out_a, NT * (layer + 1))
                pe.wait_ge(qk_out_v, NT * (layer + 1))
                scores(0)
                pe.wait_ge(z_out, NT * (INW // CB) * (layer + 1))
                scores(1)
                pe.wait_ge(ws_out, 2 * (layer + 1))
                pe.wait_ge(v_done, NT * (layer + 1))
                for half in range(2):
                    for g in range(4):
                        gg = 4 * half + g
                        last = pe.matmul(bank[4 + half][:, 2 * GD * g:2 * GD * g + 2 * GD].rearrange("p (a n) -> p a n", a=NT),
                                         wsT[:, gg, :], z[:, :, GW + GD * gg:GW + GD * gg + GD], start=True, stop=True)
                    last.then_inc(vm_mm, 1)
                def mix_tile(a, k):
                    c0 = P * k if k < 4 else 2 * GW + P * (k - 4)
                    return z[:, a, c0:c0 + P]

                def head_map(h):
                    pe.wait_ge(a_done, NH * layer + h + 1)
                    for i in range(3):
                        last = pe.transpose(bank[4 + h % 2][:, P * i:P * i + P], prob[:, h % 2, 0, P * i:P * i + P], ident[:, :])
                    last.then_inc(at_mm, 1)

                def head_values(h):
                    pe.wait_ge(at_out, NH * layer + h + 1)
                    if h:
                        pe.wait_ge(osq_done, NT * (NH * layer + h))
                    v0 = 2 * GW + 2 * NH * DV + DV * h
                    dst = FB * (h % 2)
                    pe.matmul(bank[6][:, dst:dst + DV], aT[:, 0:P], z[:, 0, v0:v0 + DV], start=True, stop=True)
                    pe.matmul(bank[6][:, dst + DV:dst + 2 * DV], aT[:, P:2 * P], z[:, 0, v0:v0 + DV], start=True, stop=False)
                    pe.matmul(bank[6][:, dst + DV:dst + 2 * DV], aT[:, 2 * P:3 * P], z[:, 1, v0:v0 + DV],
                              start=False, stop=True).then_inc(o_mm, 1)

                pe.wait_ge(exp_done, 4 * (NH * layer + 1))
                scores(2)
                pe.wait_ge(ua_done, 8 * (layer + 1))
                head_map(0)
                pe.wait_ge(exp_done, 4 * (NH * layer + 2))
                scores(3)
                head_values(0)
                pe.wait_ge(ada_out, ada_no[0])
                keep_warm(WARM_HEAD)
                head_map(1)
                head_values(1)
                tr = 3 * layer + 1
                pe.wait_ge(exp_done, 4 * (NH * layer + 3))
                transposes(tr, 0, mix_tile, lambda a: None)
                head_map(2)
                head_values(2)
                keep_warm(WARM_HEAD)
                head_map(3)
                head_values(3)

                def out_piece(piece):
                    j, half, q = (piece // 2) % 2, piece // 4, piece % 2
                    s = S_OUT[layer] + piece
                    pe.wait_ge(split_done, taken(WHERE[("out", layer, j, half)], q))
                    for a in range(NT):
                        for kk in range(2):
                            k = 4 * half + 2 * q + kk
                            cols = slice(CB * kk, CB * kk + CB)
                            last = three(bank[2 * j + a][:, :], hT_hi[:, k, P * a:P * a + P], hT_lo[:, k, P * a:P * a + P],
                                         hi_of(s)[:, cols], lo_of(s)[:, cols], k == 0, k == KT - 1)
                    last.then_inc(split_used, 1)

                pe.wait_ge(tr_lo, 4 * tr + 2)
                out_piece(0)
                out_piece(1)
                out_piece(2)
                transposes(tr, 1, mix_tile, lambda a: pe.wait_ge(ob_done, NH * (NT * layer + a + 1)))
                out_piece(3)
                pe.wait_ge(tr_lo, 4 * tr + 4)
                for piece in range(4, 8):
                    out_piece(piece)
                    if piece == 6:
                        ada_sum()
                if layer == 0:
                    keep_warm(WARM_NORM, 6)
                    h_transposes(2, 1, 0)
                    for b in range(NBLK + 1):
                        for q in range(4):
                            if q == 3 and b and BESIDE_FFN[b - 1]:
                                ada_sum()
                            if b < NBLK:
                                if b == 0 and q in (0, 2):
                                    pe.wait_ge(tr_lo, 4 * 2 + 2 + q)
                                if b == 0 and q == 1:
                                    h_transposes(2, 1, 1)
                                s = S_FFN + split_in_block(b, q)
                                pe.wait_ge(split_done, taken(WHERE[("gate", 0, b, 0)], q))
                                if q == 0 and b:
                                    pe.wait_ge(act_done, NT * b)
                                for a in range(NT):
                                    for kk in range(2):
                                        k = 2 * q + kk
                                        wh = hi_of(s).rearrange("p (g k n) -> p g k n", g=2, k=2)[:, :, kk, :]
                                        wl = lo_of(s).rearrange("p (g k n) -> p g k n", g=2, k=2)[:, :, kk, :]
                                        last = three(bank[4 + a][:, :].rearrange("p (g n) -> p g n", g=2),
                                                     hT_hi[:, k, P * a:P * a + P], hT_lo[:, k, P * a:P * a + P], wh, wl,
                                                     k == 0, k == KT - 1)
                                    if q == 3 and a == 0:
                                        last.then_inc(gu_mm, 1)
                                last.then_inc(split_used, 1)
                            if q == 1 and b:
                                for a in range(NT):
                                    pe.wait_ge(act_done, NT * (b - 1) + a + 1)
                                    for c in range(2):
                                        last = pe.transpose(bank[6][:, FB * a + P * c:FB * a + P * c + P],
                                                            f_act[:, a, P * c:P * c + P], ident[:, :])
                                last.then_inc(fT_mm, 1)
                        if b:
                            pe.wait_ge(fT_lo_done, b)
                            for c in range(2):
                                s = S_FFN + down_split(b - 1, c)
                                pe.wait_ge(split_done, taken(WHERE[("down", 0, b - 1, 0)], c))
                                for a in range(NT):
                                    for half in range(2):
                                        cols = slice(CB * half, CB * half + CB)
                                        last = three(bank[2 * a + half][:, :], fT_hi[:, a, P * c:P * c + P],
                                                     fT_lo[:, a, P * c:P * c + P], hi_of(s)[:, cols], lo_of(s)[:, cols],
                                                     b == 1 and c == 0, b == NBLK and c == 1)
                                last.then_inc(split_used, 1)

            for half in range(2):
                for a in range(NT):
                    wait_quarter(pe, (h_done, h_own), 3, 2 * half + a)
                    for k in range(4):
                        last = pe.transpose(bank[2 * a + half][:, P * k:P * k + P],
                                            m_htok[:, a, P * (4 * half + k):P * (4 * half + k) + P], ident[:, :])
                    last.then_inc(r_mm, 1)
            pe.wait_ge(route_in, 16)
            pe.wait_ge(r_out, 4)
            for a in range(NT):
                for k in range(KT):
                    last = pe.matmul(bank[4][:, NE * a:NE * a + NE], r_hT[:, k, P * a:P * a + P], w_route[:, k, :],
                                     start=(k == 0), stop=(k == KT - 1))
            last.then_inc(logit_mm, 1)
            pe.wait_ge(mask_done, 1)
            pe.matmul(bank[4][:, 32:32 + NE], before[:, :], mask[:, 0, :], start=True, stop=True)
            pe.matmul(bank[4][:, 40:40 + NE], ones_r[:, :].bitcast(F32), mask[:, 0, :], start=True, stop=False)
            pe.matmul(bank[4][:, 40:40 + NE], before[:, :], mask[:, 1, :], start=False, stop=True)
            pe.matmul(bank[4][:, 64:64 + NE], ones_r[:, :].bitcast(F32), mask[:, 0, :], start=True, stop=False)
            pe.matmul(bank[4][:, 64:64 + NE], ones_r[:, :].bitcast(F32), mask[:, 1, :], start=False, stop=True).then_inc(count_mm, 1)

            def gather():
                for g, src in enumerate((htok_hi, htok_lo)):
                    for half in range(2):
                        dst = bank[(2, 3, 5, 7)[2 * g + half]]
                        for k in range(4):
                            c0 = P * (4 * half + k)
                            for a in range(NT):
                                last = pe.matmul(dst[:, P * k:P * k + P], src[:, a, c0:c0 + P], pick[:, a, :],
                                                 start=(a == 0), stop=(a == NT - 1))
                        last.then_inc(ga_mm, 1)

            def scatter(turn):
                pe.wait_ge(put_done, turn * 2 + 2)
                pe.wait_ge(ga_hi, turn * 2 + 2)
                pe.wait_ge(ga_lo, turn * 2 + 2)
                for half in range(2):
                    cols = slice(CB * half, CB * half + CB)
                    pe.wait_ge(m_yl, turn * 2 + (half + 1))
                    for a in range(NT):
                        dst = bank[((2, 3), (7, 6))[half][a]][:, :]
                        pe.matmul(dst, put[:, a, :], y_hi[:, cols], start=True, stop=False)
                        last = pe.matmul(dst, put[:, a, :], y_lo[:, cols], start=False, stop=True)
                    last.then_inc(m_sc, 1)

            pe.wait_ge(pick_done, 4)
            gather()
            pe.wait_ge(m_add, 1)
            for half in range(2):
                last = pe.matmul(bank[half][:, :], ones_r[:, :].bitcast(F32), m_acc[:, 0, 0:CB], start=True, stop=True)
            last.then_inc(zero_mm, 1)
            pe.wait_ge(rounds_done, 1)
            n_turns = pe.value_load(rounds[0:1, 0:1], min_val=NE, max_val=2 * NE)
            with pe.Fori(0, n_turns) as i:
                splits = i * EXPERT_SPLITS
                blocks = i * NBLK
                pe.wait_ge(ga_hi, i * 2 + 2)
                pe.wait_ge(ga_lo, i * 2 + 2)
                for b in range(NBLK + 1):
                    for q in range(4):
                        if b < NBLK:
                            s = S_MOE + split_in_block(b, q)
                            pe.wait_ge(split_done, splits + taken(N0 + EWHERE[("gate", b)], q))
                            for kk in range(2):
                                k = 2 * q + kk
                                wh = hi_of(s).rearrange("p (g k n) -> p g k n", g=2, k=2)[:, :, kk, :]
                                wl = lo_of(s).rearrange("p (g k n) -> p g k n", g=2, k=2)[:, :, kk, :]
                                last = three(bank[4 + b % 2][:, :].rearrange("p (g n) -> p g n", g=2),
                                             hgT_hi[:, k, :], hgT_lo[:, k, :], wh, wl, k == 0, k == KT - 1)
                            last.then_inc(split_used, 1)
                        if q == 2 and b == 0:
                            scatter(i)
                        if b and q == min(3, 1 + SILU_AFTER[min(b, NBLK - 1)]):
                            pe.wait_ge(m_ac, blocks + b)
                            if b == 1:
                                pe.wait_ge(m_add, i * 4 + 2)
                            for c in range(2):
                                last = pe.transpose(bank[6][:, FB * ((b - 1) % 2) + P * c:FB * ((b - 1) % 2) + P * c + P],
                                                    m_act[:, P * c:P * c + P], ident[:, :])
                            last.then_inc(m_tm, 1)
                        if b == 2 and q == 1:
                            pe.wait_ge(m_add, i * 4 + 3)
                            for a in range(NT):
                                pe.transpose(bank[7][:, P * a:P * a + P], pick[:, a, :].bitcast(F32), ident[:, :])
                            for a in range(NT):
                                last = pe.matmul(bank[7][:, 2 * P:2 * P + 1], pick[:, a, :].bitcast(F32), gate_col[:, a:a + 1],
                                                 start=(a == 0), stop=(a == NT - 1))
                            last.then_inc(pick_mm, 1)
                    if b == NBLK:
                        pe.wait_ge(pick_done, i * 4 + 8)
                        pe.wait_ge(m_add, i * 4 + 5)
                        gather()
                    if b:
                        pe.wait_ge(m_tl, blocks + b)
                        for c in range(2):
                            s = S_MOE + down_split(b - 1, c)
                            pe.wait_ge(split_done, splits + taken(N0 + EWHERE[("down", b - 1)], c))
                            for half in range(2):
                                cols = slice(CB * half, CB * half + CB)
                                last = three(bank[half][:, :], mT_hi[:, P * c:P * c + P], mT_lo[:, P * c:P * c + P],
                                             hi_of(s)[:, cols], lo_of(s)[:, cols],
                                             b == 1 and c == 0, b == NBLK and c == 1)
                            last.then_inc(split_used, 1)
            scatter(n_turns)


_IN = ["x", "c", "w_ada", "b_ada", "norm1_g", "norm2_g", "w_in", "w_out", "gmlp_vnorm_g", "gmlp_ws", "gmlp_bs",
       "lam_q1", "lam_k1", "lam_q2", "lam_k2", "diff_subln_g", "ffn_w_gate", "ffn_w_up", "ffn_w_down",
       "w_router", "moe_w_gate", "moe_w_up", "moe_w_down", "final_g"]


def kernel(**inputs):
    import concourse.bacc as bacc
    from concourse.bass_utils import run_bass_kernel_spmd

    nc = bacc.Bacc("TRN2", target_bir_lowering=False, num_devices=1)
    arrays, tensors = {}, {}
    for name in _IN:
        a = np.ascontiguousarray(inputs[name])
        arrays["in_" + name] = a
        tensors[name] = nc.dram_tensor("in_" + name, a.shape, mybir.dt.from_np(a.dtype), kind="ExternalInput").ap()
    out = nc.dram_tensor("out", (SEQ, D), F32, kind="ExternalOutput").ap()
    trunk(nc, tensors, out)
    r = run_bass_kernel_spmd(nc, [arrays], core_ids=[0])
    return np.asarray(r.results[0]["out"]).reshape(1, SEQ, D)
```
